# Optimizing a Trainium2 kernel written in Bass

```python
import math
import jax, jax.numpy as jnp
from jax import lax
import numpy as np
import jax
import jax.numpy as jnp

D_MODEL = 1024
BATCH = 1
SEQ = 256
DEPTH = 1

D_RNN = D_MODEL
RNN_BLOCKS = 8
RNN_BLOCK_W = D_RNN // RNN_BLOCKS
CONV_RNN = 4
RG_LRU_C = 8.0
DIFF_HEADS = 4
DIFF_HEAD_DIM = 64
DIFF_QK = DIFF_HEADS * 2 * DIFF_HEAD_DIM
DIFF_WIDTH = DIFF_HEADS * 2 * DIFF_HEAD_DIM
FOX_HEADS = 8
FOX_HEAD_DIM = 64
FOX_WIDTH = FOX_HEADS * FOX_HEAD_DIM
N_BUCKETS = 32
MAX_EXACT = N_BUCKETS // 2
MAX_DISTANCE = 128
Q_BLOCK = 128
D_FF = ((8 * D_MODEL // 3 + 127) // 128) * 128
CONV_FFN = 3
N_BRANCH = 3
EPS = 1e-6

IN_WIDTHS = (D_RNN, D_RNN, DIFF_QK, DIFF_QK, DIFF_WIDTH, FOX_WIDTH, FOX_WIDTH, FOX_WIDTH, FOX_HEADS, N_BRANCH * D_MODEL)
N_IN = int(sum(IN_WIDTHS))
IN_SPLITS = tuple(int(v) for v in np.cumsum(IN_WIDTHS)[:-1])


def rmsnorm(x, g):
    xf = x.astype(jnp.float32)
    y = xf * lax.rsqrt(jnp.mean(xf * xf, axis=-1, keepdims=True) + EPS)
    return (y * g.astype(jnp.float32)).astype(x.dtype)

def causal_dwconv(x, w, b):
    k = w.shape[0]
    s = x.shape[1]
    xp = jnp.pad(x, ((0, 0), (k - 1, 0), (0, 0)))
    y = b + xp[:, 0:s] * w[0]
    for j in range(1, k):
        y = y + xp[:, j:j + s] * w[j]
    return y

def _to_blocks(t):
    b, s = t.shape[:2]
    return jnp.moveaxis(t.reshape(b, s // Q_BLOCK, Q_BLOCK, *t.shape[2:]), 1, 0)

def _from_blocks(t):
    nb, b = t.shape[:2]
    t = jnp.moveaxis(t, 0, 1)
    return t.reshape(b, nb * Q_BLOCK, *t.shape[3:])

def t5_bucket(dist):
    n = jnp.maximum(dist, 0)
    nf = jnp.maximum(n, 1).astype(jnp.float32)
    large = MAX_EXACT + (jnp.log(nf / MAX_EXACT) / math.log(MAX_DISTANCE / MAX_EXACT)
                         * (N_BUCKETS - MAX_EXACT)).astype(jnp.int32)
    large = jnp.minimum(large, N_BUCKETS - 1)
    return jnp.where(n < MAX_EXACT, n, large)

def rg_lru(x, w_r, b_r, w_i, b_i, a_param):
    bsz, s, c = x.shape
    xb = x.reshape(bsz, s, RNN_BLOCKS, RNN_BLOCK_W)
    r = jax.nn.sigmoid(jnp.einsum('bsnc,ncd->bsnd', xb, w_r).reshape(bsz, s, c) + b_r)
    i = jax.nn.sigmoid(jnp.einsum('bsnc,ncd->bsnd', xb, w_i).reshape(bsz, s, c) + b_i)
    log_a = (-RG_LRU_C * r.astype(jnp.float32)) * jax.nn.softplus(-a_param.astype(jnp.float32))
    a = jnp.exp(log_a)
    u = jnp.sqrt(-jnp.expm1(2.0 * log_a)) * (i * x).astype(jnp.float32)

    def combine(left, right):
        a1, b1 = left
        a2, b2 = right
        return a1 * a2, a2 * b1 + b2

    _, h = lax.associative_scan(combine, (a, u), axis=1)
    return h.astype(x.dtype)

def diff_attention(q, k, v, lam, rel_table):
    s_len = q.shape[1]
    scale = DIFF_HEAD_DIM ** -0.5
    k_pos = jnp.arange(s_len)

    def one_block(args):
        qb, blk = args
        q_pos = blk * Q_BLOCK + jnp.arange(Q_BLOCK)
        dist = q_pos[:, None] - k_pos[None, :]
        bias = jnp.moveaxis(rel_table[t5_bucket(dist)], -1, 0)
        sc = jnp.einsum('bqhcd,bkhcd->bchqk', qb, k).astype(jnp.float32) * scale + bias.astype(jnp.float32)
        sc = jnp.where(dist >= 0, sc, -jnp.inf)
        p = jax.nn.softmax(sc, axis=-1)
        w = p[:, 0] - lam * p[:, 1]
        return jnp.einsum('bhqk,bkhd->bqhd', w.astype(v.dtype), v)

    out = lax.map(one_block, (_to_blocks(q), jnp.arange(s_len // Q_BLOCK)))
    return _from_blocks(out)

def forgetting_attention(q, k, v, log_f):
    s_len = q.shape[1]
    scale = FOX_HEAD_DIM ** -0.5
    k_pos = jnp.arange(s_len)
    c = jnp.cumsum(log_f.astype(jnp.float32), axis=1)
    ck = jnp.moveaxis(c, -1, 1)

    def one_block(args):
        qb, cq, blk = args
        q_pos = blk * Q_BLOCK + jnp.arange(Q_BLOCK)
        dist = q_pos[:, None] - k_pos[None, :]
        decay = jnp.moveaxis(cq, -1, 1)[..., None] - ck[:, :, None, :]
        sc = jnp.einsum('bqhd,bkhd->bhqk', qb, k).astype(jnp.float32) * scale + decay
        sc = jnp.where(dist >= 0, sc, -jnp.inf)
        p = jax.nn.softmax(sc, axis=-1)
        return jnp.einsum('bhqk,bkhd->bqhd', p.astype(v.dtype), v)

    out = lax.map(one_block, (_to_blocks(q), _to_blocks(c), jnp.arange(s_len // Q_BLOCK)))
    return _from_blocks(out)

def first_inputs(seed: int = 0) -> dict:
    key = jax.random.key(seed)
    ks = jax.random.split(key, 32)
    L = DEPTH

    def nrm(k, shape, scale):
        return jax.random.normal(k, shape, jnp.float32) * scale

    a_target = jax.random.uniform(ks[9], (L, D_RNN), jnp.float32, 0.9, 0.999)
    sig = a_target ** (1.0 / RG_LRU_C)
    return {
        "x": nrm(ks[0], (BATCH, SEQ, D_MODEL), 1.0),
        "norm1_g": 1.0 + nrm(ks[1], (L, D_MODEL), 0.02),
        "w_in": nrm(ks[2], (L, D_MODEL, N_IN), D_MODEL ** -0.5),
        "rnn_conv_w": nrm(ks[3], (L, CONV_RNN, D_RNN), CONV_RNN ** -0.5),
        "rnn_conv_b": nrm(ks[4], (L, D_RNN), 0.02),
        "rg_w_r": nrm(ks[5], (L, RNN_BLOCKS, RNN_BLOCK_W, RNN_BLOCK_W), RNN_BLOCK_W ** -0.5),
        "rg_b_r": nrm(ks[6], (L, D_RNN), 0.02),
        "rg_w_i": nrm(ks[7], (L, RNN_BLOCKS, RNN_BLOCK_W, RNN_BLOCK_W), RNN_BLOCK_W ** -0.5),
        "rg_b_i": nrm(ks[8], (L, D_RNN), 0.02),
        "rg_a": jnp.log(sig) - jnp.log1p(-sig),
        "diff_lq1": nrm(ks[10], (L, DIFF_HEAD_DIM), 0.1),
        "diff_lk1": nrm(ks[11], (L, DIFF_HEAD_DIM), 0.1),
        "diff_lq2": nrm(ks[12], (L, DIFF_HEAD_DIM), 0.1),
        "diff_lk2": nrm(ks[13], (L, DIFF_HEAD_DIM), 0.1),
        "diff_subln_g": 1.0 + nrm(ks[14], (L, 2 * DIFF_HEAD_DIM), 0.02),
        "rel_bias": nrm(ks[15], (N_BUCKETS, DIFF_HEADS), 0.5),
        "fox_b_f": 3.0 + nrm(ks[16], (L, FOX_HEADS), 0.5),
        "gate_b": nrm(ks[17], (L, N_BRANCH, D_MODEL), 0.02),
        "w_br_rnn": nrm(ks[18], (L, D_RNN, D_MODEL), D_RNN ** -0.5),
        "w_br_diff": nrm(ks[19], (L, DIFF_WIDTH, D_MODEL), DIFF_WIDTH ** -0.5),
        "w_br_fox": nrm(ks[20], (L, FOX_WIDTH, D_MODEL), FOX_WIDTH ** -0.5),
        "w_out": nrm(ks[21], (L, D_MODEL, D_MODEL), D_MODEL ** -0.5),
        "norm2_g": 1.0 + nrm(ks[22], (L, D_MODEL), 0.02),
        "ffn_up": nrm(ks[23], (L, D_MODEL, 2 * D_FF), D_MODEL ** -0.5),
        "ffn_conv_w": nrm(ks[24], (L, CONV_FFN, 2 * D_FF), CONV_FFN ** -0.5),
        "ffn_conv_b": nrm(ks[25], (L, 2 * D_FF), 0.02),
        "ffn_down": nrm(ks[26], (L, D_FF, D_MODEL), D_FF ** -0.5),
        "final_g": 1.0 + nrm(ks[27], (D_MODEL,), 0.02),
    }

def first_block(x, norm1_g, w_in, rnn_conv_w, rnn_conv_b, rg_w_r, rg_b_r, rg_w_i, rg_b_i, rg_a,
              diff_lq1, diff_lk1, diff_lq2, diff_lk2, diff_subln_g, rel_bias, fox_b_f, gate_b,
              w_br_rnn, w_br_diff, w_br_fox, w_out, norm2_g, ffn_up, ffn_conv_w, ffn_conv_b,
              ffn_down, final_g):
    bsz, s_len, _ = x.shape
    for l in range(DEPTH):
        h = rmsnorm(x, norm1_g[l])
        proj = h @ w_in[l]
        (x_rnn, g_rnn, dq, dk, dv, fq, fk, fv, f_logit, gates) = jnp.split(proj, IN_SPLITS, axis=-1)

        x_rnn = causal_dwconv(x_rnn, rnn_conv_w[l], rnn_conv_b[l])
        y_rnn = jax.nn.gelu(g_rnn) * rg_lru(x_rnn, rg_w_r[l], rg_b_r[l], rg_w_i[l], rg_b_i[l], rg_a[l])

        lam_init = 0.8 - 0.6 * math.exp(-0.3 * l)
        lam = (jnp.exp(jnp.sum(diff_lq1[l] * diff_lk1[l]).astype(jnp.float32))
               - jnp.exp(jnp.sum(diff_lq2[l] * diff_lk2[l]).astype(jnp.float32)) + lam_init)
        o_diff = diff_attention(dq.reshape(bsz, s_len, DIFF_HEADS, 2, DIFF_HEAD_DIM),
                                dk.reshape(bsz, s_len, DIFF_HEADS, 2, DIFF_HEAD_DIM),
                                dv.reshape(bsz, s_len, DIFF_HEADS, 2 * DIFF_HEAD_DIM), lam, rel_bias)
        y_diff = (rmsnorm(o_diff, diff_subln_g[l]) * (1.0 - lam_init)).reshape(bsz, s_len, DIFF_WIDTH)

        log_f = jax.nn.log_sigmoid((f_logit + fox_b_f[l]).astype(jnp.float32))
        o_fox = forgetting_attention(fq.reshape(bsz, s_len, FOX_HEADS, FOX_HEAD_DIM),
                                     fk.reshape(bsz, s_len, FOX_HEADS, FOX_HEAD_DIM),
                                     fv.reshape(bsz, s_len, FOX_HEADS, FOX_HEAD_DIM), log_f)
        y_fox = o_fox.reshape(bsz, s_len, FOX_WIDTH)

        g = jax.nn.sigmoid(gates.reshape(bsz, s_len, N_BRANCH, D_MODEL) + gate_b[l])
        m = (g[:, :, 0] * (y_rnn @ w_br_rnn[l])
             + g[:, :, 1] * (y_diff @ w_br_diff[l])
             + g[:, :, 2] * (y_fox @ w_br_fox[l]))
        x = x + m @ w_out[l]

        h = rmsnorm(x, norm2_g[l])
        u = causal_dwconv(h @ ffn_up[l], ffn_conv_w[l], ffn_conv_b[l])
        u_gate, u_val = jnp.split(u, 2, axis=-1)
        x = x + (jax.nn.gelu(u_gate) * u_val) @ ffn_down[l]
    return rmsnorm(x, final_g)


DEPTH_2 = 2

GRID_W = 64
CTX_LEN = 256

RWKV_HEAD = 64
RWKV_WIDTH = D_MODEL
RWKV_HEADS = RWKV_WIDTH // RWKV_HEAD
LORA_W = 64
LORA_A = 64
LORA_G = 160
GN_EPS = RWKV_HEAD * 1e-5

CONV_CH = D_MODEL
CONV_K = 31

PEER_HEADS = 8
PEER_NKEYS = 128
PEER_EXPERTS = PEER_NKEYS * PEER_NKEYS
PEER_QDIM = 256
PEER_HALF = PEER_QDIM // 2
PEER_TOPK = 16
PEER_CHUNK = 256

N_BRANCH_2 = 2
NORM_EPS = 1e-6
LN_EPS = 1e-5

P_RWKV = 3 * RWKV_WIDTH + 2 * LORA_W + 2 * LORA_A + LORA_G
P_CONV = 2 * CONV_CH
P_GATE = N_BRANCH_2 * D_MODEL
P_IN = P_RWKV + P_CONV + P_GATE
RWKV_SPLITS = (RWKV_WIDTH, 2 * RWKV_WIDTH, 3 * RWKV_WIDTH,
               3 * RWKV_WIDTH + LORA_W, 3 * RWKV_WIDTH + 2 * LORA_W,
               3 * RWKV_WIDTH + 2 * LORA_W + LORA_A, 3 * RWKV_WIDTH + 2 * LORA_W + 2 * LORA_A)


def rmsnorm_2(x, g):
    xf = x.astype(jnp.float32)
    y = xf * lax.rsqrt(jnp.mean(xf * xf, axis=-1, keepdims=True) + NORM_EPS)
    return (y * g.astype(jnp.float32)).astype(x.dtype)

def layernorm(x, g, b):
    xf = x.astype(jnp.float32)
    mu = jnp.mean(xf, axis=-1, keepdims=True)
    var = jnp.mean(jnp.square(xf - mu), axis=-1, keepdims=True)
    return ((xf - mu) * lax.rsqrt(var + LN_EPS) * g + b).astype(x.dtype)

def modulate(x, g, shift, scale):
    return rmsnorm_2(x, g) * (1 + scale) + shift

def token_shift(z, mu):
    zp = jnp.pad(z[:, :-1], ((0, 0), (1, 0), (0, 0)))
    zn = jnp.pad(z[:, 1:], ((0, 0), (0, 1), (0, 0)))
    return z + mu[0] * (zp - z) + mu[1] * (zn - z)

def rwkv_scan(decay, k, v, kk, a, r, s0, reverse):
    emit = r is not None
    seq = (decay, k, v, kk, a) + ((r,) if emit else ())
    xs = tuple(jnp.moveaxis(t.astype(jnp.float32), 1, 0) for t in seq)

    def step(S, inp):
        w_t, k_t, v_t, kk_t, a_t = inp[:5]
        sa = jnp.einsum('bhvk,bhk->bhv', S, kk_t)
        S = (S * w_t[:, :, None, :]
             - sa[..., None] * (kk_t * a_t)[:, :, None, :]
             + v_t[..., None] * k_t[:, :, None, :])
        y = jnp.einsum('bhvk,bhk->bhv', S, inp[5]) if emit else None
        return S, y

    S, ys = lax.scan(step, s0, xs, reverse=reverse)
    return S, (jnp.moveaxis(ys, 0, 1) if emit else None)

def rwkv_branch(zr, p, s0, emit):
    B, L, _ = zr.shape
    H, N = RWKV_HEADS, RWKV_HEAD
    r, k, v, w1f, w1b, a1f, a1b, g1 = jnp.split(zr, RWKV_SPLITS, axis=-1)
    heads = lambda t: t.reshape(B, L, H, N)
    kkr = heads(k * p['k_k']).astype(jnp.float32)
    kk = kkr / jnp.maximum(jnp.sqrt(jnp.sum(kkr * kkr, axis=-1, keepdims=True)), 1e-12)
    states, outs, bonus = [], [], []
    for d, (w1d, a1d) in enumerate(((w1f, a1f), (w1b, a1b))):
        wlog = -jax.nn.softplus(-(p['w0'][d] + jnp.tanh(w1d) @ p['w2'][d])) - 0.5
        decay = jnp.exp(-jnp.exp(wlog.astype(jnp.float32)))
        a = jax.nn.sigmoid(a1d @ p['a2'][d] + p['a0'][d])
        kd = k * (1 + (a - 1) * p['k_a'])
        S, y = rwkv_scan(heads(decay), heads(kd), heads(v), kk, heads(a),
                         heads(r) if emit else None, s0[d], reverse=(d == 1))
        states.append(S)
        if emit:
            outs.append(y)
            bonus.append(jnp.sum(heads(r * kd) * p['r_k'], axis=-1, keepdims=True))
    if not emit:
        return None, (states[0], states[1])
    o = outs[0] + outs[1]
    mu = jnp.mean(o, axis=-1, keepdims=True)
    var = jnp.mean(jnp.square(o - mu), axis=-1, keepdims=True)
    o = ((o - mu) * lax.rsqrt(var + GN_EPS)).reshape(B, L, RWKV_WIDTH) * p['lnx_g'] + p['lnx_b']
    o = o + ((bonus[0] + bonus[1]).astype(jnp.float32) * heads(v).astype(jnp.float32)).reshape(B, L, RWKV_WIDTH)
    g = jax.nn.sigmoid(g1) @ p['g2']
    y = (o.astype(zr.dtype) * g) @ p['w_oA']
    return y, (states[0], states[1])

def conv_branch(zc, p, rows):
    B, L, _ = zc.shape
    u = zc[..., :CONV_CH] * jax.nn.sigmoid(zc[..., CONV_CH:])
    img = u.reshape(B, rows, GRID_W, CONV_CH) if rows is not None else u[:, :, None, :]
    rhs = p['conv_w'][:, None, None, :].astype(img.dtype)
    out = lax.conv_general_dilated(img, rhs, window_strides=(1, 1),
                                   padding=((CONV_K // 2, CONV_K // 2), (0, 0)),
                                   dimension_numbers=('NHWC', 'HWIO', 'NHWC'),
                                   feature_group_count=CONV_CH)
    out = layernorm(out.reshape(B, L, CONV_CH), p['cnorm_g'], p['cnorm_b'])
    return jax.nn.silu(out) @ p['w_oB']

def token_mixer(h, p, rows, s0, emit):
    w_in = p['w_in'] if emit else p['w_in'][:, :P_RWKV]
    z = h @ w_in
    zr = token_shift(z[..., :P_RWKV], p['shift_mu'])
    y_a, states = rwkv_branch(zr, p, s0, emit)
    if not emit:
        return None, states
    y_b = conv_branch(z[..., P_RWKV:P_RWKV + P_CONV], p, rows)
    gates = jax.nn.sigmoid(z[..., P_RWKV + P_CONV:] + p['gate_b'])
    m = gates[..., :D_MODEL] * y_a + gates[..., D_MODEL:] * y_b
    return m @ p['w_out'], states

def peer(h, p):
    B, L, D = h.shape
    T = B * L
    chunk = math.gcd(T, PEER_CHUNK)
    hb = h.reshape(T // chunk, chunk, D)

    def block(hc):
        q = (hc @ p['w_q']).reshape(chunk, PEER_HEADS, 2, PEER_HALF)
        s = jnp.einsum('thcd,hcnd->thcn', q, p['sub_keys']).astype(jnp.float32)
        s1, i1 = lax.top_k(s[:, :, 0], PEER_TOPK)
        s2, i2 = lax.top_k(s[:, :, 1], PEER_TOPK)
        cand = (s1[..., :, None] + s2[..., None, :]).reshape(chunk, PEER_HEADS, PEER_TOPK * PEER_TOPK)
        cidx = (i1[..., :, None] * PEER_NKEYS + i2[..., None, :]).reshape(chunk, PEER_HEADS, PEER_TOPK * PEER_TOPK)
        best, pos = lax.top_k(cand, PEER_TOPK)
        eidx = jnp.take_along_axis(cidx, pos, axis=-1)
        gw = jax.nn.softmax(best, axis=-1)
        u = jnp.take(p['peer_u'], eidx, axis=0)
        act = jax.nn.gelu(jnp.einsum('td,thkd->thk', hc, u).astype(jnp.float32), approximate=False) * gw
        v = jnp.take(p['peer_v'], eidx, axis=0)
        return jnp.einsum('thk,thkd->td', act.astype(hc.dtype), v)

    return lax.map(block, hb).reshape(B, L, D)

def second_inputs(seed: int = 0) -> dict:
    key = jax.random.key(seed)
    ks = jax.random.split(key, 40)
    f32 = jnp.float32
    nrm = lambda k, shape, s: jax.random.normal(k, shape, f32) * s
    Ly, D, W, H = DEPTH_2, D_MODEL, RWKV_WIDTH, RWKV_HEADS
    return {
        'x': nrm(ks[0], (BATCH, SEQ, D), 1.0),
        'c': nrm(ks[1], (BATCH, D), 1.0),
        'ctx': nrm(ks[2], (BATCH, CTX_LEN, D), 1.0),
        'c_ctx': nrm(ks[3], (D,), 1.0),
        'ada_w': nrm(ks[4], (Ly, D, 6 * D), 0.5 * D ** -0.5),
        'ada_b': nrm(ks[5], (Ly, 6 * D), 0.02),
        'norm1_g': 1.0 + nrm(ks[6], (Ly, D), 0.02),
        'norm2_g': 1.0 + nrm(ks[7], (Ly, D), 0.02),
        'w_in': nrm(ks[8], (Ly, D, P_IN), D ** -0.5),
        'shift_mu': jax.random.uniform(ks[9], (Ly, 2, P_RWKV), f32, 0.0, 0.5),
        'w0': jax.random.uniform(ks[10], (Ly, 2, W), f32, -6.0, 1.0),
        'w2': nrm(ks[11], (Ly, 2, LORA_W, W), 0.5 * LORA_W ** -0.5),
        'a0': nrm(ks[12], (Ly, 2, W), 0.5),
        'a2': nrm(ks[13], (Ly, 2, LORA_A, W), 0.5 * LORA_A ** -0.5),
        'g2': nrm(ks[14], (Ly, LORA_G, W), LORA_G ** -0.5),
        'k_k': 0.85 + nrm(ks[15], (Ly, W), 0.05),
        'k_a': 1.0 + nrm(ks[16], (Ly, W), 0.05),
        'r_k': nrm(ks[17], (Ly, H, RWKV_HEAD), 0.1),
        'lnx_g': 1.0 + nrm(ks[18], (Ly, W), 0.02),
        'lnx_b': nrm(ks[19], (Ly, W), 0.02),
        'w_oA': nrm(ks[20], (Ly, W, D), W ** -0.5),
        'conv_w': nrm(ks[21], (Ly, CONV_K, CONV_CH), CONV_K ** -0.5),
        'cnorm_g': 1.0 + nrm(ks[22], (Ly, CONV_CH), 0.02),
        'cnorm_b': nrm(ks[23], (Ly, CONV_CH), 0.02),
        'w_oB': nrm(ks[24], (Ly, CONV_CH, D), CONV_CH ** -0.5),
        'gate_b': nrm(ks[25], (Ly, P_GATE), 0.02),
        'w_out': nrm(ks[26], (Ly, D, D), D ** -0.5),
        'w_q': nrm(ks[27], (Ly, D, PEER_HEADS * PEER_QDIM), D ** -0.5),
        'sub_keys': nrm(ks[28], (Ly, PEER_HEADS, 2, PEER_NKEYS, PEER_HALF), PEER_HALF ** -0.5),
        'peer_u': nrm(ks[29], (Ly, PEER_EXPERTS, D), D ** -0.5),
        'peer_v': nrm(ks[30], (Ly, PEER_EXPERTS, D), 0.5),
        'final_g': 1.0 + nrm(ks[31], (D,), 0.02),
    }

def second_block(x, c, ctx, c_ctx, ada_w, ada_b, norm1_g, norm2_g, w_in, shift_mu, w0, w2, a0, a2, g2,
              k_k, k_a, r_k, lnx_g, lnx_b, w_oA, conv_w, cnorm_g, cnorm_b, w_oB, gate_b, w_out,
              w_q, sub_keys, peer_u, peer_v, final_g):
    B = x.shape[0]
    rows = x.shape[1] // GRID_W
    xc = ctx
    zero_state = jnp.zeros((B, RWKV_HEADS, RWKV_HEAD, RWKV_HEAD), jnp.float32)
    for l in range(DEPTH_2):
        last = l == DEPTH_2 - 1
        p = dict(w_in=w_in[l], shift_mu=shift_mu[l], w0=w0[l], w2=w2[l], a0=a0[l], a2=a2[l],
                 g2=g2[l], k_k=k_k[l], k_a=k_a[l], r_k=r_k[l], lnx_g=lnx_g[l], lnx_b=lnx_b[l],
                 w_oA=w_oA[l], conv_w=conv_w[l], cnorm_g=cnorm_g[l], cnorm_b=cnorm_b[l],
                 w_oB=w_oB[l], gate_b=gate_b[l], w_out=w_out[l], w_q=w_q[l],
                 sub_keys=sub_keys[l], peer_u=peer_u[l], peer_v=peer_v[l])
        mod = jax.nn.silu(c) @ ada_w[l] + ada_b[l]
        sh1, sc1, gt1, sh2, sc2, gt2 = jnp.split(mod[:, None, :], 6, axis=-1)
        modc = jax.nn.silu(c_ctx) @ ada_w[l] + ada_b[l]
        csh1, csc1, cgt1, csh2, csc2, cgt2 = jnp.split(modc, 6, axis=-1)

        hc = modulate(xc, norm1_g[l], csh1, csc1)
        yc, ctx_states = token_mixer(hc, p, None, (zero_state, zero_state), emit=not last)

        h = modulate(x, norm1_g[l], sh1, sc1)
        y, _ = token_mixer(h, p, rows, ctx_states, emit=True)
        x = x + gt1 * y
        x = x + gt2 * peer(modulate(x, norm2_g[l], sh2, sc2), p)

        if not last:
            xc = xc + cgt1 * yc
            xc = xc + cgt2 * peer(modulate(xc, norm2_g[l], csh2, csc2), p)
    return rmsnorm_2(x, final_g)


def setup_inputs(seed=0):
    out = dict(first_inputs(seed))
    for name, value in second_inputs(seed + 1).items():
        if name != "x":
            out[name + "_2"] = value
    return out


def reference(
    x, norm1_g, w_in, rnn_conv_w, rnn_conv_b, rg_w_r, rg_b_r, rg_w_i, rg_b_i, rg_a, diff_lq1,
    diff_lk1, diff_lq2, diff_lk2, diff_subln_g, rel_bias, fox_b_f, gate_b, w_br_rnn, w_br_diff,
    w_br_fox, w_out, norm2_g, ffn_up, ffn_conv_w, ffn_conv_b, ffn_down, final_g, c_2, ctx_2,
    c_ctx_2, ada_w_2, ada_b_2, norm1_g_2, norm2_g_2, w_in_2, shift_mu_2, w0_2, w2_2, a0_2, a2_2,
    g2_2, k_k_2, k_a_2, r_k_2, lnx_g_2, lnx_b_2, w_oA_2, conv_w_2, cnorm_g_2, cnorm_b_2, w_oB_2,
    gate_b_2, w_out_2, w_q_2, sub_keys_2, peer_u_2, peer_v_2, final_g_2,
):
    x = first_block(
        x, norm1_g, w_in, rnn_conv_w, rnn_conv_b, rg_w_r, rg_b_r, rg_w_i, rg_b_i, rg_a,
        diff_lq1, diff_lk1, diff_lq2, diff_lk2, diff_subln_g, rel_bias, fox_b_f, gate_b,
        w_br_rnn, w_br_diff, w_br_fox, w_out, norm2_g, ffn_up, ffn_conv_w, ffn_conv_b, ffn_down,
        final_g,
    )
    return second_block(
        x, c_2, ctx_2, c_ctx_2, ada_w_2, ada_b_2, norm1_g_2, norm2_g_2, w_in_2, shift_mu_2,
        w0_2, w2_2, a0_2, a2_2, g2_2, k_k_2, k_a_2, r_k_2, lnx_g_2, lnx_b_2, w_oA_2, conv_w_2,
        cnorm_g_2, cnorm_b_2, w_oB_2, gate_b_2, w_out_2, w_q_2, sub_keys_2, peer_u_2, peer_v_2,
        final_g_2,
    )


_drawn_inputs = setup_inputs


def setup_inputs(seed=0):
    import zlib

    import numpy as np

    out = dict(_drawn_inputs(seed))
    spreads = {}
    factors = {'rg_b_r': 27.868,
     'rg_b_i': 8.0,
     'diff_lq1': 7.275,
     'diff_subln_g': 3.736,
     'gate_b': 5.486,
     'norm1_g_2': 5.032,
     'norm2_g_2': 19.733,
     'w2_2': 5.043,
     'k_k_2': 16.783,
     'k_a_2': 2.697,
     'lnx_g_2': 64.0,
     'lnx_b_2': 60.649,
     'cnorm_g_2': 53.728,
     'cnorm_b_2': 55.947,
     'gate_b_2': 8.0,
     'final_g_2': 7.947}
    for name, (base, spread) in spreads.items():
        noise = np.random.default_rng([zlib.crc32(name.encode()), seed]).standard_normal(out[name].shape)
        drawn = base * np.exp(spread * noise) if base else spread * noise
        out[name] = jnp.asarray(drawn.astype(out[name].dtype))
    for name, factor in factors.items():
        out[name] = (out[name] * factor).astype(out[name].dtype)
    return out
```

```python
import math
from contextlib import ExitStack

import numpy as np

import concourse.bass as bass
from concourse import mybir

F32 = mybir.dt.float32
U32 = mybir.dt.uint32
ALU = mybir.AluOpType
ACT = mybir.ActivationFunctionType
AX = mybir.AxisListType

P = 128
D = 1024
KD = D // P
SEQ = 256
CTX = 256
TT = SEQ // P
BANK = 512
NBANK = 8
EPS = 1e-6

RNN_BLOCKS = 8
CONV_RNN = 4
DIFF_HEADS = 4
FOX_HEADS = 8
HEAD = 64
D_FF = ((8 * D // 3 + 127) // 128) * 128
KF = D_FF // P
CONV_FFN = 3
N_BUCKETS = 32
LAM_INIT = 0.8 - 0.6 * math.exp(-0.3 * 0)
NEG = -1e30

LAYERS = 2
GRID_W = 64
RWKV_HEADS = 16
LORA_G = 160
GN_EPS = HEAD * 1e-5
LN_EPS = 1e-5
CONV_K = 31
P_RWKV = 3 * D + 4 * 64 + LORA_G
ZT = -(-P_RWKV // P)
PEER_HEADS = 8
NKEYS = 128
TOPK = 16
CHUNK = 64
NCH = SEQ // CHUNK
LEVELS = 6

RING = 2
SLOT = 4096



def tiles_of(a, kt):
    k, n = a.shape
    if k < kt * P:
        a = np.concatenate([a, np.zeros((kt * P - k, n), a.dtype)])
    return a.reshape(kt, P, n).transpose(1, 0, 2).reshape(P, kt * n)


def span(a, b):
    return [(a, b)]


def weight_plan():
    plan = []

    def add(section, name, layer, kt, spans):
        plan.append((section, name, layer, kt, spans, sum(b - a for a, b in spans)))

    for c in range(10):
        add("first", "w_in", 0, KD, span(512 * c, 512 * c + 512))
    add("first", "w_in", 0, KD, span(5120, 5128))
    for c in range(6):
        add("first", "w_in", 0, KD, span(5128 + 512 * c, 5640 + 512 * c))
    add("first", "rg", 0, 2 * RNN_BLOCKS, span(0, P))
    for c in range(2):
        add("first", "w_br_rnn", 0, 8, span(512 * c, 512 * c + 512))
        add("first", "w_br_diff", 0, 4, span(512 * c, 512 * c + 512))
        add("first", "w_br_fox", 0, 4, span(512 * c, 512 * c + 512))
    for c in range(2):
        add("first", "w_out", 0, KD, span(512 * c, 512 * c + 512))
    for c in range(KF // 2):
        add("first", "ffn_up", 0, KD, [(256 * c, 256 * c + 256), (D_FF + 256 * c, D_FF + 256 * c + 256)])
    for c in range(KD):
        add("first", "ffn_down", 0, KF, span(P * c, P * c + P))
    for layer in range(LAYERS):
        s = f"mixer{layer}"
        for c in range(12):
            add(s, "ada_w_2", layer, KD, span(512 * c, 512 * c + 512))
        for c in range(7):
            add(s, "w_in_2", layer, KD, span(512 * c, min(512 * c + 512, P_RWKV)))
        add(s, "lora_2", layer, 2, span(0, D))
        add(s, "g2_2", layer, 2, span(0, D))
        for c in range(4):
            a = P_RWKV + 256 * c
            add(s, "w_in_2", layer, KD, [(a, a + 256), (a + D, a + D + 256)])
        for c in range(4):
            a = P_RWKV + 2 * D + 512 * c
            add(s, "w_in_2", layer, KD, span(a, a + 512))
        for c in range(2):
            add(s, "w_oA_2", layer, KD, span(512 * c, 512 * c + 512))
        for c in range(2):
            add(s, "w_oB_2", layer, KD, span(512 * c, 512 * c + 512))
        for c in range(2):
            add(s, "w_out_2", layer, KD, span(512 * c, 512 * c + 512))
        s = f"peer{layer}"
        for c in range(4):
            add(s, "w_q_2", layer, KD, span(512 * c, 512 * c + 512))
        add(s, "keys_2", layer, 2 * PEER_HEADS, span(0, NKEYS))
    return plan


def weight_stream(inputs):
    w = dict(inputs)
    w["rg"] = np.concatenate([inputs["rg_w_r"], inputs["rg_w_i"]], 1).reshape(1, 2 * D, P)
    w["lora_2"] = np.concatenate([inputs["w2_2"].reshape(LAYERS, P, D), inputs["a2_2"].reshape(LAYERS, P, D)], 1)
    w["keys_2"] = inputs["sub_keys_2"].transpose(0, 1, 2, 4, 3).reshape(LAYERS, 2 * PEER_HEADS * P, NKEYS)
    blobs = []
    for _, name, layer, kt, spans, _ in weight_plan():
        cols = np.concatenate([w[name][layer][:, a:b] for a, b in spans], 1)
        blobs.append(tiles_of(cols, kt).reshape(-1))
    return np.concatenate(blobs)


def vector_plan():
    plan, width = {}, {}

    def group(name, start, entries):
        at = start
        for key, n in entries:
            plan[key] = (name, at, n)
            at += n
        width[name] = at - start
        return at

    common = group("common", 0, [("c_ctx_2", 8), ("c_2", 8), ("final_g_2", 8)])
    ends = [group("first", common, [
        ("norm1_g", 8), ("norm2_g", 8), ("final_g", 8), ("rnn_conv_w", 32), ("rnn_conv_b", 8), ("rg_b_r", 8), ("rg_b_i", 8),
        ("rg_a", 8), ("gate_b", 24), ("diff_subln_g", 1), ("diff_lq1", 1), ("diff_lk1", 1), ("diff_lq2", 1), ("diff_lk2", 1),
        ("fox_b_f", 1), ("ffn_conv_w", CONV_FFN * 2 * KF), ("ffn_conv_b", 2 * KF)])]
    for layer in range(LAYERS):
        ends.append(group(layer, common, [((name, layer), n) for name, n in (
            ("norm1_g_2", 8), ("norm2_g_2", 8), ("ada_b_2", 48), ("shift_mu_2", 2 * ZT), ("w0_2", 16), ("a0_2", 16),
            ("k_k_2", 8), ("k_a_2", 8), ("r_k_2", 8), ("lnx_g_2", 8), ("lnx_b_2", 8), ("conv_w_2", CONV_K * 8),
            ("cnorm_g_2", 8), ("cnorm_b_2", 8), ("gate_b_2", 16))]))
    return plan, width, max(ends)


def vector_arrays(inputs):
    plan, width, _ = vector_plan()
    out = {f"vectors_{g}": np.zeros((P, n), np.float32) for g, n in width.items()}
    for key, (g, at, n) in plan.items():
        v = inputs[key[0]][key[1]] if isinstance(key, tuple) else inputs[key]
        dst = out[f"vectors_{g}"]
        at -= 0 if g == "common" else width["common"]
        if key in ("diff_lq1", "diff_lk1", "diff_lq2", "diff_lk2", "fox_b_f"):
            dst[: v.size, at] = v.reshape(-1)
            continue
        if isinstance(key, tuple) and key[0] == "shift_mu_2":
            v = np.concatenate([v, np.zeros((2, ZT * P - P_RWKV), v.dtype)], 1)
        dst[:, at:at + n] = v.reshape(n, P).T
    return out


def constants():
    i = np.arange(P)
    t = i[:, None] % CHUNK
    s = np.arange(CHUNK)[None, :]
    tb, sb = i[:, None], i[None, :]
    same_head = tb // CHUNK == sb // CHUNK
    c = {
        "ident": np.eye(P),
        "ones": np.ones((P, P)),
        "head_ones": (i[:, None] // HEAD == i[None, :] // HEAD).astype(np.float32),
        "causal": np.where(i[:, None] >= i[None, :], 0.0, NEG),
        "above_bd": same_head & (sb > tb), "upto": (s >= t),
        "levels": np.concatenate([same_head & (tb // (2 * b) == sb // (2 * b)) & (tb // b > sb // b) for b in (2 ** j for j in range(LEVELS))]
                                 + [same_head & (tb // 2 == sb // 2) & (tb < sb)], 1),
        "iota": np.broadcast_to(i[None, :], (P, P)),
        "iota16": np.broadcast_to(np.arange(TOPK)[None, :], (P, TOPK)),
        "row_head": np.repeat(np.eye(P, FOX_HEADS), SEQ, axis=1),
    }
    dist = np.arange(-(SEQ - 1), SEQ)
    n = np.maximum(dist, 0)
    half = N_BUCKETS // 2
    large = half + (np.log(np.maximum(n, 1).astype(np.float32) / np.float32(half)) / math.log(128 / half)
                    * (N_BUCKETS - half)).astype(np.int32)
    bucket = np.where(n < half, n, np.minimum(large, N_BUCKETS - 1))
    c["buckets"] = np.arange(P)[:, None] == bucket[None, :]
    return {k: np.asarray(v, np.float32) for k, v in c.items()}



class Count:

    def __init__(self, nc, stack, name):
        self.sem = stack.enter_context(nc.semaphore(name))
        self.base = self.pending = 0

    def up(self, by=1):
        self.pending += by
        return by

    def at(self, k):
        return self.base + k

    def now(self):
        return self.base + self.pending

    def settle(self):
        self.base += self.pending
        self.pending = 0


class Steps:

    def __init__(self, engine, count):
        self.engine, self.count = engine, count

    def __call__(self, instruction):
        instruction.then_inc(self.count.sem, self.count.up())
        self.engine.wait_ge(self.count.sem, self.count.now())


class WeightRing:

    def __init__(self, nc, stack, slots, stream):
        self.slots, self.stream = slots, stream
        self.loaded = [stack.enter_context(nc.semaphore(f"weights_loaded_{i}")) for i in range(RING)]
        self.plan = weight_plan()
        self.offset = list(np.cumsum([0] + [P * kt * n for _, _, _, kt, _, n in self.plan]))
        self.used = []
        self.issued = 0

    def last_of(self, section):
        return max(i for i, c in enumerate(self.plan) if c[0] == section) + 1

    def chunk(self, n):
        kt, width = self.plan[n][3], self.plan[n][5]
        return self.slots[n % RING][:, 0:kt * width].rearrange("p (k n) -> p k n", k=kt)

    def at(self, n):
        return 16 * (n // RING + 1)

    def release(self, n, mark):
        assert len(self.used) == n
        self.used.append(mark)

    def load(self, engine, section):
        end = min(self.last_of(section), len(self.used) + RING)
        while self.issued < end:
            n = self.issued
            if n >= RING:
                count, value = self.used[n - RING]
                engine.wait_ge(count.sem, value)
            kt, width = self.plan[n][3], self.plan[n][5]
            a, b = int(self.offset[n]), int(self.offset[n + 1])
            engine.dma_start(self.slots[n % RING][:, 0:kt * width],
                             self.stream[a:b].rearrange("(p n) -> p n", p=P)).then_inc(self.loaded[n % RING], 16)
            self.issued += 1


class Core:

    def __init__(self, nc, stack, dram):
        self.nc, self.stack, self.dram = nc, stack, dram
        self.counts = []
        self.product = self.count("product_ready")
        self.act_read = self.count("scalar_has_read")
        self.dve_read = self.count("vector_has_read")
        self.act_step = self.count("scalar_step")
        self.dve_step = self.count("vector_step")
        self.from_act = self.count("scalar_result_ready")
        self.from_dve = self.count("vector_result_ready")
        self.vector_max = self.count("row_maximum_ready")
        self.landed = self.count("small_load_landed")
        self.stored = self.count("store_done")
        self.banks = stack.enter_context(nc.psum_tensor("banks", [P, NBANK, BANK], F32))
        self.const = {}
        self.n_tensors = 0
        self.vec = None
        self.plan, self.vector_width, self.nvec = vector_plan()
        self.ring = None
        self.next_chunk = 0

    def count(self, name):
        c = Count(self.nc, self.stack, name)
        self.counts.append(c)
        return c

    def sb(self, stack, name, shape, dtype=F32):
        self.n_tensors += 1
        return stack.enter_context(self.nc.sbuf_tensor(f"{name}_{self.n_tensors}", shape, dtype))

    def vector_load(self, group):
        at = 0 if group == "common" else self.vector_width["common"]
        return self.vec[:, at:at + self.vector_width[group]], self.dram[f"vectors_{group}"]

    def settle(self):
        for c in self.counts:
            c.settle()

    def v(self, key, i=0, n=1):
        _, at, width = self.plan[key]
        assert i + n <= width
        return self.vec[:, at + i:at + i + n]


def columns(ap, width):
    return ap.unsqueeze(2).broadcast_to([ap.shape[0], ap.shape[1], width])


def rows(ap, n):
    return ap.unsqueeze(1).broadcast_to([ap.shape[0], n, ap.shape[1]])


def load_stage(core, section):
    nc = core.nc
    with nc.Block() as block:

        @block.sync
        def _(sp):
            n = 0
            for dst, src in core.first_loads:
                sp.dma_start(dst, src).then_inc(core.landed.sem, core.landed.up(16))
                n += 16
            sp.wait_ge(core.landed.sem, core.landed.at(n))
            core.ring.load(sp, section)
    core.settle()


def norm_stage(core, src, dst, squares, rstd, segments, gain, shift, section, eps=EPS):
    nc = core.nc
    length = src.shape[2]
    mean = core.banks[:, 0, 0:length]
    with nc.Block() as block:

        @block.tensor
        def _(pe):
            pe.wait_ge(core.from_dve.sem, core.from_dve.at(1))
            for k in range(KD):
                last = nc.tensor.matmul(mean, core.const["ones"], squares[:, k, :], start=k == 0, stop=k == KD - 1)
            last.then_inc(core.product.sem, core.product.up())

        @block.scalar
        def _(act):
            act.wait_ge(core.from_dve.sem, core.from_dve.at(2))
            nc.scalar.activation(rstd, rstd, ACT.Sqrt).then_inc(core.from_act.sem, core.from_act.up())

        @block.vector
        def _(dve):
            step = Steps(dve, core.dve_step)
            nc.vector.tensor_tensor(squares, src, src, ALU.mult).then_inc(core.from_dve.sem, core.from_dve.up())
            dve.wait_ge(core.product.sem, core.product.at(1))
            nc.vector.tensor_scalar(rstd, mean, 1.0 / D, eps, ALU.mult, ALU.add).then_inc(core.from_dve.sem, core.from_dve.up())
            dve.wait_ge(core.from_act.sem, core.from_act.at(1))
            step(nc.vector.reciprocal(rstd, rstd))
            for k in range(KD):
                for i, (a, b) in enumerate(segments):
                    step(nc.vector.scalar_tensor_tensor(dst[:, k, a:b], src[:, k, a:b], gain(k, i), rstd[:, a:b],
                                                        ALU.mult, ALU.mult))
                    if shift is not None:
                        step(nc.vector.tensor_scalar(dst[:, k, a:b], dst[:, k, a:b], shift(k, i), None, ALU.add))

        @block.sync
        def _(sp):
            core.ring.load(sp, section)
    core.settle()


class Group:

    def __init__(self, reader, parts, evacuate, rows=P, cols=BANK, chunks=(), frees=()):
        self.reader, self.parts, self.evacuate = reader, parts, evacuate
        self.rows, self.cols, self.chunks, self.frees = rows, cols, chunks, frees


def product_stage(core, groups, section, stage_banks=NBANK, side=None):
    nc = core.nc
    rank, n = [], {"act": 0, "dve": 0}
    for g in groups:
        n[g.reader] += 1
        rank.append(n[g.reader])
    reads = {"act": core.act_read, "dve": core.dve_read}

    def bank(i):
        g = groups[i]
        return core.banks[0:g.rows, i % stage_banks, 0:g.cols]

    with nc.Block() as block:

        @block.tensor
        def _(pe):
            for i, g in enumerate(groups):
                if i >= stage_banks:
                    j = i - stage_banks
                    pe.wait_ge(reads[groups[j].reader].sem, reads[groups[j].reader].at(rank[j]))
                for c in g.chunks:
                    pe.wait_ge(core.ring.loaded[c % RING], core.ring.at(c))
                for k, (lhsT, rhs) in enumerate(g.parts):
                    last = nc.tensor.matmul(bank(i), lhsT, rhs, start=k == 0, stop=k == len(g.parts) - 1)
                last.then_inc(core.product.sem, core.product.up())
                for c in g.frees:
                    core.ring.release(c, (core.product, core.product.now()))

        @block.scalar
        def _(act):
            step = Steps(act, core.act_step)
            for i, g in enumerate(groups):
                if g.reader == "act":
                    act.wait_ge(core.product.sem, core.product.at(i + 1))
                    g.evacuate(step, bank(i)).then_inc(core.act_read.sem, core.act_read.up())
                    act.wait_ge(core.act_read.sem, core.act_read.now())
            if side is not None:
                side(act)

        @block.vector
        def _(dve):
            step = Steps(dve, core.dve_step)
            for i, g in enumerate(groups):
                if g.reader == "dve":
                    dve.wait_ge(core.product.sem, core.product.at(i + 1))
                    g.evacuate(step, bank(i)).then_inc(core.dve_read.sem, core.dve_read.up())
                    dve.wait_ge(core.dve_read.sem, core.dve_read.now())

        @block.sync
        def _(sp):
            core.ring.load(sp, section)
    core.settle()


def weight_groups(core, n_chunks, kt, moving, length, reader, evacuate):
    groups, m = [], 0
    for _ in range(n_chunks):
        c = core.next_chunk
        core.next_chunk += 1
        w = core.ring.chunk(c)
        width = w.shape[2]
        n_m = -(-width // P)
        for j in range(n_m):
            rows_here = min(P, width - P * j)
            parts = [(w[:, k, P * j:P * j + rows_here], moving(k)) for k in range(kt)]
            groups.append(Group(reader(m), parts, evacuate(m), rows_here, length,
                                chunks=(c,) if j == 0 else (), frees=(c,) if j == n_m - 1 else ()))
            m += 1
    return groups


def token_groups(core, kt, stationary, reader, evacuate):
    c = core.next_chunk
    core.next_chunk += 1
    w = core.ring.chunk(c)
    return [Group(reader, [(stationary(k, t), w[:, k, :]) for k in range(kt)], evacuate(t), P, w.shape[2],
                  chunks=(c,) if t == 0 else (), frees=(c,) if t == TT - 1 else ()) for t in range(TT)]


def copy_to(core, dst):
    return lambda step, ps: core.nc.vector.tensor_copy(dst, ps)


def act_to(core, dst, func, bias=0.0, scale=1.0):
    return lambda step, ps: core.nc.scalar.activation(dst, ps, func, bias=bias, scale=scale)


def projection_stage(core, h, out):
    def moving(k):
        return h[:, k, :]

    dve, act = (lambda m: "dve"), (lambda m: "act")
    g = weight_groups(core, 2, KD, moving, SEQ, dve, lambda m: copy_to(core, out["x_rnn"][:, m, :]))
    g += weight_groups(core, 2, KD, moving, SEQ, act, lambda m: act_to(core, out["g_rnn"][:, m, :], ACT.Gelu_apprx_tanh))
    g += weight_groups(core, 1, KD, moving, SEQ, dve, lambda m: copy_to(core, out["dq"][:, m, :]))
    g += weight_groups(core, 1, KD, moving, SEQ, dve, lambda m: copy_to(core, out["dk"][:, m, :]))
    g += token_groups(core, KD, lambda k, t: h[:, k, P * t:P * t + P], "dve", lambda t: copy_to(core, out["dv"][:, t, :]))
    g += weight_groups(core, 1, KD, moving, SEQ, dve, lambda m: copy_to(core, out["fq"][:, m, :]))
    g += weight_groups(core, 1, KD, moving, SEQ, dve, lambda m: copy_to(core, out["fk"][:, m, :]))
    g += token_groups(core, KD, lambda k, t: h[:, k, P * t:P * t + P], "dve", lambda t: copy_to(core, out["fv"][:, t, :]))
    g += weight_groups(core, 1, KD, moving, SEQ, act, lambda m: act_to(core, out["f_logit"], ACT.Identity,
                                                                       core.v("fox_b_f")[0:FOX_HEADS]))
    g += weight_groups(core, 6, KD, moving, SEQ, act, lambda m: act_to(core, out["gates"][:, m, :], ACT.Sigmoid,
                                                                       core.v("gate_b", m)))
    product_stage(core, g, "mixer0")


def softplus_steps(core, step, act_ready, dve, x, tmp, out, exp_result):
    nc = core.nc
    s, s2, p = tmp
    act_ready()
    step(nc.vector.tensor_scalar(s2, exp_result, 2.0, None, ALU.add))
    step(nc.vector.reciprocal(s2, s2))
    step(nc.vector.tensor_tensor(s, exp_result, s2, ALU.mult))
    step(nc.vector.tensor_tensor(s2, s, s, ALU.mult))
    step(nc.vector.tensor_scalar(p, s2, 1.0 / 17, None, ALU.mult))
    for n in (15, 13, 11, 9, 7, 5, 3):
        step(nc.vector.scalar_tensor_tensor(p, p, 1.0 / n, s2, ALU.add, ALU.mult))
    step(nc.vector.scalar_tensor_tensor(p, p, 1.0, s, ALU.add, ALU.mult))
    step(nc.vector.tensor_scalar(p, p, 2.0, None, ALU.mult))
    step(nc.vector.scalar_tensor_tensor(out, x, 0.0, p, ALU.max, ALU.add))


def rnn_stage(core, stack, out, y):
    nc = core.nc
    xr, g = out["x_rnn"], out["g_rnn"]
    xc = core.sb(stack, "rnn_conv", [P, KD, SEQ])
    r = core.sb(stack, "rnn_r", [P, KD, SEQ])
    i_gate = core.sb(stack, "rnn_i", [P, KD, SEQ])
    a = core.sb(stack, "rnn_a", [P, KD, SEQ])
    neg_a, small = core.sb(stack, "rnn_neg_a", [P, KD]), core.sb(stack, "rnn_small", [P, 5, KD])
    c = core.next_chunk
    core.next_chunk += 1
    w = core.ring.chunk(c)

    with nc.Block() as block:

        @block.tensor
        def _(pe):
            pe.wait_ge(core.ring.loaded[c % RING], core.ring.at(c))
            pe.wait_ge(core.from_dve.sem, core.from_dve.at(2))
            for n in range(2 * RNN_BLOCKS):
                if n >= NBANK:
                    pe.wait_ge(core.act_read.sem, core.act_read.at(n - NBANK + 1))
                nc.tensor.matmul(core.banks[:, n % NBANK, 0:SEQ], w[:, n, :], xc[:, n % RNN_BLOCKS, :],
                                                         start=True, stop=True).then_inc(core.product.sem, core.product.up())
            core.ring.release(c, (core.product, core.product.now()))

        @block.scalar
        def _(act):
            step = Steps(act, core.act_step)
            act.wait_ge(core.from_dve.sem, core.from_dve.at(1))
            nc.scalar.activation(small[:, 4, :], neg_a[:, :], ACT.Exp).then_inc(core.from_act.sem, core.from_act.up())
            for n in range(2 * RNN_BLOCKS):
                act.wait_ge(core.product.sem, core.product.at(n + 1))
                gate, bias = (r, "rg_b_r") if n < RNN_BLOCKS else (i_gate, "rg_b_i")
                nc.scalar.activation(gate[:, n % RNN_BLOCKS, :], core.banks[:, n % NBANK, 0:SEQ], ACT.Sigmoid,
                                                       bias=core.v(bias, n % RNN_BLOCKS)).then_inc(core.act_read.sem, core.act_read.up())
            act.wait_ge(core.from_dve.sem, core.from_dve.at(3))
            step(nc.scalar.activation(a[:, :, :], r[:, :, :], ACT.Exp))
            nc.scalar.activation(r[:, :, :], r[:, :, :], ACT.Tanh, scale=-1.0).then_inc(core.from_act.sem, core.from_act.up())
            act.wait_ge(core.from_dve.sem, core.from_dve.at(4))
            nc.scalar.activation(r[:, :, :], r[:, :, :], ACT.Sqrt).then_inc(core.from_act.sem, core.from_act.up())

        @block.vector
        def _(dve):
            step = Steps(dve, core.dve_step)
            step(nc.vector.tensor_scalar(small[:, 0, :], core.v("rg_a", 0, 8), -1.0, None, ALU.mult))
            step(nc.vector.tensor_tensor(neg_a[:, :], small[:, 0, :], core.v("rg_a", 0, 8), ALU.min))
            nc.vector.tensor_scalar(neg_a[:, :], neg_a[:, :], 1.0, None, ALU.mult).then_inc(core.from_dve.sem, core.from_dve.up())
            for n in range(KD):
                w0 = core.v("rnn_conv_w", n + 24)
                step(nc.vector.tensor_scalar(xc[:, n, :], xr[:, n, :], w0, core.v("rnn_conv_b", n), ALU.mult, ALU.add))
                for d in range(1, CONV_RNN):
                    wd = core.v("rnn_conv_w", 8 * (CONV_RNN - 1 - d) + n)
                    last = nc.vector.scalar_tensor_tensor(xc[:, n, d:], xr[:, n, 0:SEQ - d], wd, xc[:, n, d:], ALU.mult, ALU.add)
                    if n == KD - 1 and d == CONV_RNN - 1:
                        last.then_inc(core.from_dve.sem, core.from_dve.up())
                    else:
                        step(last)
            softplus_steps(core, step, lambda: dve.wait_ge(core.from_act.sem, core.from_act.at(1)), dve, small[:, 0, :],
                           (small[:, 1, :], small[:, 2, :], small[:, 3, :]), neg_a[:, :], small[:, 4, :])
            dve.wait_ge(core.act_read.sem, core.act_read.at(2 * RNN_BLOCKS))
            for n in range(KD):
                last = nc.vector.tensor_scalar(r[:, n, :], r[:, n, :], neg_a[:, n:n + 1], -8.0, ALU.mult, ALU.mult)
                last.then_inc(core.from_dve.sem, core.from_dve.up()) if n == KD - 1 else step(last)
            step(nc.vector.tensor_tensor(i_gate[:, :, :], i_gate[:, :, :], xc[:, :, :], ALU.mult))
            dve.wait_ge(core.from_act.sem, core.from_act.at(2))
            step(nc.vector.tensor_tensor(xc[:, :, :], a[:, :, :], a[:, :, :], ALU.mult))
            nc.vector.scalar_tensor_tensor(r[:, :, :], xc[:, :, :], 1.0, r[:, :, :], ALU.add, ALU.mult).then_inc(core.from_dve.sem, core.from_dve.up())
            dve.wait_ge(core.from_act.sem, core.from_act.at(3))
            step(nc.vector.tensor_tensor(i_gate[:, :, :], i_gate[:, :, :], r[:, :, :], ALU.mult))
            for n in range(KD):
                step(nc.vector.tensor_tensor_scan(y[:, n, :], a[:, n, :], i_gate[:, n, :], 0.0, ALU.mult, ALU.add))
            step(nc.vector.tensor_tensor(y[:, :, :], y[:, :, :], g[:, :, :], ALU.mult))

        @block.sync
        def _(sp):
            core.ring.load(sp, "mixer0")
    core.settle()


def attention_setup_stage(core, work, out, rel_bias, buckets):
    nc = core.nc
    lam, prod, f = work["lam"], work["lam_products"], work["f"]
    bias = work["bias"]
    with nc.Block() as block:

        @block.tensor
        def _(pe):
            pe.wait_ge(core.from_dve.sem, core.from_dve.at(1))
            nc.tensor.matmul(core.banks[:, 0, 0:2], core.const["ones"], prod[:, :], start=True, stop=True).then_inc(core.product.sem, core.product.up())
            for k in range(SEQ):
                last = nc.tensor.matmul(core.banks[:, 1 + k // P, DIFF_HEADS * (k % P):DIFF_HEADS * (k % P) + DIFF_HEADS],
                                        buckets[:, SEQ - 1 + P - k:SEQ - 1 + 2 * P - k], rel_bias[:, :], start=True, stop=True)
            last.then_inc(core.product.sem, core.product.up())

        @block.scalar
        def _(act):
            act.wait_ge(core.product.sem, core.product.at(1))
            nc.scalar.activation(lam[:, 0:2], core.banks[:, 0, 0:2], ACT.Exp).then_inc(core.from_act.sem, core.from_act.up())
            act.wait_ge(core.from_dve.sem, core.from_dve.at(2))
            nc.scalar.activation(f[:, 4, :], f[:, 3, :], ACT.Exp).then_inc(core.from_act.sem, core.from_act.up())

        @block.vector
        def _(dve):
            step = Steps(dve, core.dve_step)
            step(nc.vector.tensor_tensor(prod[:, 0:1], core.v("diff_lq1"), core.v("diff_lk1"), ALU.mult))
            nc.vector.tensor_tensor(prod[:, 1:2], core.v("diff_lq2"), core.v("diff_lk2"), ALU.mult).then_inc(core.from_dve.sem, core.from_dve.up())
            dve.wait_ge(core.from_act.sem, core.from_act.at(1))
            step(nc.vector.tensor_tensor(lam[:, 2:3], lam[:, 1:2], lam[:, 0:1], ALU.subtract))
            step(nc.vector.tensor_scalar(lam[:, 2:3], lam[:, 2:3], -LAM_INIT, None, ALU.add))
            step(nc.vector.tensor_scalar(f[:, 0, :], out["f_logit"], -1.0, None, ALU.mult))
            nc.vector.tensor_tensor(f[:, 3, :], f[:, 0, :], out["f_logit"], ALU.min).then_inc(core.from_dve.sem, core.from_dve.up())
            softplus_steps(core, step, lambda: dve.wait_ge(core.from_act.sem, core.from_act.at(2)), dve, f[:, 0, :],
                           (f[:, 1, :], f[:, 2, :], f[:, 3, :]), f[:, 5, :], f[:, 4, :])
            step(nc.vector.memset(f[:, 0, :], 1.0))
            step(nc.vector.tensor_tensor_scan(f[:, 1, :], f[:, 0, :], f[:, 5, :], 0.0, ALU.mult, ALU.add))
            step(nc.vector.tensor_scalar(f[:, 2, :], f[:, 1, :], -8.0, None, ALU.mult))
            step(nc.vector.tensor_scalar(f[:, 3, :], f[:, 1, :], 8.0, None, ALU.mult))
            dve.wait_ge(core.product.sem, core.product.at(2))
            for half in range(2):
                src = core.banks[:, 1 + half, :].rearrange("p (k h) -> p h k", h=DIFF_HEADS)
                last = nc.vector.tensor_copy(bias[:, :, P * half:P * half + P], src)
                step(last)
            step(nc.vector.tensor_tensor(bias[:, :, P:SEQ], bias[:, :, P:SEQ],
                                         rows(core.const["causal"], DIFF_HEADS), ALU.add))
    core.settle()


def attention_stage(core, work, out, o_diff, y_fox):
    nc = core.nc
    units = [("diff", h, t) for h in range(DIFF_HEADS) for t in range(TT)]
    units += [("fox", h, t) for h in range(FOX_HEADS) for t in range(TT)]
    s, w, stat, wT, f, lam = (work[k] for k in ("scores", "weights", "stat", "weightsT", "f", "lam"))
    rh = work["row_head"]
    causal, bias = core.const["causal"], work["bias"]

    with nc.Block() as block:

        @block.tensor
        def _(pe):
            for u, (kind, h, t) in enumerate(units):
                b = 4 * (u % 2)
                keys = P * (t + 1)
                q = slice(P * t, P * t + P)
                if u >= 2:
                    pe.wait_ge(core.from_dve.sem, core.from_dve.at(3 * (u - 1)))
                if kind == "diff":
                    for c in range(2):
                        r = slice(HEAD * c, HEAD * c + HEAD)
                        last = nc.tensor.matmul(core.banks[:, b + c, 0:keys], out["dq"][r, h, q], out["dk"][r, h, 0:keys],
                                                start=True, stop=True)
                else:
                    r = slice(HEAD * (h % 2), HEAD * (h % 2) + HEAD)
                    nc.tensor.matmul(core.banks[:, b, 0:keys], out["fq"][r, h // 2, q], out["fk"][r, h // 2, 0:keys],
                                     start=True, stop=False)
                    nc.tensor.matmul(core.banks[:, b, 0:keys], f[:, 2, q], rh[:, 2 * P * h:2 * P * h + keys], start=False, stop=False)
                    last = nc.tensor.matmul(core.banks[:, b, 0:keys], rh[:, 2 * P * h:2 * P * h + P], f[:, 3, 0:keys],
                                            start=False, stop=True)
                last.then_inc(core.product.sem, core.product.up())
                pe.wait_ge(core.from_dve.sem, core.from_dve.at(3 * u + 1))
                for j in range(t + 1):
                    last = nc.tensor.transpose(core.banks[:, b + 2, P * j:P * j + P], w[:, P * j:P * j + P], core.const["ident"])
                last.then_inc(core.product.sem, core.product.up())
                pe.wait_ge(core.from_dve.sem, core.from_dve.at(3 * u + 2))
                if kind == "diff":
                    dst = core.banks[:, b + 3, 0:P]
                    v = [out["dv"][:, j, P * h:P * h + P] for j in range(t + 1)]
                else:
                    dst = core.banks[HEAD * (h % 2):HEAD * (h % 2) + HEAD, b + 3, 0:P]
                    v = [out["fv"][:, j, HEAD * h:HEAD * h + HEAD] for j in range(t + 1)]
                for j in range(t + 1):
                    last = nc.tensor.matmul(dst, v[j], wT[:, P * j:P * j + P], start=j == 0, stop=j == t)
                last.then_inc(core.product.sem, core.product.up())

        @block.scalar
        def _(act):
            n = 0
            for u, (kind, h, t) in enumerate(units):
                keys = P * (t + 1)
                for c in range(2 if kind == "diff" else 1):
                    n += 1
                    act.wait_ge(core.vector_max.sem, core.vector_max.at(n))
                    nc.scalar.activation(s[:, c, 0:keys], s[:, c, 0:keys], ACT.Exp, bias=stat[:, c:c + 1],
                                                           accum_out=stat[:, 2 + c:3 + c]).then_inc(core.from_act.sem, core.from_act.up())

        @block.vector
        def _(dve):
            step = Steps(dve, core.dve_step)
            n = 0
            for u, (kind, h, t) in enumerate(units):
                b = 4 * (u % 2)
                keys = P * (t + 1)
                maps = 2 if kind == "diff" else 1
                dve.wait_ge(core.product.sem, core.product.at(3 * u + 1))
                for c in range(maps):
                    src = core.banks[:, b + c, 0:keys]
                    if kind == "diff":
                        extra = bias[:, h, SEQ - keys:SEQ]
                        step(nc.vector.scalar_tensor_tensor(s[:, c, 0:keys], src, HEAD ** -0.5, extra, ALU.mult, ALU.add))
                    else:
                        step(nc.vector.tensor_scalar(s[:, c, 0:keys], src, HEAD ** -0.5, None, ALU.mult))
                        step(nc.vector.tensor_tensor(s[:, c, keys - P:keys], s[:, c, keys - P:keys], causal, ALU.add))
                    n += 1
                    nc.vector.tensor_reduce(stat[:, c:c + 1], s[:, c, 0:keys], AX.X, ALU.max, negate=True).then_inc(core.vector_max.sem, core.vector_max.up())
                dve.wait_ge(core.from_act.sem, core.from_act.at(n))
                step(nc.vector.reciprocal(stat[:, 4:4 + maps], stat[:, 2:2 + maps]))
                if kind == "diff":
                    step(nc.vector.tensor_scalar(stat[:, 5:6], stat[:, 5:6], lam[:, 2:3], None, ALU.mult))
                    step(nc.vector.tensor_scalar(s[:, 1, 0:keys], s[:, 1, 0:keys], stat[:, 5:6], None, ALU.mult))
                    last = nc.vector.scalar_tensor_tensor(w[:, 0:keys], s[:, 0, 0:keys], stat[:, 4:5], s[:, 1, 0:keys],
                                                          ALU.mult, ALU.add)
                else:
                    last = nc.vector.tensor_scalar(w[:, 0:keys], s[:, 0, 0:keys], stat[:, 4:5], None, ALU.mult)
                last.then_inc(core.from_dve.sem, core.from_dve.up())
                dve.wait_ge(core.product.sem, core.product.at(3 * u + 2))
                nc.vector.tensor_copy(wT[:, 0:keys], core.banks[:, b + 2, 0:keys]).then_inc(core.from_dve.sem, core.from_dve.up())
                dve.wait_ge(core.product.sem, core.product.at(3 * u + 3))
                q = slice(P * t, P * t + P)
                if kind == "diff":
                    last = nc.vector.tensor_copy(o_diff[:, h, q], core.banks[:, b + 3, 0:P])
                else:
                    r = slice(HEAD * (h % 2), HEAD * (h % 2) + HEAD)
                    last = nc.vector.tensor_copy(y_fox[r, h // 2, q], core.banks[r, b + 3, 0:P])
                last.then_inc(core.from_dve.sem, core.from_dve.up())
    core.settle()


def head_norm_stage(core, o, squares, rstd):
    nc = core.nc
    with nc.Block() as block:

        @block.tensor
        def _(pe):
            pe.wait_ge(core.from_dve.sem, core.from_dve.at(1))
            for h in range(DIFF_HEADS):
                last = nc.tensor.matmul(core.banks[:, h, 0:SEQ], core.const["ones"], squares[:, h, :], start=True, stop=True)
            last.then_inc(core.product.sem, core.product.up())

        @block.scalar
        def _(act):
            act.wait_ge(core.from_dve.sem, core.from_dve.at(2))
            nc.scalar.activation(rstd, rstd, ACT.Sqrt).then_inc(core.from_act.sem, core.from_act.up())

        @block.vector
        def _(dve):
            step = Steps(dve, core.dve_step)
            nc.vector.tensor_tensor(squares, o, o, ALU.mult).then_inc(core.from_dve.sem, core.from_dve.up())
            dve.wait_ge(core.product.sem, core.product.at(1))
            nc.vector.tensor_scalar(rstd, core.banks[:, 0:DIFF_HEADS, 0:SEQ], 1.0 / P, EPS, ALU.mult, ALU.add).then_inc(core.from_dve.sem, core.from_dve.up())
            dve.wait_ge(core.from_act.sem, core.from_act.at(1))
            step(nc.vector.reciprocal(rstd, rstd))
            step(nc.vector.tensor_scalar(o, o, core.v("diff_subln_g"), 1.0 - LAM_INIT, ALU.mult, ALU.mult))
            step(nc.vector.tensor_tensor(o, o, rstd, ALU.mult))
    core.settle()


def branch_stage(core, ys, gates, m, tmp):
    nc = core.nc
    groups = []
    for half in range(2):
        for br, (y, kt) in enumerate(ys):
            def evacuate(j, br=br, half=half):
                mt = 4 * half + j

                def run(step, ps):
                    g = gates[:, 8 * br + mt, :]
                    if br == 0:
                        return nc.vector.tensor_tensor(m[:, mt, :], ps, g, ALU.mult)
                    step(nc.vector.tensor_tensor(tmp, ps, g, ALU.mult))
                    return nc.vector.tensor_tensor(m[:, mt, :], m[:, mt, :], tmp, ALU.add)
                return run
            groups += weight_groups(core, 1, kt, lambda k, y=y: y[:, k, :], m.shape[2], lambda j: "dve", evacuate)
    product_stage(core, groups, "mixer0")


def residual_stage(core, moving, length, kt, n_chunks, x, scale, section, segments=None):
    nc = core.nc
    segments = segments or [(0, length)]

    def evacuate(m):
        def run(step, ps):
            last = None
            for i, (a, b) in enumerate(segments):
                if last is not None:
                    step(last)
                last = nc.vector.scalar_tensor_tensor(x[:, m, a:b], ps[:, a:b], scale(m, i), x[:, m, a:b], ALU.mult, ALU.add)
            return last
        return run
    product_stage(core, weight_groups(core, n_chunks, kt, moving, length, lambda m: "dve", evacuate), section)


def ffn_up_stage(core, h, a, gate, val):
    nc = core.nc

    def evacuate(m):
        c, j = divmod(m, 4)
        is_val, f = j // 2, 2 * c + j % 2
        tile = f + KF * is_val
        dst = (val if is_val else gate)[:, j % 2, :]

        def run(step, ps):
            step(nc.vector.tensor_scalar(dst, ps, core.v("ffn_conv_w", 2 * 2 * KF + tile), core.v("ffn_conv_b", tile),
                                         ALU.mult, ALU.add))
            for d in range(1, CONV_FFN):
                last = nc.vector.scalar_tensor_tensor(dst[:, d:], ps[:, 0:SEQ - d], core.v("ffn_conv_w", (2 - d) * 2 * KF + tile),
                                                      dst[:, d:], ALU.mult, ALU.add)
                if d < CONV_FFN - 1 or is_val:
                    step(last)
            if is_val:
                nc.vector.wait_ge(core.from_act.sem, core.from_act.at(f + 1))
                last = nc.vector.tensor_tensor(a[:, f, :], a[:, f, :], dst, ALU.mult)
            return last
        return run

    groups = weight_groups(core, KF // 2, KD, lambda k: h[:, k, :], SEQ, lambda m: "dve", evacuate)
    product_stage(core, groups, "mixer0", side=lambda act: gelu_work(core, act, gate, a))


def gelu_work(core, act, gate, a):
    for f in range(KF):
        c, j = divmod(f, 2)
        act.wait_ge(core.dve_read.sem, core.dve_read.at(4 * c + j + 1))
        core.nc.scalar.activation(a[:, f, :], gate[:, j, :], ACT.Gelu_apprx_tanh).then_inc(core.from_act.sem, core.from_act.up())


def first_block(core, x, rel_dram, stack0):
    with ExitStack() as s:
        h = core.sb(s, "h", [P, KD, SEQ])
        squares = core.sb(s, "squares", [P, KD, SEQ])
        rstd = core.sb(s, "rstd", [P, SEQ])
        y_rnn = core.sb(s, "y_rnn", [P, KD, SEQ])
        o_diff = core.sb(s, "o_diff", [P, 4, SEQ])
        y_fox = core.sb(s, "y_fox", [P, 4, SEQ])
        gates = core.sb(s, "gates", [P, 24, SEQ])
        seg = [(0, SEQ)]
        norm_stage(core, x, h[:, :, :], squares[:, :, :], rstd[:, :], seg, lambda k, i: core.v("norm1_g", k), None, "mixer0")
        with ExitStack() as t:
            out = {name: core.sb(t, name, [P, n, SEQ]) for name, n in
                   (("x_rnn", 8), ("g_rnn", 8), ("dq", 4), ("dk", 4), ("fq", 4), ("fk", 4))}
            out["dv"] = core.sb(t, "dv", [P, TT, 512])
            out["fv"] = core.sb(t, "fv", [P, TT, 512])
            flog = core.sb(t, "f_logit", [FOX_HEADS, SEQ])
            out["f_logit"] = flog[:, :]
            out["gates"] = gates
            projection_stage(core, h, out)
            with ExitStack() as u:
                rnn_stage(core, u, out, y_rnn)
            with ExitStack() as u:
                work = {"lam": core.sb(u, "lam", [P, 4]), "lam_products": core.sb(u, "lam_products", [P, 2]),
                        "f": core.sb(u, "forget", [FOX_HEADS, 6, SEQ]), "bias": core.sb(u, "bias", [P, DIFF_HEADS, SEQ]),
                        "scores": core.sb(u, "scores", [P, 2, SEQ]), "weights": core.sb(u, "attention", [P, SEQ]),
                        "weightsT": core.sb(u, "attentionT", [P, SEQ]), "stat": core.sb(u, "softmax_stat", [P, 6]),
                        "row_head": core.sb(u, "row_head", [FOX_HEADS, FOX_HEADS * SEQ])}
                buckets = core.sb(u, "buckets", [N_BUCKETS, 2 * SEQ - 1])
                rel = core.sb(u, "rel_bias", [N_BUCKETS, DIFF_HEADS])
                causal = core.sb(u, "causal", [P, P])
                core.const["causal"] = causal[:, :]
                small_load_stage(core, [(causal[:, :], core.dram["c_causal"]),
                                        (work["row_head"][:, :], core.dram["c_row_head"][0:FOX_HEADS, :]),
                                        (buckets[:, :], core.dram["c_buckets"][0:N_BUCKETS, :]),
                                        (rel[:, :], rel_dram)])
                attention_setup_stage(core, work, out, rel, buckets)
                attention_stage(core, work, out, o_diff, y_fox)
                head_norm_stage(core, o_diff[:, :, :], squares[:, 0:4, :], squares[:, 4:8, :])
        m = core.sb(s, "mixed", [P, KD, SEQ])
        branch_stage(core, [(y_rnn, 8), (o_diff, 4), (y_fox, 4)], gates, m, rstd[:, :])
        residual_stage(core, lambda k: m[:, k, :], SEQ, KD, 2, x, lambda m_, i: 1.0, "mixer0")
        norm_stage(core, x, h[:, :, :], squares[:, :, :], rstd[:, :], seg, lambda k, i: core.v("norm2_g", k), None, "mixer0")
        a = core.sb(s, "ffn", [P, KF, SEQ])
        gate, val = core.sb(s, "ffn_gate", [P, 2, SEQ]), core.sb(s, "ffn_value", [P, 2, SEQ])
        ffn_up_stage(core, h, a, gate, val)
        residual_stage(core, lambda k: a[:, k, :], SEQ, KF, KD, x, lambda m_, i: 1.0, "mixer0")
        norm_stage(core, x, x, squares[:, :, :], rstd[:, :], seg, lambda k, i: core.v("final_g", k), None, "mixer0")


def small_load_stage(core, loads, wait=True):
    nc = core.nc
    with nc.Block() as block:

        @block.sync
        def _(sp):
            for dst, src in loads:
                sp.dma_start(dst, src).then_inc(core.landed.sem, core.landed.up(16))
            if wait:
                sp.wait_ge(core.landed.sem, core.landed.at(16 * len(loads)))
    core.settle()


def store_stage(core, dst, src):
    nc = core.nc
    with nc.Block() as block:

        @block.sync
        def _(sp):
            sp.dma_start(dst, src).then_inc(core.stored.sem, core.stored.up(16))
            sp.wait_ge(core.stored.sem, core.stored.at(16))
    core.settle()



def modulation_stage(core, layer, cc, mod, g1, g2):
    nc = core.nc
    section = f"mixer{layer}"
    with nc.Block() as block:

        @block.scalar
        def _(act):
            for i, name in enumerate(("c_ctx_2", "c_2")):
                nc.scalar.activation(cc[:, :, i], core.v(name, 0, 8), ACT.Silu).then_inc(core.act_step.sem, core.act_step.up())
    core.settle()

    def evacuate(m):
        return lambda step, ps: nc.vector.tensor_scalar(mod[:, m, :], ps, core.v(("ada_b_2", layer), m), None, ALU.add)
    product_stage(core, weight_groups(core, 12, KD, lambda k: cc[:, k, :], 2, lambda m: "dve", evacuate), section)
    with nc.Block() as block:

        @block.vector
        def _(dve):
            step = Steps(dve, core.dve_step)
            for g, name, at in ((g1, "norm1_g_2", 8), (g2, "norm2_g_2", 32)):
                step(nc.vector.scalar_tensor_tensor(g[:, :, :], mod[:, at:at + 8, :], 1.0, columns(core.v((name, layer), 0, 8), 2),
                                                    ALU.add, ALU.mult))
    core.settle()



def rwkv_projection_stage(core, layer, h, z, zs, mu):
    nc = core.nc
    with nc.Block() as block:

        @block.vector
        def _(dve):
            step = Steps(dve, core.dve_step)
            key = ("shift_mu_2", layer)
            step(nc.vector.scalar_tensor_tensor(mu, core.v(key, 0, ZT), -1.0, core.v(key, ZT, ZT), ALU.mult, ALU.subtract))
            step(nc.vector.tensor_scalar(mu, mu, 1.0, None, ALU.add))
    core.settle()

    def evacuate(m):
        n = min(P, P_RWKV - P * m)
        dst = (z[0:n, m, :] if m < 24 else zs[0:n, m - 24, :]).rearrange("p (s t) -> p s t", s=2)

        def run(step, ps):
            src = ps.rearrange("p (s t) -> p s t", s=2)
            before, after = (core.v(("shift_mu_2", layer), m + ZT * j)[0:n] for j in range(2))
            step(nc.vector.tensor_scalar(dst, src, mu[0:n, m:m + 1], None, ALU.mult))
            step(nc.vector.scalar_tensor_tensor(dst[:, :, 1:], src[:, :, 0:SEQ - 1], before, dst[:, :, 1:], ALU.mult, ALU.add))
            return nc.vector.scalar_tensor_tensor(dst[:, :, 0:SEQ - 1], src[:, :, 1:], after, dst[:, :, 0:SEQ - 1],
                                                  ALU.mult, ALU.add)
        return run
    product_stage(core, weight_groups(core, 7, KD, lambda k: h[:, k, :], 2 * SEQ, lambda m: "dve", evacuate), f"mixer{layer}")


def bank_tiles(core):
    return core.banks[:, 0:4, :].rearrange("p b (j t) -> p (b j) t", j=2)


def head_sums(core, pe, src):
    out = bank_tiles(core)
    for m in range(KD):
        last = core.nc.tensor.matmul(out[:, m, :], core.const["head_ones"], src[:, m, :], start=True, stop=True)
    return last


def key_direction_stage(core, layer, k, kk, tmp):
    nc = core.nc
    with nc.Block() as block:

        @block.tensor
        def _(pe):
            pe.wait_ge(core.from_dve.sem, core.from_dve.at(1))
            head_sums(core, pe, tmp).then_inc(core.product.sem, core.product.up())

        @block.scalar
        def _(act):
            act.wait_ge(core.from_dve.sem, core.from_dve.at(2))
            nc.scalar.activation(tmp, tmp, ACT.Sqrt).then_inc(core.from_act.sem, core.from_act.up())

        @block.vector
        def _(dve):
            step = Steps(dve, core.dve_step)
            for m in range(KD):
                step(nc.vector.tensor_scalar(kk[:, m, :], k[:, m, :], core.v(("k_k_2", layer), m), None, ALU.mult))
            nc.vector.tensor_tensor(tmp, kk, kk, ALU.mult).then_inc(core.from_dve.sem, core.from_dve.up())
            dve.wait_ge(core.product.sem, core.product.at(1))
            nc.vector.tensor_scalar(tmp, bank_tiles(core), 1e-24, None, ALU.max).then_inc(core.from_dve.sem, core.from_dve.up())
            dve.wait_ge(core.from_act.sem, core.from_act.at(1))
            step(nc.vector.reciprocal(tmp, tmp))
            step(nc.vector.tensor_tensor(kk, kk, tmp, ALU.mult))
    core.settle()


def decay_stage(core, layer, d, t0, lora, tw, zs, a, ld):
    nc = core.nc
    r = slice(HEAD * d, HEAD * d + HEAD)
    groups = []
    for which, (moving, dst, bias) in enumerate(((tw[r, t0:t0 + SEQ], ld, "w0_2"), (zs[r, 1, t0:t0 + SEQ], a, "a0_2"))):
        for m in range(KD):
            out = dst[:, m, ::-1] if d else dst[:, m, :]
            groups.append(Group("act", [(lora[r, which, P * m:P * m + P], moving)],
                                act_to(core, out, ACT.Sigmoid, core.v((bias, layer), KD * d + m)), P, SEQ))
    product_stage(core, groups, f"mixer{layer}")


DECAY = math.exp(-0.5)


def factor_stage(core, layer, d, stream, a, ld, cum, e, alpha_rho, beta, kappa, bonus, last_decay, one_minus_ka):
    nc = core.nc
    r, k, kk = stream["r"], stream["k"], stream["kk"]
    alpha, rho = (alpha_rho[:, :, :, i, :] for i in range(2))
    flat = [x.rearrange("p m t -> p (m t)") for x in (cum[:, :, :], ld[:, :, :])]
    scratch = alpha_rho.rearrange("p m c i t -> p (m c i t)")[:, 0:KD * SEQ]

    def order(x):
        return x[:, :, ::-1] if d else x[:, :, :]

    def chunked(x):
        return x.rearrange("p m (c t) -> p m c t", t=CHUNK)

    with nc.Block() as block:

        @block.scalar
        def _(act):
            act.wait_ge(core.from_dve.sem, core.from_dve.at(1))
            nc.scalar.activation(ld[:, :, :], ld[:, :, :], ACT.Exp, scale=-DECAY).then_inc(core.from_act.sem, core.from_act.up())
            nc.scalar.activation(e[:, :, :], cum[:, :, :], ACT.Exp, scale=-DECAY).then_inc(core.from_act.sem, core.from_act.up())
            nc.scalar.activation(cum[:, :, :], cum[:, :, :], ACT.Exp, scale=DECAY).then_inc(core.from_act.sem, core.from_act.up())

        @block.vector
        def _(dve):
            step = Steps(dve, core.dve_step)
            step(nc.vector.memset(scratch, 1.0))
            step(nc.vector.memset(scratch[:, 0::CHUNK], 0.0))
            step(nc.vector.tensor_tensor_scan(flat[0], scratch, flat[1], 0.0, ALU.mult, ALU.add))
            dve.wait_ge(core.landed.sem, core.landed.at(0))
            for m in range(KD):
                step(nc.vector.tensor_scalar(kappa[:, m, :], a[:, m, :], core.v(("k_a_2", layer), m), one_minus_ka[:, m:m + 1],
                                             ALU.mult, ALU.add))
            step(nc.vector.tensor_tensor(kappa[:, :, :], kappa[:, :, :], order(k), ALU.mult))
            if d == 0:
                step(nc.vector.tensor_tensor(bonus[:, :, :], kappa[:, :, :], r[:, :, :], ALU.mult))
            else:
                product = scratch.rearrange("p (m t) -> p m t", m=KD)
                step(nc.vector.tensor_tensor(product, kappa[:, :, :], order(r), ALU.mult))
                step(nc.vector.tensor_tensor(order(bonus), order(bonus), product, ALU.add))
            step(nc.vector.tensor_tensor(beta[:, :, :], a[:, :, :], order(kk), ALU.mult))
            nc.vector.tensor_tensor(ld[:, :, :], cum[:, :, :], ld[:, :, :], ALU.subtract).then_inc(core.from_dve.sem, core.from_dve.up())
            dve.wait_ge(core.from_act.sem, core.from_act.at(1))
            step(nc.vector.tensor_tensor(alpha, chunked(ld[:, :, :]), chunked(order(kk)), ALU.mult))
            dve.wait_ge(core.from_act.sem, core.from_act.at(2))
            step(nc.vector.tensor_tensor(rho, chunked(e[:, :, :]), chunked(order(r)), ALU.mult))
            step(nc.vector.tensor_copy(last_decay[:, :, :], e[:, :, CHUNK - 1::CHUNK]))
            dve.wait_ge(core.from_act.sem, core.from_act.at(3))
            step(nc.vector.tensor_tensor(kappa[:, :, :], kappa[:, :, :], cum[:, :, :], ALU.mult))
            step(nc.vector.tensor_tensor(beta[:, :, :], beta[:, :, :], cum[:, :, :], ALU.mult))
    core.settle()


def delta_order():
    levels = range(1, LEVELS)
    prepare = ["krow", "vrow", "LakT", "brow", "N", "Y0"]
    for i in levels:
        prepare += [f"Y{i}"] + ([f"T{i}"] if i < LEVELS - 1 else []) + [f"Z{i}"]
    order = []
    for pair in range(NCH // 2):
        order += [(2 * pair + j, name) for name in prepare for j in range(2)]
        order += [(2 * pair + j, name) for j in range(2) for name in ("B", "U", "S", "Y")]
    by_scalar = ("krow", "brow", "vrow", "B", "U")
    place, rank, n = {}, {}, [0, 0]
    for i, entry in enumerate(order):
        e = 0 if entry[1] in by_scalar else 1
        n[e] += 1
        place[entry], rank[entry] = i, (e, n[e])
    return order, place, rank


def delta_needs(name, c):
    last = LEVELS - 1
    table = {"Y0": ["N"], "Y1": ["Y0", "N"], "T1": ["N", "Y1"], "Z1": ["N", "Y1"], "B": ["LakT", "vrow"],
             "U": ["B", f"Z{last}"], "S": ["krow", "brow", "U"], "Y": ["LakT", "N", "U"]}
    if name in table:
        needs = [(c, x) for x in table[name]]
        return needs + ([(c - 1, "S")] if c and name == "B" else [])
    if name[0] in "YTZ" and name[1:].isdigit():
        i = int(name[1:])
        return [(c, f"T{i - 1}"), (c, f"Z{i - 1}")] if name[0] == "Y" else [(c, f"Y{i}"), (c, f"Z{i - 1}")]
    return []


PLACES = (("kappa", "T"), ("v", "Y"), ("beta", "Z"), ("N", "alpha", "B"), ("LakT", "U"), ("krow",), ("brow",), ("vrow",))


def delta_stage(core, d, v, alpha_rho, beta, kappa, last_decay, state, next_state, y, sets):
    nc = core.nc
    order, place, rank = delta_order()
    read = (core.act_read, core.dve_read)
    ident, above, upto, masks = (core.const[k] for k in ("ident", "above_bd", "upto", "levels"))
    states = (state, next_state)
    slots = NBANK // 2

    def bank(entry):
        b = 2 * (place[entry] % slots)
        return core.banks[:, b:b + 2, :].rearrange("p b (m t) -> p (b m) t", t=P)

    def mask(i):
        return rows(masks[:, P * i:P * i + P], KD)

    with nc.Block() as block:

        @block.tensor
        def _(pe):
            for i, (c, name) in enumerate(order):
                w = sets[c % 2]
                if i >= slots:
                    e, k = rank[order[i - slots]]
                    pe.wait_ge(read[e].sem, read[e].at(k))
                for needed in delta_needs(name, c):
                    e, k = rank[needed]
                    pe.wait_ge(read[e].sem, read[e].at(k))
                if name in ("krow", "vrow", "brow", "B"):
                    made = 4 * (c // 2) * 2 + {"krow": 2, "vrow": 4, "brow": 5 + c % 2, "B": 7 + c % 2}[name]
                    pe.wait_ge(core.from_act.sem, core.from_act.at(made))
                out = bank((c, name))
                if name == "Y":
                    out, al_rh = out[:, :, 0:CHUNK], alpha_rho[:, :, c, 1, :]
                    pairs = [(states[c % 2], al_rh), (w["vrow"], w["MrkT"]), (w["U"], w["MrbT"])]
                elif name[0] == "Y" and name != "Y0":
                    pairs = [(w["N"], w["T"])]
                else:
                    both = alpha_rho[:, :, c, :, :].rearrange("p m i t -> p m (i t)")
                    eye = rows(ident, KD)
                    pairs = {"krow": [(w["kappa"], eye)], "vrow": [(w["v"], eye)], "LakT": [(w["kappa"], both)], "brow": [(w["beta"], eye)],
                             "N": [(w["beta"], both)], "Y0": [(w["N"], eye)], "T": [(w["Z"], w["Y"])], "Z": [(w["Y"], w["Z"])],
                             "B": [(w["alpha"], states[c % 2]), (w["LakT"], w["vrow"])], "U": [(w["Z"], w["B"])],
                             "S": [(w["krow"], w["vrow"]), (w["brow"], w["U"])]}[name if name == "Y0" else name.rstrip("12345")]
                for m in range(KD):
                    for n, (lhsT, rhs) in enumerate(pairs):
                        last = nc.tensor.matmul(out[:, m, :], lhsT[:, m, :], rhs[:, m, :], start=n == 0, stop=n == len(pairs) - 1)
                last.then_inc(core.product.sem, core.product.up())

        @block.scalar
        def _(act):
            def diagonal(c, name, src):
                for hh in range(2):
                    r = slice(HEAD * hh, HEAD * hh + HEAD)
                    last = nc.scalar.activation(sets[c % 2][name][r, :, CHUNK * hh:CHUNK * hh + CHUNK],
                                                src[r, :, CHUNK * c:CHUNK * c + CHUNK], ACT.Identity)
                last.then_inc(core.from_act.sem, core.from_act.up())

            def inputs(pair):
                for c in (2 * pair, 2 * pair + 1):
                    diagonal(c, "kappa", kappa)
                for c in (2 * pair, 2 * pair + 1):
                    diagonal(c, "v", v[:, :, ::-1] if d else v)

            inputs(0)
            for c in range(2):
                diagonal(c, "beta", beta)
            for c, name in order:
                if rank[(c, name)][0]:
                    continue
                if name == "B":
                    if c % 2 == 0:
                        for j in (c, c + 1):
                            act.wait_ge(core.product.sem, core.product.at(place[(j, f"Y{LEVELS - 1}")] + 1))
                            w = sets[j % 2]
                            for hh in range(2):
                                r = slice(HEAD * hh, HEAD * hh + HEAD)
                                last = nc.scalar.activation(w["alpha"][r, :, CHUNK * hh:CHUNK * hh + CHUNK], alpha_rho[r, :, j, 0, :],
                                                            ACT.Identity)
                            last.then_inc(core.from_act.sem, core.from_act.up())
                act.wait_ge(core.product.sem, core.product.at(place[(c, name)] + 1))
                scale = -1.0 if name == "brow" else 1.0
                nc.scalar.activation(sets[c % 2][name], bank((c, name)), ACT.Identity, scale=scale
                                     ).then_inc(core.act_read.sem, core.act_read.up())
                if name == "U" and c % 2 == 0 and c + 2 < NCH:
                    act.wait_ge(core.product.sem, core.product.at(place[(c + 1, f"Z{LEVELS - 1}")] + 1))
                    inputs(c // 2 + 1)
                if name == "U" and c % 2 and c + 1 < NCH:
                    for j in (c + 1, c + 2):
                        diagonal(j, "beta", beta)

        @block.vector
        def _(dve):
            step = Steps(dve, core.dve_step)
            eye = rows(ident, KD)
            for c, name in order:
                if not rank[(c, name)][0]:
                    continue
                w, ps = sets[c % 2], bank((c, name))
                dve.wait_ge(core.product.sem, core.product.at(place[(c, name)] + 1))
                if name in ("LakT", "N"):
                    twice = ps[:, :, 0:CHUNK].unsqueeze(2).broadcast_to([P, KD, 2, CHUNK])

                    def diagonal(x):
                        return x.rearrange("p m (h t) -> p m h t", h=2)

                    def masked(m):
                        return diagonal(rows(m, KD))
                    step(nc.vector.tensor_tensor(diagonal(w[name]), twice, masked(above), ALU.mult))
                    if name == "N":
                        step(nc.vector.scalar_tensor_tensor(w["Z"], w["N"], -1.0, mask(LEVELS), ALU.mult, ALU.mult))
                        step(nc.vector.tensor_tensor(w["Z"], w["Z"], eye, ALU.add))
                    key, sign = ("MrbT", -1.0) if name == "N" else ("MrkT", 1.0)
                    last = nc.vector.scalar_tensor_tensor(w[key], ps[:, :, CHUNK:], sign, rows(upto, KD), ALU.mult, ALU.mult)
                elif name == "Y0":
                    step(nc.vector.scalar_tensor_tensor(w["T"], ps, -1.0, mask(0), ALU.mult, ALU.mult))
                    last = nc.vector.tensor_tensor(w["T"], w["T"], eye, ALU.add)
                elif name == "Y":
                    t, ps = slice(CHUNK * c, CHUNK * c + CHUNK), ps[:, :, 0:CHUNK]
                    if d == 0:
                        last = nc.vector.tensor_copy(y[:, :, t], ps)
                    else:
                        yt = y[:, :, ::-1][:, :, t]
                        last = nc.vector.tensor_tensor(yt, ps, yt, ALU.add)
                elif name[0] == "Y":
                    last = nc.vector.tensor_tensor(w["Y"], ps, mask(int(name[1:])), ALU.mult)
                elif name[0] in "TZ":
                    x = w[name[0]]
                    last = nc.vector.scalar_tensor_tensor(x, ps, -1.0, x, ALU.mult, ALU.add)
                elif name == "S":
                    old, new = states[c % 2], states[(c + 1) % 2]
                    step(nc.vector.tensor_tensor(new, ps, old, ALU.add))
                    last = nc.vector.tensor_tensor(new, new, last_decay[:, :, c:c + 1].broadcast_to([P, KD, P]), ALU.mult)
                last.then_inc(core.dve_read.sem, core.dve_read.up())
                dve.wait_ge(core.dve_read.sem, core.dve_read.now())
    core.settle()


def rwkv_output_stage(core, layer, t0, stream, y, bonus, tmp, g2w, sg):
    nc = core.nc
    v = stream["v"]
    sums = bank_tiles(core)
    gate = core.banks[:, 4:8, :].rearrange("p b (j t) -> p (b j) t", j=2)
    with nc.Block() as block:

        @block.tensor
        def _(pe):
            head_sums(core, pe, y).then_inc(core.product.sem, core.product.up())
            for m in range(KD):
                nc.tensor.matmul(gate[:, m, :], g2w[:, 0, P * m:P * m + P], sg[:, 0, t0:t0 + SEQ], start=True, stop=False)
                n = LORA_G - P
                last = nc.tensor.matmul(gate[:, m, :], g2w[0:n, 1, P * m:P * m + P], sg[0:n, 1, t0:t0 + SEQ], start=False, stop=True)
            last.then_inc(core.product.sem, core.product.up())
            pe.wait_ge(core.from_dve.sem, core.from_dve.at(1))
            head_sums(core, pe, tmp).then_inc(core.product.sem, core.product.up())
            pe.wait_ge(core.from_dve.sem, core.from_dve.at(3))
            head_sums(core, pe, bonus).then_inc(core.product.sem, core.product.up())

        @block.scalar
        def _(act):
            act.wait_ge(core.from_dve.sem, core.from_dve.at(2))
            nc.scalar.activation(tmp, tmp, ACT.Sqrt).then_inc(core.from_act.sem, core.from_act.up())

        @block.vector
        def _(dve):
            step = Steps(dve, core.dve_step)
            dve.wait_ge(core.product.sem, core.product.at(1))
            step(nc.vector.scalar_tensor_tensor(y, sums, -1.0 / HEAD, y, ALU.mult, ALU.add))
            nc.vector.tensor_tensor(tmp, y, y, ALU.mult).then_inc(core.from_dve.sem, core.from_dve.up())
            dve.wait_ge(core.product.sem, core.product.at(3))
            nc.vector.tensor_scalar(tmp, sums, 1.0 / HEAD, GN_EPS, ALU.mult, ALU.add).then_inc(core.from_dve.sem, core.from_dve.up())
            for m in range(KD):
                last = nc.vector.tensor_scalar(bonus[:, m, :], bonus[:, m, :], core.v(("r_k_2", layer), m), None, ALU.mult)
                last.then_inc(core.from_dve.sem, core.from_dve.up()) if m == KD - 1 else step(last)
            dve.wait_ge(core.from_act.sem, core.from_act.at(1))
            step(nc.vector.reciprocal(tmp, tmp))
            step(nc.vector.tensor_tensor(y, y, tmp, ALU.mult))
            for m in range(KD):
                step(nc.vector.tensor_scalar(y[:, m, :], y[:, m, :], core.v(("lnx_g_2", layer), m), core.v(("lnx_b_2", layer), m),
                                             ALU.mult, ALU.add))
            dve.wait_ge(core.product.sem, core.product.at(4))
            step(nc.vector.tensor_tensor(tmp, sums, v[:, :, :], ALU.mult))
            step(nc.vector.tensor_tensor(y, y, tmp, ALU.add))
            dve.wait_ge(core.product.sem, core.product.at(2))
            step(nc.vector.tensor_tensor(y, gate, y, ALU.mult))
    core.settle()


def rwkv_branch(core, layer, x, mod, g1, z_dram, y_dram, emits):
    nc = core.nc
    section = f"mixer{layer}"
    with ExitStack() as s:
        zs = core.sb(s, "z_small", [P, 4, 2 * SEQ])
        with ExitStack() as t:
            h = core.sb(t, "h", [P, KD, 2 * SEQ])
            rstd = core.sb(t, "rstd", [P, 2 * SEQ])
            z = core.sb(t, "z", [P, 24, 2 * SEQ])
            mu = core.sb(t, "mu", [P, ZT])
            norm_stage(core, x, h[:, :, :], z[:, 0:KD, :], rstd[:, :], [(0, SEQ), (SEQ, 2 * SEQ)],
                       lambda k, i: g1[:, k, i:i + 1], lambda k, i: mod[:, k, i:i + 1], section)
            rwkv_projection_stage(core, layer, h, z, zs, mu[:, :])
            store_stage(core, z_dram, z[:, :, :])
        lora_chunk, g2_chunk = core.next_chunk, core.next_chunk + 1
        core.next_chunk += 2
        lora, g2w = core.ring.chunk(lora_chunk), core.ring.chunk(g2_chunk)
        tw = core.sb(s, "tanh_w", [P, 2 * SEQ])
        st = {k: core.sb(s, f"stream_{k}", [P, KD, SEQ]) for k in ("r", "k", "v", "kk")}
        a, ld, cum, beta, kappa = (core.sb(s, n, [P, KD, SEQ]) for n in ("rate", "log_decay", "cumulated", "beta", "kappa"))
        alpha_rho = core.sb(s, "alpha_rho", [P, KD, NCH, 2, CHUNK])[:, :, :, :, :]
        y, bonus = core.sb(s, "y", [P, KD, SEQ]), core.sb(s, "bonus", [P, KD, SEQ])
        last_decay, omk = core.sb(s, "last_decay", [P, KD, NCH]), core.sb(s, "one_minus_ka", [P, KD])
        masks = {name: core.sb(s, name, [P, n])[:, :] for name, n in (("levels", (LEVELS + 1) * P), ("above_bd", P), ("upto", CHUNK))}
        core.const.update(masks)
        small_load_stage(core, [(ap, core.dram["c_" + name]) for name, ap in masks.items()], False)
        states = [core.sb(s, f"state_{d}", [P, KD, P])[:, :, :] for d in range(2)]
        next_state = core.sb(s, "next_state", [P, KD, P])[:, :, :]
        pool = core.sb(s, "chunk_pool", [P, 4, KD * P])
        kept = [pool[:, i, :] for i in range(4)] + [slot[:, KD * P * i:KD * P * (i + 1)] for slot in core.ring.slots for i in (2, 3)]
        lent = [x[:, :, :].rearrange("p m t -> p (m t)")[:, KD * P * i:KD * P * (i + 1)]
                for x in (a, ld, cum, st["r"], st["k"]) for i in range(2)]
        sets = [{}, {}]
        for i, w in enumerate(sets):
            for j, names in enumerate(PLACES):
                at = kept[4 * i + j] if j < 4 else lent[5 * i + j - 4]
                w.update({name: at.rearrange("p (m t) -> p m t", m=KD) for name in names})
            w["MrkT"], w["MrbT"] = (lent[5 * i + 4][:, KD * CHUNK * n:KD * CHUNK * (n + 1)].rearrange("p (m t) -> p m t", m=KD)
                                    for n in range(2))
        with nc.Block() as block:

            @block.sync
            def _(sp):
                core.ring.load(sp, section)

            @block.scalar
            def _(act):
                nc.scalar.activation(tw[:, :], zs[:, 0, :], ACT.Tanh).then_inc(core.act_step.sem, core.act_step.up())
                nc.scalar.activation(zs[:, 2, :], zs[:, 2, :], ACT.Sigmoid).then_inc(core.act_step.sem, core.act_step.up())
                n = LORA_G - P
                nc.scalar.activation(zs[0:n, 3, :], zs[0:n, 3, :], ACT.Sigmoid).then_inc(core.act_step.sem, core.act_step.up())

            @block.vector
            def _(dve):
                step = Steps(dve, core.dve_step)
                for w in sets:
                    for names in PLACES[0:4]:
                        step(nc.vector.memset(w[names[0]], 0.0))
                for state in states:
                    step(nc.vector.memset(state, 0.0))
                step(nc.vector.tensor_scalar(omk[:, :], core.v(("k_a_2", layer), 0, 8), -1.0, 1.0, ALU.mult, ALU.add))

            @block.tensor
            def _(pe):
                pe.wait_ge(core.ring.loaded[lora_chunk % RING], core.ring.at(lora_chunk))
                pe.wait_ge(core.ring.loaded[g2_chunk % RING], core.ring.at(g2_chunk))
        core.settle()
        for seq in range(2):
            t0 = SEQ * seq
            small_load_stage(core, [(st[n][:, :, :], z_dram[:, KD * i:KD * i + KD, t0:t0 + SEQ]) for i, n in enumerate("rkv")])
            key_direction_stage(core, layer, st["k"], st["kk"][:, :, :], cum[:, :, :])
            for d in range(2):
                if d:
                    small_load_stage(core, [(st[n][:, :, :], z_dram[:, KD * i:KD * i + KD, t0:t0 + SEQ]) for i, n in enumerate("rk")], False)
                decay_stage(core, layer, d, t0, lora, tw, zs, a, ld)
                factor_stage(core, layer, d, st, a, ld, cum, a, alpha_rho, beta, kappa, bonus, last_decay, omk)
                delta_stage(core, d, st["v"], alpha_rho, beta, kappa, last_decay, states[d], next_state, y, sets)
            if seq in emits:
                rwkv_output_stage(core, layer, t0, st, y[:, :, :], bonus[:, :, :], cum[:, :, :], g2w, zs[:, 2:4, :])
                store_stage(core, y_dram[:, :, t0:t0 + SEQ], y[:, :, :])
        core.ring.release(lora_chunk, (core.product, core.product.base))
        core.ring.release(g2_chunk, (core.product, core.product.base))



def glu_stage(core, layer, h, u, sg, gates, length):
    def moving(k):
        return h[:, k, :]

    def reader(m):
        return "act" if m % 4 >= 2 else "dve"

    def evacuate(m):
        c, j = divmod(m, 4)
        if j < 2:
            return copy_to(core, u[:, 2 * c + j, :])
        return act_to(core, sg[:, 2 * c + j - 2, :], ACT.Sigmoid)
    g = weight_groups(core, 4, KD, moving, length, reader, evacuate)
    g += weight_groups(core, 4, KD, moving, length, lambda m: "act",
                       lambda m: act_to(core, gates[:, m, :], ACT.Sigmoid, core.v(("gate_b_2", layer), m)))
    product_stage(core, g, f"mixer{layer}")


def conv_stage(core, layer, u, sg, out, sequences):
    nc = core.nc
    half = CONV_K // 2
    with nc.Block() as block:

        @block.vector
        def _(dve):
            step = Steps(dve, core.dve_step)
            step(nc.vector.tensor_tensor(u, u, sg, ALU.mult))
            for m in range(KD):
                for t0, row in sequences:
                    def tap(k):
                        return core.v(("conv_w_2", layer), KD * k + m)
                    src, dst = u[:, m, t0:t0 + SEQ], out[:, m, t0:t0 + SEQ]
                    step(nc.vector.tensor_scalar(dst, src, tap(half), None, ALU.mult))
                    for k in range(CONV_K):
                        off = (k - half) * row
                        if k == half or abs(off) >= SEQ:
                            continue
                        a, b = max(0, -off), SEQ - max(0, off)
                        step(nc.vector.scalar_tensor_tensor(dst[:, a:b], src[:, a + off:b + off], tap(k), dst[:, a:b],
                                                            ALU.mult, ALU.add))
    core.settle()


def layer_norm_stage(core, layer, x, tmp, rstd, length):
    nc = core.nc
    with nc.Block() as block:

        @block.tensor
        def _(pe):
            for n, src in enumerate((x, tmp)):
                if n:
                    pe.wait_ge(core.from_dve.sem, core.from_dve.at(1))
                for k in range(KD):
                    last = nc.tensor.matmul(core.banks[:, n, 0:length], core.const["ones"], src[:, k, :], start=k == 0, stop=k == KD - 1)
                last.then_inc(core.product.sem, core.product.up())

        @block.scalar
        def _(act):
            act.wait_ge(core.from_dve.sem, core.from_dve.at(2))
            nc.scalar.activation(rstd, rstd, ACT.Sqrt).then_inc(core.from_act.sem, core.from_act.up())
            for m in range(KD):
                act.wait_ge(core.from_dve.sem, core.from_dve.at(3 + m))
                nc.scalar.activation(x[:, m, :], x[:, m, :], ACT.Silu).then_inc(core.act_step.sem, core.act_step.up())

        @block.vector
        def _(dve):
            step = Steps(dve, core.dve_step)
            dve.wait_ge(core.product.sem, core.product.at(1))
            step(nc.vector.tensor_scalar(rstd, core.banks[:, 0, 0:length], -1.0 / D, None, ALU.mult))
            step(nc.vector.tensor_tensor(x, x, rows(rstd, KD), ALU.add))
            nc.vector.tensor_tensor(tmp, x, x, ALU.mult).then_inc(core.from_dve.sem, core.from_dve.up())
            dve.wait_ge(core.product.sem, core.product.at(2))
            nc.vector.tensor_scalar(rstd, core.banks[:, 1, 0:length], 1.0 / D, LN_EPS, ALU.mult, ALU.add).then_inc(core.from_dve.sem, core.from_dve.up())
            dve.wait_ge(core.from_act.sem, core.from_act.at(1))
            step(nc.vector.reciprocal(rstd, rstd))
            step(nc.vector.tensor_tensor(x, x, rows(rstd, KD), ALU.mult))
            for m in range(KD):
                nc.vector.tensor_scalar(x[:, m, :], x[:, m, :], core.v(("cnorm_g_2", layer), m),
                                                          core.v(("cnorm_b_2", layer), m), ALU.mult, ALU.add).then_inc(core.from_dve.sem, core.from_dve.up())
    core.settle()


def mix_stage(core, layer, ya, yb, gates, m, tmp, length):
    nc = core.nc
    groups = []
    for br, y in enumerate((ya, yb)):
        def evacuate(mt, br=br):
            def run(step, ps):
                g = gates[:, KD * br + mt, :]
                if br == 0:
                    return nc.vector.tensor_tensor(m[:, mt, :], ps, g, ALU.mult)
                step(nc.vector.tensor_tensor(tmp, ps, g, ALU.mult))
                return nc.vector.tensor_tensor(m[:, mt, :], m[:, mt, :], tmp, ALU.add)
            return run
        groups += weight_groups(core, 2, KD, lambda k, y=y: y[:, k, :], length, lambda j: "dve", evacuate)
    product_stage(core, groups, f"mixer{layer}")


def mixer(core, layer, x, mod, g1, z_dram, y_dram):
    last_layer = layer == LAYERS - 1
    section = f"mixer{layer}"
    rwkv_branch(core, layer, x, mod, g1, z_dram, y_dram, (1,) if last_layer else (0, 1))
    t0, length = (SEQ, SEQ) if last_layer else (0, 2 * SEQ)
    segs = [(0, SEQ)] if last_layer else [(0, SEQ), (SEQ, 2 * SEQ)]
    first = 1 if last_layer else 0
    xs = x[:, :, t0:t0 + length]
    with ExitStack() as s:
        h, u = core.sb(s, "h", [P, KD, length]), core.sb(s, "u", [P, KD, length])
        rstd, gates = core.sb(s, "rstd", [P, length]), core.sb(s, "gates", [P, 2 * KD, length])
        sg = core.sb(s, "sg", [P, KD, length])
        norm_stage(core, xs, h[:, :, :], u[:, :, :], rstd[:, :], segs, lambda k, i: g1[:, k, first + i:first + i + 1],
                   lambda k, i: mod[:, k, first + i:first + i + 1], section)
        glu_stage(core, layer, h, u, sg, gates, length)
        yb = h
        sequences = [(0, GRID_W)] if last_layer else [(0, 1), (SEQ, GRID_W)]
        conv_stage(core, layer, u[:, :, :], sg[:, :, :], yb, sequences)
        layer_norm_stage(core, layer, yb[:, :, :], u[:, :, :], rstd[:, :], length)
        small_load_stage(core, [(u[:, :, :], y_dram[:, :, t0:t0 + length])])
        mix_stage(core, layer, u, yb, gates, sg, rstd[:, :], length)
        residual_stage(core, lambda k: sg[:, k, :], length, KD, 2, xs,
                       lambda m, i: mod[:, 2 * KD + m, first + i:first + i + 1], section, segs)



def peer_query_stage(core, layer, h, q, length):
    product_stage(core, weight_groups(core, 4, KD, lambda k: h[:, k, :], length, lambda m: "dve",
                                      lambda m: copy_to(core, q[:, m, :])), f"peer{layer}")


def route_stage(core, layer, q, n_tiles, keys_chunk, w, routeT):
    nc = core.nc
    keys = core.ring.chunk(keys_chunk)
    H, K, N = PEER_HEADS, TOPK, 2 * PEER_HEADS
    s, rest, top, num, cand, crest, best, pos = (w[k] for k in ("scores", "rest", "top", "numbers", "candidates",
                                                                "candidate_rest", "best", "position"))
    eq, ab, gw, stat, numf = (w[k] for k in ("equal", "halves", "weights", "stat", "numbers_f"))
    iota16 = core.const["iota16"]

    with nc.Block() as block:

        @block.tensor
        def _(pe):
            pe.wait_ge(core.ring.loaded[keys_chunk % RING], core.ring.at(keys_chunk))
            for t in range(n_tiles):
                if t:
                    pe.wait_ge(core.from_dve.sem, core.from_dve.at(2 * t - 1))
                for n in range(N):
                    last = nc.tensor.matmul(core.banks[:, n // 4, P * (n % 4):P * (n % 4) + P], q[:, n, P * t:P * t + P],
                                            keys[:, n, :], start=True, stop=True)
                last.then_inc(core.product.sem, core.product.up())
                read_keys = core.product.now()
                pe.wait_ge(core.from_dve.sem, core.from_dve.at(2 * t + 2))
                for i in range(3):
                    back = nc.tensor.transpose(core.banks[:, 4, P * i:P * i + P], gw[:, i, :], core.const["ident"])
                back.then_inc(core.product.sem, core.product.up())
            core.ring.release(keys_chunk, (core.product, read_keys))

        @block.scalar
        def _(act):
            for t in range(n_tiles):
                act.wait_ge(core.vector_max.sem, core.vector_max.at(t + 1))
                nc.scalar.activation(best[:, :, :], best[:, :, :], ACT.Exp).then_inc(core.from_act.sem, core.from_act.up())

        @block.vector
        def _(dve):
            step = Steps(dve, core.dve_step)

            def top16(values, scratch, out, numbers):
                step(nc.vector.max(out[:, 0:8], values))
                step(nc.vector.max_index(numbers[:, 0:8], out[:, 0:8], values))
                step(nc.vector.match_replace(scratch, out[:, 0:8], values, NEG))
                step(nc.vector.max(out[:, 8:16], scratch))
                step(nc.vector.max_index(numbers[:, 8:16], out[:, 8:16], scratch))

            for t in range(n_tiles):
                dve.wait_ge(core.product.sem, core.product.at(2 * t + 1))
                nc.vector.tensor_copy(s[:, :, :], core.banks[:, 0:4, :].rearrange("p b (n k) -> p (b n) k", k=NKEYS)).then_inc(core.from_dve.sem, core.from_dve.up())
                dve.wait_ge(core.from_dve.sem, core.from_dve.at(2 * t + 1))
                for n in range(N):
                    top16(s[:, n, :], rest[:, :], top[:, n, :], num[:, n, :])
                step(nc.vector.tensor_copy(numf[:, :, :], num[:, :, :]))
                for h in range(H):
                    c = cand[:, h, :]
                    step(nc.vector.tensor_tensor(c.rearrange("p (a b) -> p a b", a=K), columns(top[:, 2 * h, :], K),
                                                 rows(top[:, 2 * h + 1, :], K), ALU.add))
                    top16(c, crest[:, :], best[:, h, :], pos[:, h, :])
                step(nc.vector.tensor_copy(stat[:, 0:H], best[:, :, 0]))
                nc.vector.tensor_tensor(best[:, :, :], best[:, :, :], columns(stat[:, 0:H], K), ALU.subtract).then_inc(core.vector_max.sem, core.vector_max.up())
                step(nc.vector.tensor_scalar(pos[:, H:2 * H, :], pos[:, 0:H, :], 4, None, ALU.logical_shift_right))
                step(nc.vector.tensor_scalar(pos[:, 0:H, :], pos[:, 0:H, :], TOPK - 1, None, ALU.bitwise_and))
                step(nc.vector.tensor_copy(ab[:, :, :], pos[:, :, :]))
                for side in range(2):
                    for h in range(H):
                        place = ab[:, H * (1 - side) + h, :]
                        step(nc.vector.tensor_tensor(eq[:, :, :], columns(place, K), rows(iota16, K), ALU.is_equal))
                        step(nc.vector.tensor_tensor(eq[:, :, :], eq[:, :, :], rows(numf[:, 2 * h + side, :], K), ALU.mult))
                        step(nc.vector.tensor_reduce(gw[:, 1 + side, K * h:K * h + K], eq[:, :, :], AX.X, ALU.add))
                dve.wait_ge(core.from_act.sem, core.from_act.at(t + 1))
                step(nc.vector.tensor_reduce(stat[:, H:2 * H], best[:, :, :], AX.X, ALU.add))
                step(nc.vector.reciprocal(stat[:, H:2 * H], stat[:, H:2 * H]))
                nc.vector.tensor_tensor(gw[:, 0, :].rearrange("p (h k) -> p h k", h=H), best[:, :, :],
                                                          columns(stat[:, H:2 * H], K), ALU.mult).then_inc(core.from_dve.sem, core.from_dve.up())
                dve.wait_ge(core.product.sem, core.product.at(2 * t + 2))
                step(nc.vector.tensor_copy(routeT[:, :, P * t:P * t + P],
                                           core.banks[:, 4, 0:3 * P].rearrange("p (i t) -> p i t", i=3)))
    core.settle()


SPREAD = 8


def spread_stage(core, t0, routeT, pick, weight, g):
    nc = core.nc
    iota = core.const["iota"]
    turns = SEQ // SPREAD
    hot, prod, taken = core.from_dve, core.product, core.act_read

    with nc.Block() as block:

        @block.vector
        def _(dve):
            with dve.Fori(0, turns) as i:
                for b in range(SPREAD):
                    dve.wait_ge(prod.sem, i * 2 + (prod.base + b // 4 - 1))
                    t = i * SPREAD + (t0 + b)
                    nc.vector.tensor_scalar(pick[:, b, :], iota, routeT[:, 1, bass.ds(t, 1)], None, ALU.is_equal)
                    nc.vector.tensor_scalar(weight[:, b, :], iota, routeT[:, 2, bass.ds(t, 1)], routeT[:, 0, bass.ds(t, 1)],
                                            ALU.is_equal, ALU.mult).then_inc(hot.sem, 1)

        @block.tensor
        def _(pe):
            with pe.Fori(0, turns) as i:
                for half in range(2):
                    pe.wait_ge(taken.sem, i * 2 + (taken.base + half - 1))
                    for b in range(4):
                        pe.wait_ge(hot.sem, i * SPREAD + (hot.base + 4 * half + b + 1))
                        last = nc.tensor.matmul(core.banks[:, half, P * b:P * b + P], pick[:, 4 * half + b, :],
                                                weight[:, 4 * half + b, :], start=True, stop=True)
                    last.then_inc(prod.sem, 1)

        @block.scalar
        def _(act):
            with act.Fori(0, turns) as i:
                for half in range(2):
                    act.wait_ge(prod.sem, i * 2 + (prod.base + half + 1))
                    dst = g[:, :, bass.ds(i * SPREAD + 4 * half, 4)]
                    nc.scalar.activation(dst, core.banks[:, half, :].rearrange("p (t j) -> p j t", t=4),
                                         ACT.Identity).then_inc(taken.sem, 1)
    hot.pending += SPREAD * turns
    prod.pending += 2 * turns
    taken.pending += 2 * turns
    core.settle()


SLOTS = 4


def experts_stage(core, layer, h, x, g, slots, act_buf, gain, experts):
    nc = core.nc
    turns = NKEYS // SLOTS
    up, down, read, gated = core.product, core.down_done, core.act_read, core.from_dve
    loaded = core.experts_loaded

    with nc.Block() as block:

        @block.sync
        def _(sp):
            for b in range(SLOTS):
                sp.dma_start(slots[:, b, :], experts[layer, b]).then_inc(loaded[b].sem, 16)
            with sp.Fori(1, turns) as i:
                for b in range(SLOTS):
                    sp.wait_ge(down.sem, i * SLOTS + (down.base + b - SLOTS + 1))
                    sp.dma_start(slots[:, b, :], experts[layer, bass.ds(i * SLOTS + b, 1)].rearrange("o p n -> p (o n)")
                                 ).then_inc(loaded[b].sem, 16)

        @block.tensor
        def _(pe):
            def scores(i, b, first):
                pe.wait_ge(loaded[b].sem, i * 16 + (loaded[b].base + 16))
                if not first:
                    pe.wait_ge(read.sem, i * SLOTS + (read.base + b - SLOTS + 1))
                for k in range(KD):
                    last = nc.tensor.matmul(core.banks[:, 4 + b, 0:SEQ], slots[:, b, P * k:P * k + P], h[:, k, :],
                                            start=k == 0, stop=k == KD - 1)
                last.then_inc(up.sem, 1)

            def outputs(i, b, start, stop):
                pe.wait_ge(gated.sem, i * SLOTS + (gated.base + b + 1))
                for m in range(KD):
                    last = nc.tensor.matmul(core.banks[:, m // 2, SEQ * (m % 2):SEQ * (m % 2) + SEQ],
                                            slots[:, b, D + P * m:D + P * m + P], act_buf[:, b % 2, :],
                                            start=start and m % 2 == 0, stop=stop, skip_group_check=True)
                last.then_inc(down.sem, 1)

            scores(0, 0, True)
            for b in range(SLOTS):
                scores((b + 1) // SLOTS, (b + 1) % SLOTS, b + 1 < SLOTS)
                outputs(0, b, b == 0, False)
            with pe.Fori(1, turns - 1) as i:
                for b in range(SLOTS):
                    scores(i + (b + 1) // SLOTS, (b + 1) % SLOTS, False)
                    outputs(i, b, False, False)
            for b in range(SLOTS):
                if b + 1 < SLOTS:
                    scores(turns - 1, b + 1, False)
                outputs(turns - 1, b, False, b == SLOTS - 1)

        @block.scalar
        def _(act):
            def gelu(i, b, first):
                act.wait_ge(up.sem, i * SLOTS + (up.base + b + 1))
                if not first:
                    act.wait_ge(down.sem, i * SLOTS + (down.base + b - 1))
                nc.scalar.activation(act_buf[:, b % 2, :], core.banks[:, 4 + b, 0:SEQ], ACT.Gelu).then_inc(read.sem, 1)

            for b in range(SLOTS):
                gelu(0, b, b < 2)
            with act.Fori(1, turns) as i:
                for b in range(SLOTS):
                    gelu(i, b, False)

        @block.vector
        def _(dve):
            with dve.Fori(0, turns) as i:
                for b in range(SLOTS):
                    dve.wait_ge(read.sem, i * SLOTS + (read.base + b + 1))
                    nc.vector.tensor_tensor(act_buf[:, b % 2, :], act_buf[:, b % 2, :],
                                            g[:, bass.ds(i * SLOTS + b, 1), :].rearrange("p o t -> p (o t)"),
                                            ALU.mult).then_inc(gated.sem, 1)
            step = Steps(dve, core.dve_step)
            dve.wait_ge(down.sem, down.base + NKEYS)
            for m in range(KD):
                step(nc.vector.scalar_tensor_tensor(x[:, m, :], core.banks[:, m // 2, SEQ * (m % 2):SEQ * (m % 2) + SEQ],
                                                    gain(m), x[:, m, :], ALU.mult, ALU.add))
    for c in (up, down, read, gated):
        c.pending += NKEYS
    for c in loaded:
        c.pending += 16 * turns
    core.settle()


def peer(core, layer, x, mod, g2, experts, close_ring):
    last_layer = layer == LAYERS - 1
    section = f"peer{layer}"
    t0, length = (SEQ, SEQ) if last_layer else (0, 2 * SEQ)
    segs = [(0, SEQ)] if last_layer else [(0, SEQ), (SEQ, 2 * SEQ)]
    first = 1 if last_layer else 0
    xs = x[:, :, t0:t0 + length]
    H, K = PEER_HEADS, TOPK
    h, routeT = core.peer_h[:, :, 0:length], core.route[:, :, 0:length]
    with ExitStack() as s:
        q = core.sb(s, "q", [P, 2 * KD, length])
        with ExitStack() as t:
            squares, rstd = core.sb(t, "squares", [P, KD, length]), core.sb(t, "rstd", [P, length])
            norm_stage(core, xs, h, squares[:, :, :], rstd[:, :], segs,
                       lambda k, i: g2[:, k, first + i:first + i + 1],
                       lambda k, i: mod[:, 3 * KD + k, first + i:first + i + 1], section)
        peer_query_stage(core, layer, h, q, length)
        w = {"scores": core.sb(s, "scores", [P, 2 * H, NKEYS]), "rest": core.sb(s, "rest", [P, NKEYS]),
             "top": core.sb(s, "top", [P, 2 * H, K]), "numbers": core.sb(s, "numbers", [P, 2 * H, K], U32),
             "numbers_f": core.sb(s, "numbers_f", [P, 2 * H, K]),
             "candidates": core.sb(s, "candidates", [P, H, K * K]), "candidate_rest": core.sb(s, "candidate_rest", [P, K * K]),
             "best": core.sb(s, "best", [P, H, K]), "position": core.sb(s, "position", [P, 2 * H, K], U32),
             "equal": core.sb(s, "equal", [P, K, K]), "halves": core.sb(s, "halves", [P, 2 * H, K]),
             "weights": core.sb(s, "route", [P, 3, P]), "stat": core.sb(s, "route_stat", [P, 2 * H])}
        keys = core.next_chunk
        core.next_chunk += 1
        route_stage(core, layer, q, length // P, keys, w, routeT)
    close_ring()
    with ExitStack() as s:
        g = core.sb(s, "expert_weights", [P, NKEYS, SEQ])
        slots, act_buf = core.sb(s, "expert_tiles", [P, SLOTS, 2 * D]), core.sb(s, "activated", [P, 2, SEQ])
        for i, (a, b) in enumerate(segs):
            pick, weight = (slots[:, n, 0:SPREAD * P].rearrange("p (s n) -> p s n", n=P) for n in range(2))
            spread_stage(core, a, routeT, pick, weight, g)
            experts_stage(core, layer, h[:, :, a:b], xs[:, :, a:b], g, slots, act_buf,
                          lambda m, i=i: mod[:, 5 * KD + m, first + i:first + i + 1], experts)



CONSTANTS = ("ident", "ones", "head_ones", "iota", "iota16")


def build(nc, dram, debug=None):
    with ExitStack() as stack:
        core = Core(nc, stack, dram)
        core.down_done = core.count("expert_outputs_done")
        core.experts_loaded = [core.count(f"experts_loaded_{b}") for b in range(SLOTS)]
        x = core.sb(stack, "x", [P, KD, 2 * SEQ])[:, :, :]
        vec = core.sb(stack, "vectors", [P, core.nvec])
        core.vec = vec
        shapes = {k: v.shape[1] for k, v in constants().items()}
        for name in CONSTANTS:
            core.const[name] = core.sb(stack, name, [P, shapes[name]])[:, :]
        cc, mod = core.sb(stack, "silu_c", [P, KD, 2]), core.sb(stack, "modulation", [P, 48, 2])
        g1, g2 = core.sb(stack, "gain1", [P, KD, 2]), core.sb(stack, "gain2", [P, KD, 2])
        z_dram = [nc.dram_tensor(f"z_scratch_{i}", [P, 24, 2 * SEQ], F32, kind="Internal").ap() for i in range(LAYERS)]
        y_dram = [nc.dram_tensor(f"y_scratch_{i}", [P, KD, 2 * SEQ], F32, kind="Internal").ap() for i in range(LAYERS)]
        core.first_loads = [(x[:, :, 0:SEQ], dram["ctxT"]), (x[:, :, SEQ:], dram["xT"]), core.vector_load("common"), core.vector_load("first")]
        core.first_loads += [(core.const[name], dram["c_" + name]) for name in CONSTANTS]
        ring = WeightRing(nc, stack, None, dram["weights"])
        core.ring = ring
        xs = x[:, :, SEQ:]

        def mixer_layer(layer):
            small_load_stage(core, [core.vector_load(layer)])
            modulation_stage(core, layer, cc, mod, g1, g2)
            mixer(core, layer, x, mod, g1, z_dram[layer], y_dram[layer])
            if debug:
                debug(core, f"mixed{layer}", x[:, :, :])

        def peer_layer(layer, ring_stack):
            with ExitStack() as s:
                core.peer_h, core.route = core.sb(s, "peer_h", [P, KD, 2 * SEQ]), core.sb(s, "route_T", [P, 3, 2 * SEQ])
                inner = ExitStack()
                ring.slots = [core.sb(inner, f"weight_slot_{i}", [P, SLOT]) for i in range(RING)]
                peer(core, layer, x, mod, g2, dram["experts"], inner.close)
            if debug:
                debug(core, f"layer{layer}", x[:, :, :])

        with ExitStack() as s:
            ring.slots = [core.sb(s, f"weight_slot_{i}", [P, SLOT]) for i in range(RING)]
            load_stage(core, "mixer0")
            first_block(core, xs, dram["rel_bias"], stack)
            if debug:
                debug(core, "first", xs)
            mixer_layer(0)
        peer_layer(0, None)
        with ExitStack() as s:
            ring.slots = [core.sb(s, f"weight_slot_{i}", [P, SLOT]) for i in range(RING)]
            mixer_layer(1)
        peer_layer(1, None)
        with ExitStack() as s:
            squares, rstd = core.sb(s, "squares", [P, KD, SEQ]), core.sb(s, "rstd", [P, SEQ])
            norm_stage(core, xs, xs, squares[:, :, :], rstd[:, :], [(0, SEQ)], lambda k, i: core.v("final_g_2", k), None, "peer1")
        store_stage(core, dram["out"], xs)



def device_arrays(inputs):
    u, v = inputs["peer_u_2"], inputs["peer_v_2"]
    ut = u.reshape(LAYERS, NKEYS, NKEYS, KD, P).transpose(0, 2, 4, 3, 1).reshape(LAYERS, NKEYS, P, D)
    vt = v.reshape(LAYERS, NKEYS, NKEYS, D).transpose(0, 2, 1, 3)
    out = {
        "xT": inputs["x"][0].T.reshape(KD, P, SEQ).transpose(1, 0, 2),
        "ctxT": inputs["ctx_2"][0].T.reshape(KD, P, CTX).transpose(1, 0, 2),
        "rel_bias": inputs["rel_bias"],
        "weights": weight_stream(inputs),
        "experts": np.concatenate([ut, vt], 3),
    }
    out.update(vector_arrays(inputs))
    out.update({"c_" + k: a for k, a in constants().items()})
    return {k: np.ascontiguousarray(a) for k, a in out.items()}


def kernel(**inputs):
    from concourse import bacc
    from concourse.bass_utils import run_bass_kernel_spmd

    arrays = device_arrays(inputs)
    nc = bacc.Bacc("TRN2", target_bir_lowering=False, num_devices=1)
    dram = {k: nc.dram_tensor(k, a.shape, F32, kind="ExternalInput").ap() for k, a in arrays.items()}
    dram["out"] = nc.dram_tensor("out", (P, KD, SEQ), F32, kind="ExternalOutput").ap()
    build(nc, dram)
    r = run_bass_kernel_spmd(nc, [arrays], core_ids=[0])
    return np.ascontiguousarray(r.results[0]["out"].transpose(1, 0, 2).reshape(D, SEQ).T)[None]
```

```python
import math
from contextlib import ExitStack

import numpy as np

import concourse.bass as bass
from concourse import mybir

F32 = mybir.dt.float32
F32R = mybir.dt.float32r
U32 = mybir.dt.uint32
ALU = mybir.AluOpType
ACT = mybir.ActivationFunctionType
AX = mybir.AxisListType

P = 128
D = 1024
KD = D // P
SEQ = 256
CTX = 256
TT = SEQ // P
BANK = 512
NBANK = 8
EPS = 1e-6

RNN_BLOCKS = 8
CONV_RNN = 4
DIFF_HEADS = 4
FOX_HEADS = 8
HEAD = 64
D_FF = ((8 * D // 3 + 127) // 128) * 128
KF = D_FF // P
CONV_FFN = 3
N_BUCKETS = 32
LAM_INIT = 0.8 - 0.6 * math.exp(-0.3 * 0)
NEG = -1e30

LAYERS = 2
GRID_W = 64
RWKV_HEADS = 16
LORA_G = 160
GN_EPS = HEAD * 1e-5
LN_EPS = 1e-5
CONV_K = 31
P_RWKV = 3 * D + 4 * 64 + LORA_G
ZT = -(-P_RWKV // P)
PEER_HEADS = 8
NKEYS = 128
TOPK = 16
CHUNK = 64
NCH = SEQ // CHUNK
LEVELS = 6

RING = 2
SLOT = 4096



def tiles_of(a, kt):
    k, n = a.shape
    if k < kt * P:
        a = np.concatenate([a, np.zeros((kt * P - k, n), a.dtype)])
    return a.reshape(kt, P, n).transpose(1, 0, 2).reshape(P, kt * n)


def span(a, b):
    return [(a, b)]


def weight_plan():
    plan = []

    def add(section, name, layer, kt, spans):
        plan.append((section, name, layer, kt, spans, sum(b - a for a, b in spans)))

    for c in range(10):
        add("first", "w_in", 0, KD, span(512 * c, 512 * c + 512))
    add("first", "w_in", 0, KD, span(5120, 5128))
    for c in range(6):
        add("first", "w_in", 0, KD, span(5128 + 512 * c, 5640 + 512 * c))
    add("first", "rg", 0, 2 * RNN_BLOCKS, span(0, P))
    for c in range(2):
        add("first", "w_br_rnn", 0, 8, span(512 * c, 512 * c + 512))
        add("first", "w_br_diff", 0, 4, span(512 * c, 512 * c + 512))
        add("first", "w_br_fox", 0, 4, span(512 * c, 512 * c + 512))
    for c in range(2):
        add("first", "w_out", 0, KD, span(512 * c, 512 * c + 512))
    for c in range(KF // 2):
        add("first", "ffn_up", 0, KD, [(256 * c, 256 * c + 256), (D_FF + 256 * c, D_FF + 256 * c + 256)])
    for c in range(KD):
        add("first", "ffn_down", 0, KF, span(P * c, P * c + P))
    for layer in range(LAYERS):
        s = f"mixer{layer}"
        for c in range(12):
            add(s, "ada_w_2", layer, KD, span(512 * c, 512 * c + 512))
        for c in range(7):
            add(s, "w_in_2", layer, KD, span(512 * c, min(512 * c + 512, P_RWKV)))
        add(s, "lora_2", layer, 2, span(0, D))
        add(s, "g2_2", layer, 2, span(0, D))
        for c in range(4):
            a = P_RWKV + 256 * c
            add(s, "w_in_2", layer, KD, [(a, a + 256), (a + D, a + D + 256)])
        for c in range(4):
            a = P_RWKV + 2 * D + 512 * c
            add(s, "w_in_2", layer, KD, span(a, a + 512))
        for c in range(2):
            add(s, "w_oA_2", layer, KD, span(512 * c, 512 * c + 512))
        for c in range(2):
            add(s, "w_oB_2", layer, KD, span(512 * c, 512 * c + 512))
        for c in range(2):
            add(s, "w_out_2", layer, KD, span(512 * c, 512 * c + 512))
        s = f"peer{layer}"
        for c in range(4):
            add(s, "w_q_2", layer, KD, span(512 * c, 512 * c + 512))
        add(s, "keys_2", layer, 2 * PEER_HEADS, span(0, NKEYS))
    return plan


def weight_stream(inputs):
    w = dict(inputs)
    w["rg"] = np.concatenate([inputs["rg_w_r"], inputs["rg_w_i"]], 1).reshape(1, 2 * D, P)
    w["lora_2"] = np.concatenate([inputs["w2_2"].reshape(LAYERS, P, D), inputs["a2_2"].reshape(LAYERS, P, D)], 1)
    w["keys_2"] = inputs["sub_keys_2"].transpose(0, 1, 2, 4, 3).reshape(LAYERS, 2 * PEER_HEADS * P, NKEYS)
    blobs = []
    for _, name, layer, kt, spans, _ in weight_plan():
        cols = np.concatenate([w[name][layer][:, a:b] for a, b in spans], 1)
        blobs.append(tiles_of(cols, kt).reshape(-1))
    return np.concatenate(blobs)


def vector_plan():
    plan, width = {}, {}

    def group(name, start, entries):
        at = start
        for key, n in entries:
            plan[key] = (name, at, n)
            at += n
        width[name] = at - start
        return at

    common = group("common", 0, [("c_ctx_2", 8), ("c_2", 8), ("final_g_2", 8)])
    ends = [group("first", common, [
        ("norm1_g", 8), ("norm2_g", 8), ("final_g", 8), ("rnn_conv_w", 32), ("rnn_conv_b", 8), ("rg_b_r", 8), ("rg_b_i", 8),
        ("rg_a", 8), ("gate_b", 24), ("diff_subln_g", 1), ("diff_lq1", 1), ("diff_lk1", 1), ("diff_lq2", 1), ("diff_lk2", 1),
        ("fox_b_f", 1), ("ffn_conv_w", CONV_FFN * 2 * KF), ("ffn_conv_b", 2 * KF)])]
    for layer in range(LAYERS):
        ends.append(group(layer, common, [((name, layer), n) for name, n in (
            ("norm1_g_2", 8), ("norm2_g_2", 8), ("ada_b_2", 48), ("shift_mu_2", 2 * ZT), ("w0_2", 16), ("a0_2", 16),
            ("k_k_2", 8), ("k_a_2", 8), ("r_k_2", 8), ("lnx_g_2", 8), ("lnx_b_2", 8), ("conv_w_2", CONV_K * 8),
            ("cnorm_g_2", 8), ("cnorm_b_2", 8), ("gate_b_2", 16))]))
    return plan, width, max(ends)


def vector_arrays(inputs):
    plan, width, _ = vector_plan()
    out = {f"vectors_{g}": np.zeros((P, n), np.float32) for g, n in width.items()}
    for key, (g, at, n) in plan.items():
        v = inputs[key[0]][key[1]] if isinstance(key, tuple) else inputs[key]
        dst = out[f"vectors_{g}"]
        at -= 0 if g == "common" else width["common"]
        if key in ("diff_lq1", "diff_lk1", "diff_lq2", "diff_lk2", "fox_b_f"):
            dst[: v.size, at] = v.reshape(-1)
            continue
        if isinstance(key, tuple) and key[0] == "shift_mu_2":
            v = np.concatenate([v, np.zeros((2, ZT * P - P_RWKV), v.dtype)], 1)
        dst[:, at:at + n] = v.reshape(n, P).T
    return out


def constants():
    i = np.arange(P)
    t = i[:, None] % CHUNK
    s = np.arange(CHUNK)[None, :]
    tb, sb = i[:, None], i[None, :]
    same_head = tb // CHUNK == sb // CHUNK
    c = {
        "ident": np.eye(P),
        "ones": np.ones((P, P)),
        "head_ones": (i[:, None] // HEAD == i[None, :] // HEAD).astype(np.float32),
        "causal": np.where(i[:, None] >= i[None, :], 0.0, NEG),
        "above_bd": same_head & (sb > tb), "upto": (s >= t),
        "head_back": tb == np.arange(D)[None, :] // HEAD,
        "head_pattern": 14 + tb // HEAD == np.arange(30)[None, :],
        "levels": np.concatenate([same_head & (tb // (2 * b) == sb // (2 * b)) & (tb // b < sb // b)
                                  for b in (2 ** j for j in range(LEVELS))], 1),
        "iota": np.broadcast_to(i[None, :], (P, P)),
        "iota16": np.broadcast_to(np.arange(TOPK)[None, :], (P, TOPK)),
        "row_head": np.repeat(np.eye(P, FOX_HEADS), SEQ, axis=1),
    }
    dist = SEQ - 1 - np.arange(2 * SEQ - 1)
    n = np.maximum(dist, 0)
    half = N_BUCKETS // 2
    large = half + (np.log(np.maximum(n, 1).astype(np.float32) / np.float32(half)) / math.log(128 / half)
                    * (N_BUCKETS - half)).astype(np.int32)
    bucket = np.where(n < half, n, np.minimum(large, N_BUCKETS - 1))
    c["buckets"] = np.arange(P)[:, None] == bucket[None, :]
    return {k: np.asarray(v, np.float32) for k, v in c.items()}



class Count:

    def __init__(self, nc, stack, name):
        self.sem = stack.enter_context(nc.semaphore(name))
        self.base = self.pending = 0

    def up(self, by=1):
        self.pending += by
        return by

    def at(self, k):
        return self.base + k

    def now(self):
        return self.base + self.pending

    def settle(self):
        self.base += self.pending
        self.pending = 0


class Steps:

    def __init__(self, engine, count):
        self.engine, self.count = engine, count

    def __call__(self, instruction):
        instruction.then_inc(self.count.sem, self.count.up())
        self.engine.wait_ge(self.count.sem, self.count.now())


class WeightRing:

    def __init__(self, nc, stack, slots, stream):
        self.slots, self.stream = slots, stream
        self.loaded = [stack.enter_context(nc.semaphore(f"weights_loaded_{i}")) for i in range(RING)]
        self.plan = weight_plan()
        self.offset = list(np.cumsum([0] + [P * kt * n for _, _, _, kt, _, n in self.plan]))
        self.used = []
        self.issued = 0

    def last_of(self, section):
        return max(i for i, c in enumerate(self.plan) if c[0] == section) + 1

    def chunk(self, n):
        kt, width = self.plan[n][3], self.plan[n][5]
        return self.slots[n % RING][:, 0:kt * width].rearrange("p (k n) -> p k n", k=kt)

    def at(self, n):
        return 16 * (n // RING + 1)

    def release(self, n, mark):
        assert len(self.used) == n
        self.used.append(mark)

    def load(self, engine, section):
        end = min(self.last_of(section), len(self.used) + RING)
        while self.issued < end:
            n = self.issued
            if n >= RING:
                count, value = self.used[n - RING]
                engine.wait_ge(count.sem, value)
            kt, width = self.plan[n][3], self.plan[n][5]
            a, b = int(self.offset[n]), int(self.offset[n + 1])
            engine.dma_start(self.slots[n % RING][:, 0:kt * width],
                             self.stream[a:b].rearrange("(p n) -> p n", p=P)).then_inc(self.loaded[n % RING], 16)
            self.issued += 1


class Core:

    def __init__(self, nc, stack, dram):
        self.nc, self.stack, self.dram = nc, stack, dram
        self.counts = []
        self.product = self.count("product_ready")
        self.act_read = self.count("scalar_has_read")
        self.dve_read = self.count("vector_has_read")
        self.act_step = self.count("scalar_step")
        self.dve_step = self.count("vector_step")
        self.from_act = self.count("scalar_result_ready")
        self.from_dve = self.count("vector_result_ready")
        self.masked = self.count("level_part_masked")
        self.high_ready = self.count("high_part_ready")
        self.low_ready = self.count("low_part_ready")
        self.vector_max = self.count("row_maximum_ready")
        self.landed = self.count("small_load_landed")
        self.stored = self.count("store_done")
        self.banks = stack.enter_context(nc.psum_tensor("banks", [P, NBANK, BANK], F32))
        self.const = {}
        self.n_tensors = 0
        self.vec = None
        self.plan, self.vector_width, self.nvec = vector_plan()
        self.ring = None
        self.next_chunk = 0

    def count(self, name):
        c = Count(self.nc, self.stack, name)
        self.counts.append(c)
        return c

    def sb(self, stack, name, shape, dtype=F32):
        self.n_tensors += 1
        return stack.enter_context(self.nc.sbuf_tensor(f"{name}_{self.n_tensors}", shape, dtype))

    def vector_load(self, group):
        at = 0 if group == "common" else self.vector_width["common"]
        return self.vec[:, at:at + self.vector_width[group]], self.dram[f"vectors_{group}"]

    def settle(self):
        for c in self.counts:
            c.settle()

    def v(self, key, i=0, n=1):
        _, at, width = self.plan[key]
        assert i + n <= width
        return self.vec[:, at + i:at + i + n]


def columns(ap, width):
    return ap.unsqueeze(2).broadcast_to([ap.shape[0], ap.shape[1], width])


def rows(ap, n):
    return ap.unsqueeze(1).broadcast_to([ap.shape[0], n, ap.shape[1]])


def load_stage(core, section):
    nc = core.nc
    with nc.Block() as block:

        @block.sync
        def _(sp):
            n = 0
            for dst, src in core.first_loads:
                sp.dma_start(dst, src).then_inc(core.landed.sem, core.landed.up(16))
                n += 16
            sp.wait_ge(core.landed.sem, core.landed.at(n))
            core.ring.load(sp, section)
    core.settle()


def norm_stage(core, src, dst, squares, rstd, segments, gain, shift, section, eps=EPS):
    nc = core.nc
    length = src.shape[2]
    mean = core.banks[:, 0, 0:length]
    with nc.Block() as block:

        @block.tensor
        def _(pe):
            for k in range(KD):
                pe.wait_ge(core.from_dve.sem, core.from_dve.at(k + 1))
                last = nc.tensor.matmul(mean, core.const["ones"], squares[:, k, :], start=k == 0, stop=k == KD - 1)
            last.then_inc(core.product.sem, core.product.up())

        @block.scalar
        def _(act):
            act.wait_ge(core.from_dve.sem, core.from_dve.at(KD + 1))
            nc.scalar.activation(rstd, rstd, ACT.Sqrt).then_inc(core.from_act.sem, core.from_act.up())
            if shift is not None:
                for k in range(KD):
                    act.wait_ge(core.from_dve.sem, core.from_dve.at(KD + 2 + k))
                    for i, (a, b) in enumerate(segments):
                        nc.scalar.activation(dst[:, k, a:b], dst[:, k, a:b], ACT.Identity, bias=shift(k, i), scale=gain(k, i)
                                             ).then_inc(core.act_step.sem, core.act_step.up())

        @block.vector
        def _(dve):
            step = Steps(dve, core.dve_step)
            for k in range(KD):
                nc.vector.tensor_tensor(squares[:, k, :], src[:, k, :], src[:, k, :], ALU.mult
                                        ).then_inc(core.from_dve.sem, core.from_dve.up())
            dve.wait_ge(core.product.sem, core.product.at(1))
            nc.vector.tensor_scalar(rstd, mean, 1.0 / D, eps, ALU.mult, ALU.add).then_inc(core.from_dve.sem, core.from_dve.up())
            dve.wait_ge(core.from_act.sem, core.from_act.at(1))
            step(nc.vector.reciprocal(rstd, rstd))
            for k in range(KD):
                if shift is not None:
                    nc.vector.tensor_tensor(dst[:, k, :], src[:, k, :], rstd, ALU.mult
                                            ).then_inc(core.from_dve.sem, core.from_dve.up())
                    continue
                for i, (a, b) in enumerate(segments):
                    last = nc.vector.scalar_tensor_tensor(dst[:, k, a:b], src[:, k, a:b], gain(k, i), rstd[:, a:b],
                                                          ALU.mult, ALU.mult)
            if shift is None:
                step(last)

        @block.sync
        def _(sp):
            core.ring.load(sp, section)
    core.settle()


SPLIT = 3


def split_moving(core, stack, h):
    length = h.shape[2]
    moving = [core.sb(stack, f"moving_{name}", [P, KD, length], F32R)[:, :, :] for name in ("high", "low")]
    slots = [core.sb(stack, f"weights_{name}", [P, SPLIT, KD, P], F32R) for name in ("high", "low")]
    halves_stage(core, h, *moving)
    return {"moving": moving, "slots": slots}


def halves_stage(core, src, high, low):
    nc = core.nc
    with nc.Block() as block:

        @block.scalar
        def _(act):
            for k in range(KD):
                nc.scalar.activation(high[:, k, :], src[:, k, :], ACT.Identity).then_inc(core.from_act.sem, core.from_act.up())

        @block.vector
        def _(dve):
            for k in range(KD):
                dve.wait_ge(core.from_act.sem, core.from_act.at(k + 1))
                nc.vector.tensor_tensor(low[:, k, :], src[:, k, :], high[:, k, :].bitcast(F32), ALU.subtract
                                        ).then_inc(core.dve_step.sem, core.dve_step.up())
    core.settle()


class Group:

    def __init__(self, reader, parts, evacuate, rows=P, cols=BANK, chunks=(), frees=(), tile=None):
        self.reader, self.parts, self.evacuate, self.tile = reader, parts, evacuate, tile
        self.rows, self.cols, self.chunks, self.frees = rows, cols, chunks, frees


def product_stage(core, groups, section, stage_banks=NBANK, side=None, vector_side=None, split=None):
    nc = core.nc
    in_parts = [i for i, g in enumerate(groups) if split is not None and g.tile is not None]
    nth = {i: n for n, i in enumerate(in_parts)}
    rank, n = [], {"act": 0, "dve": 0}
    for g in groups:
        n[g.reader] += 1
        rank.append(n[g.reader])
    reads = {"act": core.act_read, "dve": core.dve_read}

    def bank(i):
        g = groups[i]
        return core.banks[0:g.rows, i % stage_banks, 0:g.cols]

    with nc.Block() as block:

        @block.tensor
        def _(pe):
            for i, g in enumerate(groups):
                if i >= stage_banks:
                    j = i - stage_banks
                    pe.wait_ge(reads[groups[j].reader].sem, reads[groups[j].reader].at(rank[j]))
                if i in nth:
                    pe.wait_ge(core.low_ready.sem, core.low_ready.at(nth[i] + 1))
                    (h_high, h_low), w_high, w_low = split["moving"], *(x[:, nth[i] % SPLIT] for x in split["slots"])
                    for k in range(KD):
                        nc.tensor.matmul(bank(i), w_high[:, k, :], h_high[:, k, :], start=k == 0, stop=False)
                        nc.tensor.matmul(bank(i), w_high[:, k, :], h_low[:, k, :], start=False, stop=False)
                        last = nc.tensor.matmul(bank(i), w_low[:, k, :], h_high[:, k, :], start=False, stop=k == KD - 1)
                else:
                    for c in g.chunks:
                        pe.wait_ge(core.ring.loaded[c % RING], core.ring.at(c))
                    for k, (lhsT, rhs) in enumerate(g.parts):
                        last = nc.tensor.matmul(bank(i), lhsT, rhs, start=k == 0, stop=k == len(g.parts) - 1)
                last.then_inc(core.product.sem, core.product.up())
                for c in g.frees:
                    mark = (core.low_ready, core.low_ready.base + nth[i] + 1) if i in nth else (core.product, core.product.now())
                    core.ring.release(c, mark)

        @block.scalar
        def _(act):
            step = Steps(act, core.act_step)

            def high_part(n):
                if n < len(in_parts):
                    g = groups[in_parts[n]]
                    act.wait_ge(core.ring.loaded[g.chunk % RING], core.ring.at(g.chunk))
                    if n >= SPLIT:
                        act.wait_ge(core.product.sem, core.product.at(in_parts[n - SPLIT] + 1))
                    nc.scalar.activation(split["slots"][0][:, n % SPLIT], g.tile, ACT.Identity
                                         ).then_inc(core.high_ready.sem, core.high_ready.up())

            for n in range(SPLIT):
                high_part(n)
            for i, g in enumerate(groups):
                if g.reader == "act":
                    act.wait_ge(core.product.sem, core.product.at(i + 1))
                    g.evacuate(step, bank(i)).then_inc(core.act_read.sem, core.act_read.up())
                    act.wait_ge(core.act_read.sem, core.act_read.now())
                if i in nth:
                    high_part(nth[i] + SPLIT)
            if side is not None:
                side(act)

        @block.vector
        def _(dve):
            step = Steps(dve, core.dve_step)

            def low_part(n):
                if n < len(in_parts):
                    dve.wait_ge(core.high_ready.sem, core.high_ready.at(n + 1))
                    high, low = (x[:, n % SPLIT] for x in split["slots"])
                    nc.vector.tensor_tensor(low, groups[in_parts[n]].tile, high.bitcast(F32), ALU.subtract
                                            ).then_inc(core.low_ready.sem, core.low_ready.up())

            for n in range(SPLIT):
                low_part(n)
            for i, g in enumerate(groups):
                if g.reader == "dve":
                    dve.wait_ge(core.product.sem, core.product.at(i + 1))
                    g.evacuate(step, bank(i)).then_inc(core.dve_read.sem, core.dve_read.up())
                    dve.wait_ge(core.dve_read.sem, core.dve_read.now())
                if i in nth:
                    low_part(nth[i] + SPLIT)
            if vector_side is not None:
                vector_side(step)

        @block.sync
        def _(sp):
            core.ring.load(sp, section)
    core.settle()


def weight_groups(core, n_chunks, kt, moving, length, reader, evacuate):
    groups, m = [], 0
    for _ in range(n_chunks):
        c = core.next_chunk
        core.next_chunk += 1
        w = core.ring.chunk(c)
        width = w.shape[2]
        n_m = -(-width // P)
        for j in range(n_m):
            rows_here = min(P, width - P * j)
            parts = [(w[:, k, P * j:P * j + rows_here], moving(k)) for k in range(kt)]
            groups.append(Group(reader(m), parts, evacuate(m), rows_here, length,
                                chunks=(c,) if j == 0 or rows_here < P else (), frees=(c,) if j == n_m - 1 else (),
                                tile=w[:, :, P * j:P * j + P] if rows_here == P and kt == KD else None))
            groups[-1].chunk = c
            m += 1
    return groups


def token_groups(core, kt, stationary, reader, evacuate):
    c = core.next_chunk
    core.next_chunk += 1
    w = core.ring.chunk(c)
    return [Group(reader, [(stationary(k, t), w[:, k, :]) for k in range(kt)], evacuate(t), P, w.shape[2],
                  chunks=(c,) if t == 0 else (), frees=(c,) if t == TT - 1 else ()) for t in range(TT)]


def copy_to(core, dst):
    return lambda step, ps: core.nc.vector.tensor_copy(dst, ps)


def act_to(core, dst, func, bias=0.0, scale=1.0):
    return lambda step, ps: core.nc.scalar.activation(dst, ps, func, bias=bias, scale=scale)


def projection_stage(core, h, out):
    def moving(k):
        return h[:, k, :]

    dve, act = (lambda m: "dve"), (lambda m: "act")
    g = weight_groups(core, 2, KD, moving, SEQ, dve, lambda m: copy_to(core, out["x_rnn"][:, m, :]))
    g += weight_groups(core, 2, KD, moving, SEQ, act, lambda m: act_to(core, out["g_rnn"][:, m, :], ACT.Gelu_apprx_tanh))
    g += weight_groups(core, 1, KD, moving, SEQ, dve, lambda m: copy_to(core, out["dq"][:, m, :]))
    g += weight_groups(core, 1, KD, moving, SEQ, dve, lambda m: copy_to(core, out["dk"][:, m, :]))
    g += token_groups(core, KD, lambda k, t: h[:, k, P * t:P * t + P], "dve", lambda t: copy_to(core, out["dv"][:, t, :]))
    g += weight_groups(core, 1, KD, moving, SEQ, dve, lambda m: copy_to(core, out["fq"][:, m, :]))
    g += weight_groups(core, 1, KD, moving, SEQ, dve, lambda m: copy_to(core, out["fk"][:, m, :]))
    g += token_groups(core, KD, lambda k, t: h[:, k, P * t:P * t + P], "dve", lambda t: copy_to(core, out["fv"][:, t, :]))
    g += weight_groups(core, 1, KD, moving, SEQ, act, lambda m: act_to(core, out["f_logit"], ACT.Identity,
                                                                       core.v("fox_b_f")[0:FOX_HEADS]))
    g += weight_groups(core, 6, KD, moving, SEQ, act, lambda m: act_to(core, out["gates"][:, m, :], ACT.Sigmoid,
                                                                       core.v("gate_b", m)))
    with ExitStack() as s:
        product_stage(core, g, "mixer0", split=split_moving(core, s, h[:, :, :]))


def softplus_steps(core, step, act_ready, dve, x, tmp, out, exp_result):
    nc = core.nc
    s, s2, p = tmp
    act_ready()
    step(nc.vector.tensor_scalar(s2, exp_result, 2.0, None, ALU.add))
    step(nc.vector.reciprocal(s2, s2))
    step(nc.vector.tensor_tensor(s, exp_result, s2, ALU.mult))
    step(nc.vector.tensor_tensor(s2, s, s, ALU.mult))
    step(nc.vector.tensor_scalar(p, s2, 1.0 / 17, None, ALU.mult))
    for n in (15, 13, 11, 9, 7, 5, 3):
        step(nc.vector.scalar_tensor_tensor(p, p, 1.0 / n, s2, ALU.add, ALU.mult))
    step(nc.vector.scalar_tensor_tensor(p, p, 1.0, s, ALU.add, ALU.mult))
    step(nc.vector.tensor_scalar(p, p, 2.0, None, ALU.mult))
    step(nc.vector.scalar_tensor_tensor(out, x, 0.0, p, ALU.max, ALU.add))


def rnn_stage(core, stack, out, y):
    nc = core.nc
    xr, g = out["x_rnn"], out["g_rnn"]
    xc = core.sb(stack, "rnn_conv", [P, KD, SEQ])
    r = core.sb(stack, "rnn_r", [P, KD, SEQ])
    i_gate = core.sb(stack, "rnn_i", [P, KD, SEQ])
    a = core.sb(stack, "rnn_a", [P, KD, SEQ])
    neg_a, small = core.sb(stack, "rnn_neg_a", [P, KD]), core.sb(stack, "rnn_small", [P, 5, KD])
    c = core.next_chunk
    core.next_chunk += 1
    w = core.ring.chunk(c)

    with nc.Block() as block:

        @block.tensor
        def _(pe):
            pe.wait_ge(core.ring.loaded[c % RING], core.ring.at(c))
            pe.wait_ge(core.from_dve.sem, core.from_dve.at(2))
            for n in range(2 * RNN_BLOCKS):
                if n >= NBANK:
                    pe.wait_ge(core.act_read.sem, core.act_read.at(n - NBANK + 1))
                nc.tensor.matmul(core.banks[:, n % NBANK, 0:SEQ], w[:, n, :], xc[:, n % RNN_BLOCKS, :],
                                                         start=True, stop=True).then_inc(core.product.sem, core.product.up())
            core.ring.release(c, (core.product, core.product.now()))

        @block.scalar
        def _(act):
            step = Steps(act, core.act_step)
            act.wait_ge(core.from_dve.sem, core.from_dve.at(1))
            nc.scalar.activation(small[:, 4, :], neg_a[:, :], ACT.Exp).then_inc(core.from_act.sem, core.from_act.up())
            for n in range(2 * RNN_BLOCKS):
                act.wait_ge(core.product.sem, core.product.at(n + 1))
                gate, bias = (r, "rg_b_r") if n < RNN_BLOCKS else (i_gate, "rg_b_i")
                nc.scalar.activation(gate[:, n % RNN_BLOCKS, :], core.banks[:, n % NBANK, 0:SEQ], ACT.Sigmoid,
                                                       bias=core.v(bias, n % RNN_BLOCKS)).then_inc(core.act_read.sem, core.act_read.up())
            act.wait_ge(core.from_dve.sem, core.from_dve.at(3))
            step(nc.scalar.activation(a[:, :, :], r[:, :, :], ACT.Exp))
            nc.scalar.activation(r[:, :, :], r[:, :, :], ACT.Tanh, scale=-1.0).then_inc(core.from_act.sem, core.from_act.up())
            act.wait_ge(core.from_dve.sem, core.from_dve.at(4))
            nc.scalar.activation(r[:, :, :], r[:, :, :], ACT.Sqrt).then_inc(core.from_act.sem, core.from_act.up())

        @block.vector
        def _(dve):
            step = Steps(dve, core.dve_step)
            step(nc.vector.tensor_scalar(small[:, 0, :], core.v("rg_a", 0, 8), -1.0, None, ALU.mult))
            step(nc.vector.tensor_tensor(neg_a[:, :], small[:, 0, :], core.v("rg_a", 0, 8), ALU.min))
            nc.vector.tensor_scalar(neg_a[:, :], neg_a[:, :], 1.0, None, ALU.mult).then_inc(core.from_dve.sem, core.from_dve.up())
            for n in range(KD):
                w0 = core.v("rnn_conv_w", n + 24)
                step(nc.vector.tensor_scalar(xc[:, n, :], xr[:, n, :], w0, core.v("rnn_conv_b", n), ALU.mult, ALU.add))
                for d in range(1, CONV_RNN):
                    wd = core.v("rnn_conv_w", 8 * (CONV_RNN - 1 - d) + n)
                    last = nc.vector.scalar_tensor_tensor(xc[:, n, d:], xr[:, n, 0:SEQ - d], wd, xc[:, n, d:], ALU.mult, ALU.add)
                    if n == KD - 1 and d == CONV_RNN - 1:
                        last.then_inc(core.from_dve.sem, core.from_dve.up())
                    else:
                        step(last)
            softplus_steps(core, step, lambda: dve.wait_ge(core.from_act.sem, core.from_act.at(1)), dve, small[:, 0, :],
                           (small[:, 1, :], small[:, 2, :], small[:, 3, :]), neg_a[:, :], small[:, 4, :])
            dve.wait_ge(core.act_read.sem, core.act_read.at(2 * RNN_BLOCKS))
            for n in range(KD):
                last = nc.vector.tensor_scalar(r[:, n, :], r[:, n, :], neg_a[:, n:n + 1], -8.0, ALU.mult, ALU.mult)
                last.then_inc(core.from_dve.sem, core.from_dve.up()) if n == KD - 1 else step(last)
            step(nc.vector.tensor_tensor(i_gate[:, :, :], i_gate[:, :, :], xc[:, :, :], ALU.mult))
            dve.wait_ge(core.from_act.sem, core.from_act.at(2))
            step(nc.vector.tensor_tensor(xc[:, :, :], a[:, :, :], a[:, :, :], ALU.mult))
            nc.vector.scalar_tensor_tensor(r[:, :, :], xc[:, :, :], 1.0, r[:, :, :], ALU.add, ALU.mult).then_inc(core.from_dve.sem, core.from_dve.up())
            dve.wait_ge(core.from_act.sem, core.from_act.at(3))
            step(nc.vector.tensor_tensor(i_gate[:, :, :], i_gate[:, :, :], r[:, :, :], ALU.mult))
            for n in range(KD):
                step(nc.vector.tensor_tensor_scan(y[:, n, :], a[:, n, :], i_gate[:, n, :], 0.0, ALU.mult, ALU.add))
            step(nc.vector.tensor_tensor(y[:, :, :], y[:, :, :], g[:, :, :], ALU.mult))

        @block.sync
        def _(sp):
            core.ring.load(sp, "mixer0")
    core.settle()


DISTANCES = 384


def attention_setup_stage(core, work, out, rel_bias, buckets, repeated, by_distance, scratch):
    nc = core.nc
    lam, prod, f = work["lam"], work["lam_products"], work["f"]
    bias = work["bias"]
    with nc.Block() as block:

        @block.tensor
        def _(pe):
            pe.wait_ge(core.vector_max.sem, core.vector_max.at(1))
            for h in range(DIFF_HEADS):
                last = nc.tensor.matmul(core.banks[:, 1 + h, 0:DISTANCES], repeated[:, h, :], buckets[:, 0:DISTANCES], start=True, stop=True)
            last.then_inc(core.product.sem, core.product.up())
            pe.wait_ge(core.from_dve.sem, core.from_dve.at(1))
            nc.tensor.matmul(core.banks[:, 0, 0:2], core.const["ones"], prod[:, :], start=True, stop=True).then_inc(core.product.sem, core.product.up())

        @block.sync
        def _(sp):
            sp.wait_ge(core.vector_max.sem, core.vector_max.at(2))
            flat = scratch.rearrange("h (p w) -> p h w", w=DISTANCES)
            sp.dma_start(flat, by_distance[:, :, :]).then_inc(core.stored.sem, core.stored.up(16))
            sp.wait_ge(core.stored.sem, core.stored.at(16))
            w = DISTANCES - 1
            shifted = scratch[:, P - 1:P - 1 + P * w].rearrange("h (p w) -> p h w", w=w)[:, :, 0:SEQ]
            sp.dma_start(bias[:, :, :], shifted).then_inc(core.landed.sem, core.landed.up(16))

        @block.scalar
        def _(act):
            act.wait_ge(core.product.sem, core.product.at(2))
            nc.scalar.activation(lam[:, 0:2], core.banks[:, 0, 0:2], ACT.Exp).then_inc(core.from_act.sem, core.from_act.up())
            act.wait_ge(core.from_dve.sem, core.from_dve.at(2))
            nc.scalar.activation(f[:, 4, :], f[:, 3, :], ACT.Exp).then_inc(core.from_act.sem, core.from_act.up())

        @block.vector
        def _(dve):
            step = Steps(dve, core.dve_step)
            nc.vector.tensor_copy(repeated[:, :, :], columns(rel_bias, P)).then_inc(core.vector_max.sem, core.vector_max.up())
            dve.wait_ge(core.product.sem, core.product.at(1))
            nc.vector.tensor_copy(by_distance[:, :, :], core.banks[:, 1:1 + DIFF_HEADS, 0:DISTANCES]
                                  ).then_inc(core.vector_max.sem, core.vector_max.up())
            step(nc.vector.tensor_tensor(prod[:, 0:1], core.v("diff_lq1"), core.v("diff_lk1"), ALU.mult))
            nc.vector.tensor_tensor(prod[:, 1:2], core.v("diff_lq2"), core.v("diff_lk2"), ALU.mult).then_inc(core.from_dve.sem, core.from_dve.up())
            dve.wait_ge(core.from_act.sem, core.from_act.at(1))
            step(nc.vector.tensor_tensor(lam[:, 2:3], lam[:, 1:2], lam[:, 0:1], ALU.subtract))
            step(nc.vector.tensor_scalar(lam[:, 2:3], lam[:, 2:3], -LAM_INIT, None, ALU.add))
            step(nc.vector.tensor_scalar(f[:, 0, :], out["f_logit"], -1.0, None, ALU.mult))
            nc.vector.tensor_tensor(f[:, 3, :], f[:, 0, :], out["f_logit"], ALU.min).then_inc(core.from_dve.sem, core.from_dve.up())
            softplus_steps(core, step, lambda: dve.wait_ge(core.from_act.sem, core.from_act.at(2)), dve, f[:, 0, :],
                           (f[:, 1, :], f[:, 2, :], f[:, 3, :]), f[:, 5, :], f[:, 4, :])
            step(nc.vector.memset(f[:, 0, :], 1.0))
            step(nc.vector.tensor_tensor_scan(f[:, 1, :], f[:, 0, :], f[:, 5, :], 0.0, ALU.mult, ALU.add))
            step(nc.vector.tensor_scalar(f[:, 2, :], f[:, 1, :], -8.0, None, ALU.mult))
            step(nc.vector.tensor_scalar(f[:, 3, :], f[:, 1, :], 8.0, None, ALU.mult))
            dve.wait_ge(core.landed.sem, core.landed.at(16))
            step(nc.vector.tensor_tensor(bias[:, :, P:SEQ], bias[:, :, P:SEQ],
                                         rows(core.const["causal"], DIFF_HEADS), ALU.add))
    core.settle()


def attention_stage(core, work, out, o_diff, y_fox):
    nc = core.nc
    units = [("diff", h, t) for h in range(DIFF_HEADS) for t in range(TT)]
    units += [("fox", h, t) for h in range(FOX_HEADS) for t in range(TT)]
    s, w, stat, wT, f, lam = (work[k] for k in ("scores", "weights", "stat", "weightsT", "f", "lam"))
    rh = work["row_head"]
    causal, bias = core.const["causal"], work["bias"]

    with nc.Block() as block:

        @block.tensor
        def _(pe):
            for u, (kind, h, t) in enumerate(units):
                b = 4 * (u % 2)
                keys = P * (t + 1)
                q = slice(P * t, P * t + P)
                if u >= 2:
                    pe.wait_ge(core.from_dve.sem, core.from_dve.at(3 * (u - 1)))
                if kind == "diff":
                    for c in range(2):
                        r = slice(HEAD * c, HEAD * c + HEAD)
                        last = nc.tensor.matmul(core.banks[:, b + c, 0:keys], out["dq"][r, h, q], out["dk"][r, h, 0:keys],
                                                start=True, stop=True)
                else:
                    r = slice(HEAD * (h % 2), HEAD * (h % 2) + HEAD)
                    nc.tensor.matmul(core.banks[:, b, 0:keys], out["fq"][r, h // 2, q], out["fk"][r, h // 2, 0:keys],
                                     start=True, stop=False)
                    nc.tensor.matmul(core.banks[:, b, 0:keys], f[:, 2, q], rh[:, 2 * P * h:2 * P * h + keys], start=False, stop=False)
                    last = nc.tensor.matmul(core.banks[:, b, 0:keys], rh[:, 2 * P * h:2 * P * h + P], f[:, 3, 0:keys],
                                            start=False, stop=True)
                last.then_inc(core.product.sem, core.product.up())
                pe.wait_ge(core.from_dve.sem, core.from_dve.at(3 * u + 1))
                for j in range(t + 1):
                    last = nc.tensor.transpose(core.banks[:, b + 2, P * j:P * j + P], w[:, P * j:P * j + P], core.const["ident"])
                last.then_inc(core.product.sem, core.product.up())
                pe.wait_ge(core.from_dve.sem, core.from_dve.at(3 * u + 2))
                if kind == "diff":
                    dst = core.banks[:, b + 3, 0:P]
                    v = [out["dv"][:, j, P * h:P * h + P] for j in range(t + 1)]
                else:
                    dst = core.banks[HEAD * (h % 2):HEAD * (h % 2) + HEAD, b + 3, 0:P]
                    v = [out["fv"][:, j, HEAD * h:HEAD * h + HEAD] for j in range(t + 1)]
                for j in range(t + 1):
                    last = nc.tensor.matmul(dst, v[j], wT[:, P * j:P * j + P], start=j == 0, stop=j == t)
                last.then_inc(core.product.sem, core.product.up())

        @block.scalar
        def _(act):
            n = 0
            for u, (kind, h, t) in enumerate(units):
                keys = P * (t + 1)
                for c in range(2 if kind == "diff" else 1):
                    n += 1
                    act.wait_ge(core.vector_max.sem, core.vector_max.at(n))
                    nc.scalar.activation(s[:, c, 0:keys], s[:, c, 0:keys], ACT.Exp, bias=stat[:, c:c + 1],
                                                           accum_out=stat[:, 2 + c:3 + c]).then_inc(core.from_act.sem, core.from_act.up())

        @block.vector
        def _(dve):
            step = Steps(dve, core.dve_step)
            n = 0
            for u, (kind, h, t) in enumerate(units):
                b = 4 * (u % 2)
                keys = P * (t + 1)
                maps = 2 if kind == "diff" else 1
                dve.wait_ge(core.product.sem, core.product.at(3 * u + 1))
                for c in range(maps):
                    src = core.banks[:, b + c, 0:keys]
                    if kind == "diff":
                        extra = bias[:, h, SEQ - keys:SEQ]
                        step(nc.vector.scalar_tensor_tensor(s[:, c, 0:keys], src, HEAD ** -0.5, extra, ALU.mult, ALU.add))
                    else:
                        step(nc.vector.tensor_scalar(s[:, c, 0:keys], src, HEAD ** -0.5, None, ALU.mult))
                        step(nc.vector.tensor_tensor(s[:, c, keys - P:keys], s[:, c, keys - P:keys], causal, ALU.add))
                    n += 1
                    nc.vector.tensor_reduce(stat[:, c:c + 1], s[:, c, 0:keys], AX.X, ALU.max, negate=True).then_inc(core.vector_max.sem, core.vector_max.up())
                dve.wait_ge(core.from_act.sem, core.from_act.at(n))
                step(nc.vector.reciprocal(stat[:, 4:4 + maps], stat[:, 2:2 + maps]))
                if kind == "diff":
                    step(nc.vector.tensor_scalar(stat[:, 5:6], stat[:, 5:6], lam[:, 2:3], None, ALU.mult))
                    step(nc.vector.tensor_scalar(s[:, 1, 0:keys], s[:, 1, 0:keys], stat[:, 5:6], None, ALU.mult))
                    last = nc.vector.scalar_tensor_tensor(w[:, 0:keys], s[:, 0, 0:keys], stat[:, 4:5], s[:, 1, 0:keys],
                                                          ALU.mult, ALU.add)
                else:
                    last = nc.vector.tensor_scalar(w[:, 0:keys], s[:, 0, 0:keys], stat[:, 4:5], None, ALU.mult)
                last.then_inc(core.from_dve.sem, core.from_dve.up())
                dve.wait_ge(core.product.sem, core.product.at(3 * u + 2))
                nc.vector.tensor_copy(wT[:, 0:keys], core.banks[:, b + 2, 0:keys]).then_inc(core.from_dve.sem, core.from_dve.up())
                dve.wait_ge(core.product.sem, core.product.at(3 * u + 3))
                q = slice(P * t, P * t + P)
                if kind == "diff":
                    last = nc.vector.tensor_copy(o_diff[:, h, q], core.banks[:, b + 3, 0:P])
                else:
                    r = slice(HEAD * (h % 2), HEAD * (h % 2) + HEAD)
                    last = nc.vector.tensor_copy(y_fox[r, h // 2, q], core.banks[r, b + 3, 0:P])
                last.then_inc(core.from_dve.sem, core.from_dve.up())
    core.settle()


def head_norm_stage(core, o, squares, rstd):
    nc = core.nc
    with nc.Block() as block:

        @block.tensor
        def _(pe):
            pe.wait_ge(core.from_dve.sem, core.from_dve.at(1))
            for h in range(DIFF_HEADS):
                last = nc.tensor.matmul(core.banks[:, h, 0:SEQ], core.const["ones"], squares[:, h, :], start=True, stop=True)
            last.then_inc(core.product.sem, core.product.up())

        @block.scalar
        def _(act):
            act.wait_ge(core.from_dve.sem, core.from_dve.at(2))
            nc.scalar.activation(rstd, rstd, ACT.Sqrt).then_inc(core.from_act.sem, core.from_act.up())

        @block.vector
        def _(dve):
            step = Steps(dve, core.dve_step)
            nc.vector.tensor_tensor(squares, o, o, ALU.mult).then_inc(core.from_dve.sem, core.from_dve.up())
            dve.wait_ge(core.product.sem, core.product.at(1))
            nc.vector.tensor_scalar(rstd, core.banks[:, 0:DIFF_HEADS, 0:SEQ], 1.0 / P, EPS, ALU.mult, ALU.add).then_inc(core.from_dve.sem, core.from_dve.up())
            dve.wait_ge(core.from_act.sem, core.from_act.at(1))
            step(nc.vector.reciprocal(rstd, rstd))
            step(nc.vector.tensor_scalar(o, o, core.v("diff_subln_g"), 1.0 - LAM_INIT, ALU.mult, ALU.mult))
            step(nc.vector.tensor_tensor(o, o, rstd, ALU.mult))
    core.settle()


def branch_stage(core, ys, gates, m, tmp):
    nc = core.nc
    groups = []
    for half in range(2):
        for br, (y, kt) in enumerate(ys):
            def evacuate(j, br=br, half=half):
                mt = 4 * half + j

                def run(step, ps):
                    g = gates[:, 8 * br + mt, :]
                    if br == 0:
                        return nc.vector.tensor_tensor(m[:, mt, :], ps, g, ALU.mult)
                    step(nc.vector.tensor_tensor(tmp, ps, g, ALU.mult))
                    return nc.vector.tensor_tensor(m[:, mt, :], m[:, mt, :], tmp, ALU.add)
                return run
            groups += weight_groups(core, 1, kt, lambda k, y=y: y[:, k, :], m.shape[2], lambda j: "dve", evacuate)
    product_stage(core, groups, "mixer0")


def residual_stage(core, moving, length, kt, n_chunks, x, scale, section, segments=None):
    nc = core.nc
    segments = segments or [(0, length)]

    def evacuate(m):
        def run(step, ps):
            last = None
            for i, (a, b) in enumerate(segments):
                if last is not None:
                    step(last)
                last = nc.vector.scalar_tensor_tensor(x[:, m, a:b], ps[:, a:b], scale(m, i), x[:, m, a:b], ALU.mult, ALU.add)
            return last
        return run
    product_stage(core, weight_groups(core, n_chunks, kt, moving, length, lambda m: "dve", evacuate), section)


def ffn_up_stage(core, h, a, gate, val):
    nc = core.nc

    def evacuate(m):
        c, j = divmod(m, 4)
        is_val, f = j // 2, 2 * c + j % 2
        tile = f + KF * is_val
        dst = (val if is_val else gate)[:, j % 2, :]

        def run(step, ps):
            step(nc.vector.tensor_scalar(dst, ps, core.v("ffn_conv_w", 2 * 2 * KF + tile), core.v("ffn_conv_b", tile),
                                         ALU.mult, ALU.add))
            for d in range(1, CONV_FFN):
                last = nc.vector.scalar_tensor_tensor(dst[:, d:], ps[:, 0:SEQ - d], core.v("ffn_conv_w", (2 - d) * 2 * KF + tile),
                                                      dst[:, d:], ALU.mult, ALU.add)
                if d < CONV_FFN - 1 or is_val:
                    step(last)
            if is_val:
                nc.vector.wait_ge(core.from_act.sem, core.from_act.at(f + 1))
                last = nc.vector.tensor_tensor(a[:, f, :], a[:, f, :], dst, ALU.mult)
            return last
        return run

    groups = weight_groups(core, KF // 2, KD, lambda k: h[:, k, :], SEQ, lambda m: "dve", evacuate)
    product_stage(core, groups, "mixer0", side=lambda act: gelu_work(core, act, gate, a))


def gelu_work(core, act, gate, a):
    for f in range(KF):
        c, j = divmod(f, 2)
        act.wait_ge(core.dve_read.sem, core.dve_read.at(4 * c + j + 1))
        core.nc.scalar.activation(a[:, f, :], gate[:, j, :], ACT.Gelu_apprx_tanh).then_inc(core.from_act.sem, core.from_act.up())


def first_block(core, x, rel_dram, stack0):
    with ExitStack() as s:
        h = core.sb(s, "h", [P, KD, SEQ])
        squares = core.sb(s, "squares", [P, KD, SEQ])
        rstd = core.sb(s, "rstd", [P, SEQ])
        y_rnn = core.sb(s, "y_rnn", [P, KD, SEQ])
        o_diff = core.sb(s, "o_diff", [P, 4, SEQ])
        y_fox = core.sb(s, "y_fox", [P, 4, SEQ])
        gates = core.sb(s, "gates", [P, 24, SEQ])
        seg = [(0, SEQ)]
        norm_stage(core, x, h[:, :, :], squares[:, :, :], rstd[:, :], seg, lambda k, i: core.v("norm1_g", k), None, "mixer0")
        with ExitStack() as t:
            out = {name: core.sb(t, name, [P, n, SEQ]) for name, n in
                   (("x_rnn", 8), ("g_rnn", 8), ("dq", 4), ("dk", 4), ("fq", 4), ("fk", 4))}
            out["dv"] = core.sb(t, "dv", [P, TT, 512])
            out["fv"] = core.sb(t, "fv", [P, TT, 512])
            flog = core.sb(t, "f_logit", [FOX_HEADS, SEQ])
            out["f_logit"] = flog[:, :]
            out["gates"] = gates
            projection_stage(core, h, out)
            with ExitStack() as u:
                rnn_stage(core, u, out, y_rnn)
            with ExitStack() as u:
                work = {"lam": core.sb(u, "lam", [P, 4]), "lam_products": core.sb(u, "lam_products", [P, 2]),
                        "f": core.sb(u, "forget", [FOX_HEADS, 6, SEQ]), "bias": core.sb(u, "bias", [P, DIFF_HEADS, SEQ]),
                        "scores": core.sb(u, "scores", [P, 2, SEQ]), "weights": core.sb(u, "attention", [P, SEQ]),
                        "weightsT": core.sb(u, "attentionT", [P, SEQ]), "stat": core.sb(u, "softmax_stat", [P, 6]),
                        "row_head": core.sb(u, "row_head", [FOX_HEADS, FOX_HEADS * SEQ])}
                buckets = core.sb(u, "buckets", [N_BUCKETS, 2 * SEQ - 1])
                rel = core.sb(u, "rel_bias", [N_BUCKETS, DIFF_HEADS])
                causal = core.sb(u, "causal", [P, P])
                core.const["causal"] = causal[:, :]
                small_load_stage(core, [(causal[:, :], core.dram["c_causal"]),
                                        (work["row_head"][:, :], core.dram["c_row_head"][0:FOX_HEADS, :]),
                                        (buckets[:, :], core.dram["c_buckets"][0:N_BUCKETS, :]),
                                        (rel[:, :], rel_dram)])
                with ExitStack() as w:
                    repeated = core.sb(w, "repeated_bias", [N_BUCKETS, DIFF_HEADS, P])
                    by_distance = core.sb(w, "bias_by_distance", [P, DIFF_HEADS, DISTANCES])
                    scratch = core.nc.dram_tensor("bias_scratch", [DIFF_HEADS, P * DISTANCES], F32, kind="Internal").ap()
                    attention_setup_stage(core, work, out, rel[:, :], buckets, repeated, by_distance, scratch)
                attention_stage(core, work, out, o_diff, y_fox)
                head_norm_stage(core, o_diff[:, :, :], squares[:, 0:4, :], squares[:, 4:8, :])
        m = core.sb(s, "mixed", [P, KD, SEQ])
        branch_stage(core, [(y_rnn, 8), (o_diff, 4), (y_fox, 4)], gates, m, rstd[:, :])
        residual_stage(core, lambda k: m[:, k, :], SEQ, KD, 2, x, lambda m_, i: 1.0, "mixer0")
        norm_stage(core, x, h[:, :, :], squares[:, :, :], rstd[:, :], seg, lambda k, i: core.v("norm2_g", k), None, "mixer0")
        a = core.sb(s, "ffn", [P, KF, SEQ])
        gate, val = core.sb(s, "ffn_gate", [P, 2, SEQ]), core.sb(s, "ffn_value", [P, 2, SEQ])
        ffn_up_stage(core, h, a, gate, val)
        residual_stage(core, lambda k: a[:, k, :], SEQ, KF, KD, x, lambda m_, i: 1.0, "mixer0")
        norm_stage(core, x, x, squares[:, :, :], rstd[:, :], seg, lambda k, i: core.v("final_g", k), None, "mixer0")


def small_load_stage(core, loads, wait=True):
    nc = core.nc
    with nc.Block() as block:

        @block.sync
        def _(sp):
            for dst, src in loads:
                sp.dma_start(dst, src).then_inc(core.landed.sem, core.landed.up(16))
            if wait:
                sp.wait_ge(core.landed.sem, core.landed.at(16 * len(loads)))
    core.settle()


def store_stage(core, dst, src):
    nc = core.nc
    with nc.Block() as block:

        @block.sync
        def _(sp):
            sp.dma_start(dst, src).then_inc(core.stored.sem, core.stored.up(16))
            sp.wait_ge(core.stored.sem, core.stored.at(16))
    core.settle()



def modulation_stage(core, layer, cc, mod, g1, g2):
    nc = core.nc
    section = f"mixer{layer}"
    with nc.Block() as block:

        @block.scalar
        def _(act):
            for i, name in enumerate(("c_ctx_2", "c_2")):
                nc.scalar.activation(cc[:, :, i], core.v(name, 0, 8), ACT.Silu).then_inc(core.act_step.sem, core.act_step.up())
    core.settle()

    with ExitStack() as s:
        row = core.sb(s, "modulation_rows", [2, 12, BANK])
        groups = []
        for n in range(12):
            c = core.next_chunk
            core.next_chunk += 1
            w = core.ring.chunk(c)
            groups.append(Group("dve", [(cc[:, k, :], w[:, k, :]) for k in range(KD)], copy_to(core, row[:, n, :]), 2, BANK,
                                chunks=(c,), frees=(c,)))
        product_stage(core, groups, section)
        features = core.banks[:, 0, 0:2 * 48].rearrange("p (m i) -> p m i", i=2)
        flat = row[:, :, :].rearrange("i n t -> i (n t)")
        with nc.Block() as block:

            @block.tensor
            def _(pe):
                for m in range(48):
                    last = nc.tensor.transpose(features[:, m, :], flat[:, P * m:P * m + P], core.const["ident"][0:2, 0:2])
                last.then_inc(core.product.sem, core.product.up())

            @block.vector
            def _(dve):
                step = Steps(dve, core.dve_step)
                dve.wait_ge(core.product.sem, core.product.at(1))
                step(nc.vector.tensor_tensor(mod[:, :, :], features, columns(core.v(("ada_b_2", layer), 0, 48), 2), ALU.add))
        core.settle()
    with nc.Block() as block:

        @block.vector
        def _(dve):
            step = Steps(dve, core.dve_step)
            for g, name, at in ((g1, "norm1_g_2", 8), (g2, "norm2_g_2", 32)):
                step(nc.vector.scalar_tensor_tensor(g[:, :, :], mod[:, at:at + 8, :], 1.0, columns(core.v((name, layer), 0, 8), 2),
                                                    ALU.add, ALU.mult))
    core.settle()



def rwkv_projection_stage(core, layer, h, z, zs, mu):
    nc = core.nc
    with nc.Block() as block:

        @block.vector
        def _(dve):
            step = Steps(dve, core.dve_step)
            key = ("shift_mu_2", layer)
            step(nc.vector.scalar_tensor_tensor(mu, core.v(key, 0, ZT), -1.0, core.v(key, ZT, ZT), ALU.mult, ALU.subtract))
            step(nc.vector.tensor_scalar(mu, mu, 1.0, None, ALU.add))
    core.settle()

    def evacuate(m):
        n = min(P, P_RWKV - P * m)
        dst = (z[0:n, m, :] if m < 24 else zs[0:n, m - 24, :]).rearrange("p (s t) -> p s t", s=2)

        def run(step, ps):
            src = ps.rearrange("p (s t) -> p s t", s=2)
            before, after = (core.v(("shift_mu_2", layer), m + ZT * j)[0:n] for j in range(2))
            step(nc.vector.tensor_scalar(dst, src, mu[0:n, m:m + 1], None, ALU.mult))
            step(nc.vector.scalar_tensor_tensor(dst[:, :, 1:], src[:, :, 0:SEQ - 1], before, dst[:, :, 1:], ALU.mult, ALU.add))
            return nc.vector.scalar_tensor_tensor(dst[:, :, 0:SEQ - 1], src[:, :, 1:], after, dst[:, :, 0:SEQ - 1],
                                                  ALU.mult, ALU.add)
        return run
    with ExitStack() as s:
        product_stage(core, weight_groups(core, 7, KD, lambda k: h[:, k, :], 2 * SEQ, lambda m: "dve", evacuate), f"mixer{layer}",
                      split=split_moving(core, s, h[:, :, :]))


def bank_tiles(core):
    return core.banks[:, 0:4, :].rearrange("p b (j t) -> p (b j) t", j=2)


def head_sums(core, pe, src):
    out = bank_tiles(core)
    for m in range(KD):
        last = core.nc.tensor.matmul(out[:, m, :], core.const["head_ones"], src[:, m, :], start=True, stop=True)
    return last


def compact_sums(core, pe, src):
    out, pattern = core.banks[0:RWKV_HEADS, 0, 0:SEQ], core.const["head_pattern"]
    for m in range(KD):
        sel = pattern[:, 14 - 2 * m:30 - 2 * m]
        last = core.nc.tensor.matmul(out, sel, src[:, m, :], start=m == 0, stop=m == KD - 1)
    return last


def spread_heads(core, pe, src, back):
    out = bank_tiles(core)
    for m in range(KD):
        last = core.nc.tensor.matmul(out[:, m, :], back[:, P * m:P * m + P], src, start=True, stop=True)
    return last


def key_direction_stage(core, layer, k, kk, tmp, back):
    nc = core.nc
    norm, compact = tmp[0:RWKV_HEADS, 0, :], core.banks[0:RWKV_HEADS, 0, 0:SEQ]
    with nc.Block() as block:

        @block.sync
        def _(sp):
            sp.dma_start(back, core.dram["c_head_back"][0:RWKV_HEADS, :]).then_inc(core.landed.sem, core.landed.up(16))

        @block.tensor
        def _(pe):
            pe.wait_ge(core.from_dve.sem, core.from_dve.at(1))
            compact_sums(core, pe, tmp).then_inc(core.product.sem, core.product.up())
            pe.wait_ge(core.from_dve.sem, core.from_dve.at(3))
            pe.wait_ge(core.landed.sem, core.landed.at(16))
            spread_heads(core, pe, norm, back).then_inc(core.product.sem, core.product.up())

        @block.scalar
        def _(act):
            act.wait_ge(core.from_dve.sem, core.from_dve.at(2))
            nc.scalar.activation(norm, norm, ACT.Sqrt).then_inc(core.from_act.sem, core.from_act.up())

        @block.vector
        def _(dve):
            step = Steps(dve, core.dve_step)
            for m in range(KD):
                last = nc.vector.tensor_scalar(kk[:, m, :], k[:, m, :], core.v(("k_k_2", layer), m), None, ALU.mult)
            step(last)
            nc.vector.tensor_tensor(tmp, kk, kk, ALU.mult).then_inc(core.from_dve.sem, core.from_dve.up())
            dve.wait_ge(core.product.sem, core.product.at(1))
            nc.vector.tensor_scalar(norm, compact, 1e-24, None, ALU.max).then_inc(core.from_dve.sem, core.from_dve.up())
            dve.wait_ge(core.from_act.sem, core.from_act.at(1))
            nc.vector.reciprocal(norm, norm).then_inc(core.from_dve.sem, core.from_dve.up())
            dve.wait_ge(core.product.sem, core.product.at(2))
            step(nc.vector.tensor_tensor(kk, bank_tiles(core), kk, ALU.mult))
    core.settle()


def scan_factors(alpha_rho):
    return alpha_rho.rearrange("p m c i t -> p (m c i t)")[:, 0:KD * SEQ]


def decay_stage(core, layer, d, t0, lora, tw, zs, a, ld, alpha_rho):
    nc = core.nc
    r = slice(HEAD * d, HEAD * d + HEAD)
    groups = []
    for which, (moving, dst, bias) in enumerate(((tw[r, t0:t0 + SEQ], ld, "w0_2"), (zs[r, 1, t0:t0 + SEQ], a, "a0_2"))):
        for m in range(KD):
            out = dst[:, m, ::-1] if d else dst[:, m, :]
            groups.append(Group("act", [(lora[r, which, P * m:P * m + P], moving)],
                                act_to(core, out, ACT.Sigmoid, core.v((bias, layer), KD * d + m)), P, SEQ))
    factors = scan_factors(alpha_rho)

    def fill(step):
        step(nc.vector.memset(factors, 1.0))
        step(nc.vector.memset(factors[:, 0::CHUNK], 0.0))
    product_stage(core, groups, f"mixer{layer}", vector_side=fill)


DECAY = math.exp(-0.5)


def factor_stage(core, layer, d, stream, a, ld, cum, e, alpha_rho, beta, kappa, bonus, last_decay, one_minus_ka):
    nc = core.nc
    r, k, kk = stream["r"], stream["k"], stream["kk"]
    alpha, rho = (alpha_rho[:, :, :, i, :] for i in range(2))
    flat = [x.rearrange("p m t -> p (m t)") for x in (cum[:, :, :], ld[:, :, :])]
    scratch = scan_factors(alpha_rho)

    def order(x):
        return x[:, :, ::-1] if d else x[:, :, :]

    def chunked(x):
        return x.rearrange("p m (c t) -> p m c t", t=CHUNK)

    with nc.Block() as block:

        @block.scalar
        def _(act):
            for m in range(KD):
                last = nc.scalar.activation(kappa[:, m, :], a[:, m, :], ACT.Identity, bias=one_minus_ka[:, m:m + 1],
                                            scale=core.v(("k_a_2", layer), m))
            last.then_inc(core.from_act.sem, core.from_act.up())
            act.wait_ge(core.from_dve.sem, core.from_dve.at(1))
            nc.scalar.activation(ld[:, :, :], ld[:, :, :], ACT.Exp, scale=-DECAY).then_inc(core.from_act.sem, core.from_act.up())
            act.wait_ge(core.from_dve.sem, core.from_dve.at(2))
            nc.scalar.activation(e[:, :, :], cum[:, :, :], ACT.Exp, scale=-DECAY).then_inc(core.from_act.sem, core.from_act.up())
            nc.scalar.activation(cum[:, :, :], cum[:, :, :], ACT.Exp, scale=DECAY).then_inc(core.from_act.sem, core.from_act.up())

        @block.vector
        def _(dve):
            step = Steps(dve, core.dve_step)
            step(nc.vector.tensor_tensor_scan(flat[0], scratch, flat[1], 0.0, ALU.mult, ALU.add))
            nc.vector.tensor_tensor(ld[:, :, :], cum[:, :, :], ld[:, :, :], ALU.subtract).then_inc(core.from_dve.sem, core.from_dve.up())
            dve.wait_ge(core.landed.sem, core.landed.at(0))
            dve.wait_ge(core.from_act.sem, core.from_act.at(1))
            step(nc.vector.tensor_tensor(kappa[:, :, :], kappa[:, :, :], order(k), ALU.mult))
            nc.vector.tensor_tensor(beta[:, :, :], a[:, :, :], order(kk), ALU.mult).then_inc(core.from_dve.sem, core.from_dve.up())
            if d == 0:
                step(nc.vector.tensor_tensor(bonus[:, :, :], kappa[:, :, :], r[:, :, :], ALU.mult))
            else:
                product = scratch.rearrange("p (m t) -> p m t", m=KD)
                step(nc.vector.tensor_tensor(product, kappa[:, :, :], order(r), ALU.mult))
                step(nc.vector.tensor_tensor(order(bonus), order(bonus), product, ALU.add))
            dve.wait_ge(core.from_act.sem, core.from_act.at(2))
            step(nc.vector.tensor_tensor(alpha, chunked(ld[:, :, :]), chunked(order(kk)), ALU.mult))
            dve.wait_ge(core.from_act.sem, core.from_act.at(3))
            step(nc.vector.tensor_tensor(rho, chunked(e[:, :, :]), chunked(order(r)), ALU.mult))
            step(nc.vector.tensor_copy(last_decay[:, :, :], e[:, :, CHUNK - 1::CHUNK]))
            dve.wait_ge(core.from_act.sem, core.from_act.at(4))
            dve.wait_ge(core.from_dve.sem, core.from_dve.at(2))
            step(nc.vector.tensor_tensor(kappa[:, :, :], kappa[:, :, :], cum[:, :, :], ALU.mult))
            step(nc.vector.tensor_tensor(beta[:, :, :], beta[:, :, :], cum[:, :, :], ALU.mult))
    core.settle()


def delta_order():
    levels = range(1, LEVELS)
    prepare = ["vrow", "brow", "N", "LakT", "krow"]
    for i in levels:
        prepare += [f"Y{i}", f"T{i}" if i < LEVELS - 1 else f"Z{i}"]
    order = []
    for pair in range(NCH // 2):
        order += [(2 * pair + j, name) for name in prepare for j in range(2)]
        order += [(2 * pair + j, name) for j in range(2) for name in ("B", "U", "S", "Y")]
    by_scalar = ("krow", "brow", "vrow", "B", "U") + tuple(f"Y{i}" for i in levels)
    place, rank, n = {}, {}, [0, 0]
    for i, entry in enumerate(order):
        e = 0 if entry[1] in by_scalar else 1
        n[e] += 1
        place[entry], rank[entry] = i, (e, n[e])
    return order, place, rank


def delta_needs(name, c):
    last = LEVELS - 1
    table = {"Y1": ["N"], "B": ["LakT", "vrow"],
             "U": ["B", f"Z{last}"], "S": ["krow", "brow", "U"], "Y": ["LakT", "N", "U"]}
    if name in table:
        needs = [(c, x) for x in table[name]]
        return needs + ([(c - 1, "S")] if c and name == "B" else [])
    if name[0] in "YTZ" and name[1:].isdigit():
        i = int(name[1:])
        return [(c, f"T{i - 1}") if name[0] == "Y" else (c, f"Y{i}")]
    return []


PLACES = (("v", "T"), ("kappa", "Y"), ("beta", "Z"), ("N", "alpha", "B"), ("LakT", "U"), ("krow",), ("brow",), ("vrow",))


def delta_stage(core, d, v, alpha_rho, beta, kappa, last_decay, state, next_state, y, sets):
    nc = core.nc
    order, place, rank = delta_order()
    read = (core.act_read, core.dve_read)
    ident, above, upto, masks = (core.const[k] for k in ("ident", "above_bd", "upto", "levels"))
    states = (state, next_state)
    slots = NBANK // 2

    def bank(entry):
        b = 2 * (place[entry] % slots)
        return core.banks[:, b:b + 2, :].rearrange("p b (m t) -> p (b m) t", t=P)

    def mask(i):
        return rows(masks[:, P * i:P * i + P], KD)

    with nc.Block() as block:

        @block.tensor
        def _(pe):
            for i, (c, name) in enumerate(order):
                w = sets[c % 2]
                if i >= slots:
                    e, k = rank[order[i - slots]]
                    pe.wait_ge(read[e].sem, read[e].at(k))
                for needed in delta_needs(name, c):
                    e, k = rank[needed]
                    if (name, needed[1]) != ("S", "U"):
                        pe.wait_ge(read[e].sem, read[e].at(k))
                level = int(name[1:]) if name[1:].isdigit() else 0
                if name[0] == "Y" and level:
                    pe.wait_ge(core.masked.sem, core.masked.at(2 * (LEVELS - 1) * (c // 2) + 2 * level - 1 + c % 2))
                elif level > 1:
                    pe.wait_ge(core.from_dve.sem, core.from_dve.at((LEVELS - 2) * (c // 2) + level - 1))
                if name in ("vrow", "brow", "LakT", "B"):
                    made = 4 * (c // 2) * 2 + {"vrow": 2, "LakT": 4, "brow": 5 + c % 2, "B": 7 + c % 2}[name]
                    pe.wait_ge(core.from_act.sem, core.from_act.at(made))
                out = bank((c, name))
                if name == "Y":
                    out, al_rh = out[:, :, 0:CHUNK], alpha_rho[:, :, c, 1, :]
                    pairs = [(states[c % 2], al_rh), (w["vrow"], w["MrkT"]), (w["U"], w["MrbT"])]
                elif name[0] == "Y":
                    pairs = [(w["N_level"], w["T"])]
                else:
                    both = alpha_rho[:, :, c, :, :].rearrange("p m i t -> p m (i t)")
                    eye = rows(ident, KD)
                    pairs = {"krow": [(w["kappa"], eye)], "vrow": [(w["v"], eye)], "LakT": [(w["kappa"], both)], "brow": [(w["beta"], eye)],
                             "N": [(w["beta"], both)], "T": [(w["Z"], w["Y"])], "Z": [(w["Y"], w["Z"])],
                             "B": [(w["alpha"], states[c % 2]), (w["LakT"], w["vrow"])], "U": [(w["Z"], w["B"])],
                             "S": []}[name.rstrip("12345")]
                if name == "S":
                    for m in range(KD):
                        nc.tensor.matmul(out[:, m, :], w["krow"][:, m, :], w["vrow"][:, m, :], start=m % 4 == 0, stop=False,
                                         skip_group_check=True)
                    e, k = rank[(c, "U")]
                    pe.wait_ge(read[e].sem, read[e].at(k))
                    for m in range(KD):
                        last = nc.tensor.matmul(out[:, m, :], w["brow"][:, m, :], w["U"][:, m, :], start=False, stop=m % 4 == 3,
                                                skip_group_check=True)
                    pairs = []
                for m in range(KD):
                    for n, (lhsT, rhs) in enumerate(pairs):
                        last = nc.tensor.matmul(out[:, m, :], lhsT[:, m, :], rhs[:, m, :], start=n == 0, stop=n == len(pairs) - 1)
                last.then_inc(core.product.sem, core.product.up())

        @block.scalar
        def _(act):
            def diagonal(c, name, src):
                for hh in range(2):
                    r = slice(HEAD * hh, HEAD * hh + HEAD)
                    last = nc.scalar.activation(sets[c % 2][name][r, :, CHUNK * hh:CHUNK * hh + CHUNK],
                                                src[r, :, CHUNK * c:CHUNK * c + CHUNK], ACT.Identity)
                last.then_inc(core.from_act.sem, core.from_act.up())

            def inputs(pair):
                for c in (2 * pair, 2 * pair + 1):
                    diagonal(c, "v", v[:, :, ::-1] if d else v)
                for c in (2 * pair, 2 * pair + 1):
                    diagonal(c, "kappa", kappa)

            inputs(0)
            for c in range(2):
                diagonal(c, "beta", beta)
            for c, name in order:
                if rank[(c, name)][0]:
                    continue
                if name == "B":
                    if c % 2 == 0:
                        for j in (c, c + 1):
                            act.wait_ge(core.product.sem, core.product.at(place[(j, f"Y{LEVELS - 1}")] + 1))
                            w = sets[j % 2]
                            for hh in range(2):
                                r = slice(HEAD * hh, HEAD * hh + HEAD)
                                last = nc.scalar.activation(w["alpha"][r, :, CHUNK * hh:CHUNK * hh + CHUNK], alpha_rho[r, :, j, 0, :],
                                                            ACT.Identity)
                            last.then_inc(core.from_act.sem, core.from_act.up())
                act.wait_ge(core.product.sem, core.product.at(place[(c, name)] + 1))
                scale = -1.0 if name == "brow" else 1.0
                nc.scalar.activation(sets[c % 2]["Y" if name[0] == "Y" else name], bank((c, name)), ACT.Identity, scale=scale
                                     ).then_inc(core.act_read.sem, core.act_read.up())
                if name == "U" and c % 2 == 0 and c + 2 < NCH:
                    act.wait_ge(core.product.sem, core.product.at(place[(c + 1, f"Z{LEVELS - 1}")] + 1))
                    inputs(c // 2 + 1)
                if name == "U" and c % 2 and c + 1 < NCH:
                    for j in (c + 1, c + 2):
                        diagonal(j, "beta", beta)

        @block.gpsimd
        def _(pool):
            for c, name in order:
                if name[0] == "Y" and name[1:]:
                    level = int(name[1:])
                    if level == 1:
                        pool.wait_ge(core.dve_read.sem, core.dve_read.at(rank[(c, "N")][1]))
                    else:
                        pool.wait_ge(core.product.sem, core.product.at(place[(c, f"Y{level - 1}")] + 1))
                    w = sets[c % 2]
                    nc.gpsimd.tensor_tensor(w["N_level"], w["N"], mask(level), ALU.mult
                                            ).then_inc(core.masked.sem, core.masked.up())

        @block.vector
        def _(dve):
            step = Steps(dve, core.dve_step)
            eye = rows(ident, KD)

            def flat(x):
                return x.rearrange("p m t -> p (m t)")

            for c, name in order:
                if not rank[(c, name)][0]:
                    continue
                w, ps = sets[c % 2], bank((c, name))
                dve.wait_ge(core.product.sem, core.product.at(place[(c, name)] + 1))
                if name in ("LakT", "N"):
                    twice = ps[:, :, 0:CHUNK].unsqueeze(2).broadcast_to([P, KD, 2, CHUNK])

                    def diagonal(x):
                        return x.rearrange("p m (h t) -> p m h t", h=2)

                    def masked(m):
                        return diagonal(rows(m, KD))
                    step(nc.vector.tensor_tensor(diagonal(w[name]), twice, masked(above), ALU.mult))
                    if name == "N":
                        step(nc.vector.scalar_tensor_tensor(w["Z"], w["N"], -1.0, mask(0), ALU.mult, ALU.mult))
                        step(nc.vector.tensor_tensor(w["Z"], w["Z"], eye, ALU.add))
                        step(nc.vector.transpose(flat(w["T"]), flat(w["Z"])))
                    key, sign = ("MrbT", -1.0) if name == "N" else ("MrkT", 1.0)
                    last = nc.vector.scalar_tensor_tensor(w[key], ps[:, :, CHUNK:], sign, rows(upto, KD), ALU.mult, ALU.mult)
                elif name == "Y":
                    t, ps = slice(CHUNK * c, CHUNK * c + CHUNK), ps[:, :, 0:CHUNK]
                    if d == 0:
                        last = nc.vector.tensor_copy(y[:, :, t], ps)
                    else:
                        yt = y[:, :, ::-1][:, :, t]
                        last = nc.vector.tensor_tensor(yt, ps, yt, ALU.add)
                elif name[0] in "TZ":
                    x = w[name[0]]
                    last = nc.vector.scalar_tensor_tensor(x, ps, -1.0, x, ALU.mult, ALU.add)
                elif name == "S":
                    old, new = states[c % 2], states[(c + 1) % 2]
                    step(nc.vector.tensor_tensor(new, ps, old, ALU.add))
                    last = nc.vector.tensor_tensor(new, new, last_decay[:, :, c:c + 1].broadcast_to([P, KD, P]), ALU.mult)
                last.then_inc(core.dve_read.sem, core.dve_read.up())
                dve.wait_ge(core.dve_read.sem, core.dve_read.now())
                if name[0] == "T" and c % 2:
                    for other in sets:
                        last = nc.vector.transpose(flat(other["Z"]), flat(other["T"]))
                    last.then_inc(core.from_dve.sem, core.from_dve.up())
                    dve.wait_ge(core.from_dve.sem, core.from_dve.now())
    core.settle()


def rwkv_output_stage(core, layer, t0, stream, y, bonus, tmp, g2w, sg, back):
    nc = core.nc
    v = stream["v"]
    sums = bank_tiles(core)
    rstd, compact = tmp[0:RWKV_HEADS, 0, :], core.banks[0:RWKV_HEADS, 0, 0:SEQ]
    gate = core.banks[:, 4:8, :].rearrange("p b (j t) -> p (b j) t", j=2)
    with nc.Block() as block:

        @block.sync
        def _(sp):
            sp.dma_start(back, core.dram["c_head_back"][0:RWKV_HEADS, :]).then_inc(core.landed.sem, core.landed.up(16))

        @block.tensor
        def _(pe):
            head_sums(core, pe, y).then_inc(core.product.sem, core.product.up())
            for m in range(KD):
                nc.tensor.matmul(gate[:, m, :], g2w[:, 0, P * m:P * m + P], sg[:, 0, t0:t0 + SEQ], start=True, stop=False)
                n = LORA_G - P
                last = nc.tensor.matmul(gate[:, m, :], g2w[0:n, 1, P * m:P * m + P], sg[0:n, 1, t0:t0 + SEQ], start=False, stop=True)
            last.then_inc(core.product.sem, core.product.up())
            pe.wait_ge(core.from_dve.sem, core.from_dve.at(1))
            compact_sums(core, pe, tmp).then_inc(core.product.sem, core.product.up())
            pe.wait_ge(core.from_dve.sem, core.from_dve.at(3))
            pe.wait_ge(core.landed.sem, core.landed.at(16))
            spread_heads(core, pe, rstd, back).then_inc(core.product.sem, core.product.up())
            pe.wait_ge(core.from_dve.sem, core.from_dve.at(4))
            head_sums(core, pe, bonus).then_inc(core.product.sem, core.product.up())

        @block.scalar
        def _(act):
            act.wait_ge(core.from_dve.sem, core.from_dve.at(2))
            nc.scalar.activation(rstd, rstd, ACT.Sqrt).then_inc(core.from_act.sem, core.from_act.up())

        @block.vector
        def _(dve):
            step = Steps(dve, core.dve_step)
            dve.wait_ge(core.product.sem, core.product.at(1))
            step(nc.vector.scalar_tensor_tensor(y, sums, -1.0 / HEAD, y, ALU.mult, ALU.add))
            nc.vector.tensor_tensor(tmp, y, y, ALU.mult).then_inc(core.from_dve.sem, core.from_dve.up())
            for m in range(KD):
                last = nc.vector.tensor_scalar(bonus[:, m, :], bonus[:, m, :], core.v(("r_k_2", layer), m), None, ALU.mult)
            step(last)
            dve.wait_ge(core.product.sem, core.product.at(3))
            nc.vector.tensor_scalar(rstd, compact, 1.0 / HEAD, GN_EPS, ALU.mult, ALU.add).then_inc(core.from_dve.sem, core.from_dve.up())
            dve.wait_ge(core.from_act.sem, core.from_act.at(1))
            nc.vector.reciprocal(rstd, rstd).then_inc(core.from_dve.sem, core.from_dve.up())
            dve.wait_ge(core.product.sem, core.product.at(4))
            nc.vector.tensor_tensor(y, sums, y, ALU.mult).then_inc(core.from_dve.sem, core.from_dve.up())
            dve.wait_ge(core.from_dve.sem, core.from_dve.at(4))
            for m in range(KD):
                last = nc.vector.tensor_scalar(y[:, m, :], y[:, m, :], core.v(("lnx_g_2", layer), m), core.v(("lnx_b_2", layer), m),
                                               ALU.mult, ALU.add)
            step(last)
            dve.wait_ge(core.product.sem, core.product.at(5))
            step(nc.vector.tensor_tensor(tmp, sums, v[:, :, :], ALU.mult))
            step(nc.vector.tensor_tensor(y, y, tmp, ALU.add))
            dve.wait_ge(core.product.sem, core.product.at(2))
            step(nc.vector.tensor_tensor(y, gate, y, ALU.mult))
    core.settle()


def rwkv_branch(core, layer, x, mod, g1, z_dram, y_dram, emits):
    nc = core.nc
    section = f"mixer{layer}"
    with ExitStack() as s:
        zs = core.sb(s, "z_small", [P, 4, 2 * SEQ])
        with ExitStack() as t:
            h = core.sb(t, "h", [P, KD, 2 * SEQ])
            rstd = core.sb(t, "rstd", [P, 2 * SEQ])
            z = core.sb(t, "z", [P, 24, 2 * SEQ])
            mu = core.sb(t, "mu", [P, ZT])
            norm_stage(core, x, h[:, :, :], z[:, 0:KD, :], rstd[:, :], [(0, SEQ), (SEQ, 2 * SEQ)],
                       lambda k, i: g1[:, k, i:i + 1], lambda k, i: mod[:, k, i:i + 1], section)
            rwkv_projection_stage(core, layer, h, z, zs, mu[:, :])
            store_stage(core, z_dram, z[:, :, :])
        lora_chunk, g2_chunk = core.next_chunk, core.next_chunk + 1
        core.next_chunk += 2
        lora, g2w = core.ring.chunk(lora_chunk), core.ring.chunk(g2_chunk)
        tw = core.sb(s, "tanh_w", [P, 2 * SEQ])
        st = {k: core.sb(s, f"stream_{k}", [P, KD, SEQ]) for k in ("r", "k", "v", "kk")}
        a, ld, cum, beta, kappa = (core.sb(s, n, [P, KD, SEQ]) for n in ("rate", "log_decay", "cumulated", "beta", "kappa"))
        alpha_rho = core.sb(s, "alpha_rho", [P, KD, NCH, 2, CHUNK])[:, :, :, :, :]
        y, bonus = core.sb(s, "y", [P, KD, SEQ]), core.sb(s, "bonus", [P, KD, SEQ])
        last_decay, omk = core.sb(s, "last_decay", [P, KD, NCH]), core.sb(s, "one_minus_ka", [P, KD])
        masks = {name: core.sb(s, name, [P, n])[:, :] for name, n in (("levels", LEVELS * P), ("above_bd", P), ("upto", CHUNK), ("head_pattern", 30))}
        core.const.update(masks)
        small_load_stage(core, [(ap, core.dram["c_" + name]) for name, ap in masks.items()], False)
        states = [core.sb(s, f"state_{d}", [P, KD, P])[:, :, :] for d in range(2)]
        next_state = core.sb(s, "next_state", [P, KD, P])[:, :, :]
        pool = core.sb(s, "chunk_pool", [P, 4, KD * P])
        kept = [pool[:, i, :] for i in range(4)] + [slot[:, KD * P * i:KD * P * (i + 1)] for slot in core.ring.slots for i in (2, 3)]
        lent = [x[:, :, :].rearrange("p m t -> p (m t)")[:, KD * P * i:KD * P * (i + 1)]
                for x in (a, ld, cum, st["r"], st["k"]) for i in range(2)]
        sets = [{}, {}]
        for i, w in enumerate(sets):
            for j, names in enumerate(PLACES):
                at = kept[4 * i + j] if j < 4 else lent[5 * i + j - 4]
                w.update({name: at.rearrange("p (m t) -> p m t", m=KD) for name in names})
            w["N_level"] = core.sb(s, f"N_level_{i}", [P, KD, P])[:, :, :]
            w["MrkT"], w["MrbT"] = (lent[5 * i + 4][:, KD * CHUNK * n:KD * CHUNK * (n + 1)].rearrange("p (m t) -> p m t", m=KD)
                                    for n in range(2))
        with nc.Block() as block:

            @block.sync
            def _(sp):
                core.ring.load(sp, section)

            @block.scalar
            def _(act):
                nc.scalar.activation(tw[:, :], zs[:, 0, :], ACT.Tanh).then_inc(core.act_step.sem, core.act_step.up())
                nc.scalar.activation(zs[:, 2, :], zs[:, 2, :], ACT.Sigmoid).then_inc(core.act_step.sem, core.act_step.up())
                n = LORA_G - P
                nc.scalar.activation(zs[0:n, 3, :], zs[0:n, 3, :], ACT.Sigmoid).then_inc(core.act_step.sem, core.act_step.up())

            @block.vector
            def _(dve):
                step = Steps(dve, core.dve_step)
                for w in sets:
                    for names in PLACES[0:4]:
                        step(nc.vector.memset(w[names[0]], 0.0))
                for state in states:
                    step(nc.vector.memset(state, 0.0))
                step(nc.vector.tensor_scalar(omk[:, :], core.v(("k_a_2", layer), 0, 8), -1.0, 1.0, ALU.mult, ALU.add))

            @block.tensor
            def _(pe):
                pe.wait_ge(core.ring.loaded[lora_chunk % RING], core.ring.at(lora_chunk))
                pe.wait_ge(core.ring.loaded[g2_chunk % RING], core.ring.at(g2_chunk))
        core.settle()
        head_back = ld[0:RWKV_HEADS, :, :].rearrange("p m t -> p (m t)")[:, 0:D]
        for seq in range(2):
            t0 = SEQ * seq
            small_load_stage(core, [(st[n][:, :, :], z_dram[:, KD * i:KD * i + KD, t0:t0 + SEQ]) for i, n in enumerate("rkv")
                                    if seq == 0 or n == "v"])
            key_direction_stage(core, layer, st["k"], st["kk"][:, :, :], cum[:, :, :], head_back)
            for d in range(2):
                if d:
                    small_load_stage(core, [(st[n][:, :, :], z_dram[:, KD * i:KD * i + KD, t0:t0 + SEQ]) for i, n in enumerate("rk")], False)
                decay_stage(core, layer, d, t0, lora, tw, zs, a, ld, alpha_rho)
                factor_stage(core, layer, d, st, a, ld, cum, a, alpha_rho, beta, kappa, bonus, last_decay, omk)
                delta_stage(core, d, st["v"], alpha_rho, beta, kappa, last_decay, states[d], next_state, y, sets)
            if seq == 0:
                small_load_stage(core, [(st[n][:, :, :], z_dram[:, KD * i:KD * i + KD, SEQ:]) for i, n in enumerate("rk")], False)
            if seq in emits:
                rwkv_output_stage(core, layer, t0, st, y[:, :, :], bonus[:, :, :], cum[:, :, :], g2w, zs[:, 2:4, :], head_back)
                store_stage(core, y_dram[:, :, t0:t0 + SEQ], y[:, :, :])
        core.ring.release(lora_chunk, (core.product, core.product.base))
        core.ring.release(g2_chunk, (core.product, core.product.base))



def glu_stage(core, layer, h, u, sg, length):
    def moving(k):
        return h[:, k, :]

    def reader(m):
        return "act" if m % 4 >= 2 else "dve"

    def evacuate(m):
        c, j = divmod(m, 4)
        if j < 2:
            return copy_to(core, u[:, 2 * c + j, :])
        return act_to(core, sg[:, 2 * c + j - 2, :], ACT.Sigmoid)
    with ExitStack() as s:
        product_stage(core, weight_groups(core, 4, KD, moving, length, reader, evacuate), f"mixer{layer}",
                      split=split_moving(core, s, h[:, :, :]))


def gates_and_conv_stage(core, layer, h, u, sg, out, gates, sequences):
    nc = core.nc
    half = CONV_K // 2
    length = h.shape[2]

    def conv(step):
        step(nc.vector.tensor_tensor(u, u, sg, ALU.mult))
        for m in range(KD):
            for t0, row in sequences:
                def tap(k):
                    return core.v(("conv_w_2", layer), KD * k + m)
                src, dst = u[:, m, t0:t0 + SEQ], out[:, m, t0:t0 + SEQ]
                step(nc.vector.tensor_scalar(dst, src, tap(half), None, ALU.mult))
                for k in range(CONV_K):
                    off = (k - half) * row
                    if k == half or abs(off) >= SEQ:
                        continue
                    a, b = max(0, -off), SEQ - max(0, off)
                    step(nc.vector.scalar_tensor_tensor(dst[:, a:b], src[:, a + off:b + off], tap(k), dst[:, a:b],
                                                        ALU.mult, ALU.add))

    g = weight_groups(core, 4, KD, lambda k: h[:, k, :], length, lambda m: "act",
                      lambda m: act_to(core, gates[:, m, :], ACT.Sigmoid, core.v(("gate_b_2", layer), m)))
    product_stage(core, g, f"mixer{layer}", vector_side=conv)


def layer_norm_stage(core, layer, x, tmp, rstd, length):
    nc = core.nc
    with nc.Block() as block:

        @block.tensor
        def _(pe):
            for n, src in enumerate((x, tmp)):
                if n:
                    pe.wait_ge(core.from_dve.sem, core.from_dve.at(1))
                for k in range(KD):
                    last = nc.tensor.matmul(core.banks[:, n, 0:length], core.const["ones"], src[:, k, :], start=k == 0, stop=k == KD - 1)
                last.then_inc(core.product.sem, core.product.up())

        @block.scalar
        def _(act):
            act.wait_ge(core.from_dve.sem, core.from_dve.at(2))
            nc.scalar.activation(rstd, rstd, ACT.Sqrt).then_inc(core.from_act.sem, core.from_act.up())
            for m in range(KD):
                act.wait_ge(core.from_dve.sem, core.from_dve.at(3 + m))
                nc.scalar.activation(x[:, m, :], x[:, m, :], ACT.Silu).then_inc(core.act_step.sem, core.act_step.up())

        @block.vector
        def _(dve):
            step = Steps(dve, core.dve_step)
            dve.wait_ge(core.product.sem, core.product.at(1))
            step(nc.vector.tensor_scalar(rstd, core.banks[:, 0, 0:length], -1.0 / D, None, ALU.mult))
            step(nc.vector.tensor_tensor(x, x, rows(rstd, KD), ALU.add))
            nc.vector.tensor_tensor(tmp, x, x, ALU.mult).then_inc(core.from_dve.sem, core.from_dve.up())
            dve.wait_ge(core.product.sem, core.product.at(2))
            nc.vector.tensor_scalar(rstd, core.banks[:, 1, 0:length], 1.0 / D, LN_EPS, ALU.mult, ALU.add).then_inc(core.from_dve.sem, core.from_dve.up())
            dve.wait_ge(core.from_act.sem, core.from_act.at(1))
            step(nc.vector.reciprocal(rstd, rstd))
            step(nc.vector.tensor_tensor(x, x, rows(rstd, KD), ALU.mult))
            for m in range(KD):
                nc.vector.tensor_scalar(x[:, m, :], x[:, m, :], core.v(("cnorm_g_2", layer), m),
                                                          core.v(("cnorm_b_2", layer), m), ALU.mult, ALU.add).then_inc(core.from_dve.sem, core.from_dve.up())
    core.settle()


def mix_stage(core, layer, ya, yb, gates, m, tmp, length):
    nc = core.nc
    groups = []
    for br, y in enumerate((ya, yb)):
        def evacuate(mt, br=br):
            def run(step, ps):
                g = gates[:, KD * br + mt, :]
                if br == 0:
                    return nc.vector.tensor_tensor(m[:, mt, :], ps, g, ALU.mult)
                step(nc.vector.tensor_tensor(tmp, ps, g, ALU.mult))
                return nc.vector.tensor_tensor(m[:, mt, :], m[:, mt, :], tmp, ALU.add)
            return run
        groups += weight_groups(core, 2, KD, lambda k, y=y: y[:, k, :], length, lambda j: "dve", evacuate)
    product_stage(core, groups, f"mixer{layer}")


def mixer(core, layer, x, mod, g1, z_dram, y_dram):
    last_layer = layer == LAYERS - 1
    section = f"mixer{layer}"
    rwkv_branch(core, layer, x, mod, g1, z_dram, y_dram, (1,) if last_layer else (0, 1))
    t0, length = (SEQ, SEQ) if last_layer else (0, 2 * SEQ)
    segs = [(0, SEQ)] if last_layer else [(0, SEQ), (SEQ, 2 * SEQ)]
    first = 1 if last_layer else 0
    xs = x[:, :, t0:t0 + length]
    with ExitStack() as s:
        h, u = core.sb(s, "h", [P, KD, length]), core.sb(s, "u", [P, KD, length])
        rstd, gates = core.sb(s, "rstd", [P, length]), core.sb(s, "gates", [P, 2 * KD, length])
        sg = core.sb(s, "sg", [P, KD, length])
        norm_stage(core, xs, h[:, :, :], u[:, :, :], rstd[:, :], segs, lambda k, i: g1[:, k, first + i:first + i + 1],
                   lambda k, i: mod[:, k, first + i:first + i + 1], section)
        glu_stage(core, layer, h, u, sg, length)
        yb = sg
        sequences = [(0, GRID_W)] if last_layer else [(0, 1), (SEQ, GRID_W)]
        gates_and_conv_stage(core, layer, h, u[:, :, :], sg[:, :, :], yb, gates, sequences)
        layer_norm_stage(core, layer, yb[:, :, :], u[:, :, :], rstd[:, :], length)
        small_load_stage(core, [(u[:, :, :], y_dram[:, :, t0:t0 + length])])
        mixed = h
        mix_stage(core, layer, u, yb, gates, mixed, rstd[:, :], length)
        residual_stage(core, lambda k: mixed[:, k, :], length, KD, 2, xs,
                       lambda m, i: mod[:, 2 * KD + m, first + i:first + i + 1], section, segs)



def peer_query_stage(core, layer, h, q, length):
    with ExitStack() as s:
        product_stage(core, weight_groups(core, 4, KD, lambda k: h[:, k, :], length, lambda m: "dve",
                                          lambda m: copy_to(core, q[:, m, :])), f"peer{layer}", split=split_moving(core, s, h))


def route_stage(core, layer, q, n_tiles, keys_chunk, w, routeT):
    nc = core.nc
    keys = core.ring.chunk(keys_chunk)
    H, K, N = PEER_HEADS, TOPK, 2 * PEER_HEADS
    s, rest, top, num, cand, crest, best, pos = (w[k] for k in ("scores", "rest", "top", "numbers", "candidates",
                                                                "candidate_rest", "best", "position"))
    eq, ab, gw, stat, numf = (w[k] for k in ("equal", "halves", "weights", "stat", "numbers_f"))
    iota16 = core.const["iota16"]

    with nc.Block() as block:

        @block.tensor
        def _(pe):
            pe.wait_ge(core.ring.loaded[keys_chunk % RING], core.ring.at(keys_chunk))
            def scores(t):
                for n in range(N):
                    last = nc.tensor.matmul(core.banks[:, n // 4, P * (n % 4):P * (n % 4) + P], q[:, n, P * t:P * t + P],
                                            keys[:, n, :], start=True, stop=True)
                last.then_inc(core.product.sem, core.product.up())
                return core.product.now()

            read_keys = scores(0)
            for t in range(n_tiles):
                if t + 1 < n_tiles:
                    pe.wait_ge(core.from_dve.sem, core.from_dve.at(2 * t + 1))
                    read_keys = scores(t + 1)
                pe.wait_ge(core.from_dve.sem, core.from_dve.at(2 * t + 2))
                for i in range(3):
                    back = nc.tensor.transpose(core.banks[:, 4, P * i:P * i + P], gw[:, i, :], core.const["ident"])
                back.then_inc(core.product.sem, core.product.up())
            core.ring.release(keys_chunk, (core.product, read_keys))

        @block.scalar
        def _(act):
            for t in range(n_tiles):
                act.wait_ge(core.vector_max.sem, core.vector_max.at(t + 1))
                nc.scalar.activation(best[:, :, :], best[:, :, :], ACT.Exp).then_inc(core.from_act.sem, core.from_act.up())

        @block.vector
        def _(dve):
            step = Steps(dve, core.dve_step)

            def top16(lists):
                for i in range(2):
                    for values, scratch, out, numbers in lists:
                        last = nc.vector.max(out[:, 8 * i:8 * i + 8], scratch if i else values)
                    step(last)
                    for values, scratch, out, numbers in lists:
                        last = nc.vector.max_index(numbers[:, 8 * i:8 * i + 8], out[:, 8 * i:8 * i + 8], scratch if i else values)
                        if not i:
                            last = nc.vector.match_replace(scratch, out[:, 0:8], values, NEG)
                    step(last)

            for t in range(n_tiles):
                dve.wait_ge(core.product.sem, core.product.at(max(1, 2 * t)))
                nc.vector.tensor_copy(s[:, :, :], core.banks[:, 0:4, :].rearrange("p b (n k) -> p (b n) k", k=NKEYS)).then_inc(core.from_dve.sem, core.from_dve.up())
                dve.wait_ge(core.from_dve.sem, core.from_dve.at(2 * t + 1))
                top16([(s[:, n, :], rest[:, n, :], top[:, n, :], num[:, n, :]) for n in range(N)])
                step(nc.vector.tensor_copy(numf[:, :, :], num[:, :, :]))
                for h in range(H):
                    last = nc.vector.tensor_tensor(cand[:, h, :].rearrange("p (a b) -> p a b", a=K), columns(top[:, 2 * h, :], K),
                                                   rows(top[:, 2 * h + 1, :], K), ALU.add)
                step(last)
                top16([(cand[:, h, :], crest[:, h, :], best[:, h, :], pos[:, h, :]) for h in range(H)])
                step(nc.vector.tensor_copy(stat[:, 0:H], best[:, :, 0]))
                nc.vector.tensor_tensor(best[:, :, :], best[:, :, :], columns(stat[:, 0:H], K), ALU.subtract).then_inc(core.vector_max.sem, core.vector_max.up())
                step(nc.vector.tensor_scalar(pos[:, H:2 * H, :], pos[:, 0:H, :], 4, None, ALU.logical_shift_right))
                step(nc.vector.tensor_scalar(pos[:, 0:H, :], pos[:, 0:H, :], TOPK - 1, None, ALU.bitwise_and))
                step(nc.vector.tensor_copy(ab[:, :, :], pos[:, :, :]))
                for side in range(2):
                    place = ab[:, H * (1 - side):H * (1 - side) + H, :].unsqueeze(3).broadcast_to([P, H, K, K])
                    ranks = iota16.unsqueeze(1).unsqueeze(1).broadcast_to([P, H, K, K])
                    step(nc.vector.tensor_tensor(eq[:, :, :, :], place, ranks, ALU.is_equal))
                    number = numf[:, side::2, :].unsqueeze(2).broadcast_to([P, H, K, K])
                    step(nc.vector.tensor_tensor(eq[:, :, :, :], eq[:, :, :, :], number, ALU.mult))
                    step(nc.vector.tensor_reduce(gw[:, 1 + side, :].rearrange("p (h k) -> p h k", h=H), eq[:, :, :, :], AX.X, ALU.add))
                dve.wait_ge(core.from_act.sem, core.from_act.at(t + 1))
                step(nc.vector.tensor_reduce(stat[:, H:2 * H], best[:, :, :], AX.X, ALU.add))
                step(nc.vector.reciprocal(stat[:, H:2 * H], stat[:, H:2 * H]))
                nc.vector.tensor_tensor(gw[:, 0, :].rearrange("p (h k) -> p h k", h=H), best[:, :, :],
                                                          columns(stat[:, H:2 * H], K), ALU.mult).then_inc(core.from_dve.sem, core.from_dve.up())
                dve.wait_ge(core.product.sem, core.product.at(2 * t + (3 if t + 1 < n_tiles else 2)))
                step(nc.vector.tensor_copy(routeT[:, :, P * t:P * t + P],
                                           core.banks[:, 4, 0:3 * P].rearrange("p (i t) -> p i t", i=3)))
    core.settle()


SPREAD = 8


def spread_stage(core, t0, routeT, pick, weight, g):
    nc = core.nc
    iota = core.const["iota"]
    turns = SEQ // SPREAD
    hot, prod, taken = core.from_dve, core.product, core.act_read

    with nc.Block() as block:

        @block.vector
        def _(dve):
            with dve.Fori(0, turns) as i:
                for b in range(SPREAD):
                    dve.wait_ge(prod.sem, i * 2 + (prod.base + b // 4 - 1))
                    t = i * SPREAD + (t0 + b)
                    if b % 4 == 0:
                        four = routeT[:, 1, bass.ds(t, 4)]
                        nc.vector.tensor_tensor(pick[:, b:b + 4, :], rows(iota, 4), columns(four, P), ALU.is_equal)
                    nc.vector.tensor_scalar(weight[:, b, :], iota, routeT[:, 2, bass.ds(t, 1)], routeT[:, 0, bass.ds(t, 1)],
                                            ALU.is_equal, ALU.mult).then_inc(hot.sem, 1)

        @block.tensor
        def _(pe):
            with pe.Fori(0, turns) as i:
                for half in range(2):
                    pe.wait_ge(taken.sem, i * 2 + (taken.base + half - 1))
                    for b in range(4):
                        pe.wait_ge(hot.sem, i * SPREAD + (hot.base + 4 * half + b + 1))
                        last = nc.tensor.matmul(core.banks[:, half, P * b:P * b + P], pick[:, 4 * half + b, :],
                                                weight[:, 4 * half + b, :], start=True, stop=True)
                    last.then_inc(prod.sem, 1)

        @block.scalar
        def _(act):
            with act.Fori(0, turns) as i:
                for half in range(2):
                    act.wait_ge(prod.sem, i * 2 + (prod.base + half + 1))
                    dst = g[:, :, bass.ds(i * SPREAD + 4 * half, 4)]
                    nc.scalar.activation(dst, core.banks[:, half, :].rearrange("p (t j) -> p j t", t=4),
                                         ACT.Identity).then_inc(taken.sem, 1)
    hot.pending += SPREAD * turns
    prod.pending += 2 * turns
    taken.pending += 2 * turns
    core.settle()


SLOTS = 4


def experts_stage(core, layer, h, x, x_dram, g, raw, parts, acts, gain, experts):
    nc = core.nc
    turns = 2 * NKEYS // SLOTS
    used, gelus, high_ready, low_ready, gated, own = (core.product, core.act_read, core.high_ready, core.low_ready, core.from_dve,
                                                      core.dve_step)
    loaded = core.experts_loaded
    (h_high, h_low), (high, low), (act_raw, act_high, act_low) = h, parts, acts

    def half_tile(i, b):
        if b == 0:
            return (True, 0) if isinstance(i, int) and i == 0 else (False, i * 2 - 1)
        if b == 1:
            return True, i * 2 + 1
        if b == 2:
            return False, i * 2
        return (False, NKEYS - 1) if isinstance(i, int) and i == turns - 1 else (True, i * 2 + 2)

    def one(j):
        return slice(j, j + 1) if isinstance(j, int) else bass.ds(j, 1)

    with nc.Block() as block:

        @block.sync
        def _(sp):
            def load(i, b):
                is_u, j = half_tile(i, b)
                src = experts[layer, one(j), :, 0:D] if is_u else experts[layer, one(j), :, D:]
                sp.dma_start(raw[:, b, :], src.rearrange("o p n -> p (o n)")).then_inc(loaded[b].sem, 16)

            for b in range(SLOTS):
                load(0, b)
            with sp.Fori(1, turns - 1) as i:
                for b in range(SLOTS):
                    sp.wait_ge(low_ready.sem, i * SLOTS + (low_ready.base + b - SLOTS + 1))
                    load(i, b)
            for b in range(SLOTS):
                sp.wait_ge(low_ready.sem, low_ready.base + SLOTS * (turns - 2) + b + 1)
                load(turns - 1, b)
            sp.wait_ge(low_ready.sem, low_ready.base + 2 * NKEYS)
            sp.dma_start(x, x_dram).then_inc(core.landed.sem, core.landed.up(16))

        @block.tensor
        def _(pe):
            def scores(i, b, j, first):
                pe.wait_ge(low_ready.sem, i * SLOTS + (low_ready.base + b + 1))
                if not first:
                    pe.wait_ge(gelus.sem, j + (gelus.base - 1))
                bank = core.banks[:, 4 if b in (0, 3) else 5, 0:SEQ]
                for k in range(KD):
                    uh, ul = (x_[:, b, P * k:P * k + P] for x_ in (high, low))
                    nc.tensor.matmul(bank, uh, h_high[:, k, :], start=k == 0, stop=False)
                    nc.tensor.matmul(bank, uh, h_low[:, k, :], start=False, stop=False)
                    last = nc.tensor.matmul(bank, ul, h_high[:, k, :], start=False, stop=k == KD - 1)
                last.then_inc(used.sem, 1)

            def outputs(i, b, j, n, start, stop):
                pe.wait_ge(low_ready.sem, i * SLOTS + (low_ready.base + b + 1))
                pe.wait_ge(gated.sem, j + (gated.base + 1))
                for m in range(KD):
                    out = core.banks[:, m // 2, SEQ * (m % 2):SEQ * (m % 2) + SEQ]
                    vh, vl = (x_[:, b, P * m:P * m + P] for x_ in (high, low))
                    nc.tensor.matmul(out, vh, act_high[:, n, :], start=start and m % 2 == 0, stop=False, skip_group_check=True)
                    nc.tensor.matmul(out, vh, act_low[:, n, :], start=False, stop=False, skip_group_check=True)
                    last = nc.tensor.matmul(out, vl, act_high[:, n, :], start=False, stop=stop, skip_group_check=True)
                last.then_inc(used.sem, 1)

            def turn(i):
                fixed = isinstance(i, int)
                for b in range(SLOTS):
                    is_u, j = half_tile(i, b)
                    if is_u:
                        scores(i, b, j, fixed and j < 2)
                    else:
                        outputs(i, b, j, 1 if b in (0, 3) else 0, fixed and j == 0, fixed and j == NKEYS - 1)

            turn(0)
            with pe.Fori(1, turns - 1) as i:
                turn(i)
            turn(turns - 1)

        @block.scalar
        def _(act):
            def high_part(i, b, first):
                act.wait_ge(loaded[b].sem, i * 16 + (loaded[b].base + 16))
                if not first:
                    act.wait_ge(used.sem, i * SLOTS + (used.base + b - SLOTS + 1))
                nc.scalar.activation(high[:, b, :], raw[:, b, :], ACT.Identity).then_inc(high_ready.sem, 1)

            def turn(i, last):
                for b in range(SLOTS):
                    is_u, j = half_tile(i, b)
                    if is_u:
                        act.wait_ge(used.sem, i * SLOTS + (used.base + b + 1))
                        if not (isinstance(j, int) and j == 0):
                            act.wait_ge(gated.sem, j + gated.base)
                        nc.scalar.activation(act_raw, core.banks[:, 4 if b in (0, 3) else 5, 0:SEQ], ACT.Gelu
                                             ).then_inc(gelus.sem, 1)
                    if not last:
                        high_part(i + 1, b, False)

            for b in range(SLOTS):
                high_part(0, b, True)
            turn(0, False)
            with act.Fori(1, turns - 1) as i:
                turn(i, False)
            turn(turns - 1, True)

        @block.vector
        def _(dve):
            def low_part(i, b):
                dve.wait_ge(high_ready.sem, i * SLOTS + (high_ready.base + b + 1))
                nc.vector.tensor_tensor(low[:, b, :], raw[:, b, :], high[:, b, :].bitcast(F32), ALU.subtract
                                        ).then_inc(low_ready.sem, 1)

            def turn(i, last):
                for b in range(SLOTS):
                    is_u, j = half_tile(i, b)
                    if is_u:
                        n = 0 if b in (0, 3) else 1
                        dve.wait_ge(gelus.sem, j + (gelus.base + 1))
                        gj = g[:, one(j), :].rearrange("p o t -> p (o t)")
                        nc.vector.tensor_tensor(act_high[:, n, :], act_raw, gj, ALU.mult).then_inc(own.sem, 1)
                        dve.wait_ge(own.sem, j * 2 + (own.base + 1))
                        nc.vector.tensor_tensor(act_raw, act_raw, gj, ALU.mult).then_inc(own.sem, 1)
                        dve.wait_ge(own.sem, j * 2 + (own.base + 2))
                        nc.vector.tensor_tensor(act_low[:, n, :], act_raw, act_high[:, n, :].bitcast(F32), ALU.subtract
                                                ).then_inc(gated.sem, 1)
                    if not last:
                        low_part(i + 1, b)

            for b in range(SLOTS):
                low_part(0, b)
            turn(0, False)
            with dve.Fori(1, turns - 1) as i:
                turn(i, False)
            turn(turns - 1, True)
            own.pending += 2 * NKEYS
            step = Steps(dve, own)
            dve.wait_ge(used.sem, used.base + 2 * NKEYS)
            dve.wait_ge(core.landed.sem, core.landed.at(16))
            for m in range(KD):
                step(nc.vector.scalar_tensor_tensor(x[:, m, :], core.banks[:, m // 2, SEQ * (m % 2):SEQ * (m % 2) + SEQ],
                                                    gain(m), x[:, m, :], ALU.mult, ALU.add))
    for c in (used, high_ready, low_ready):
        c.pending += 2 * NKEYS
    for c in (gelus, gated):
        c.pending += NKEYS
    for c in loaded:
        c.pending += 16 * turns
    core.settle()


def peer(core, layer, x, mod, g2, experts, h_dram, x_dram, close_ring):
    last_layer = layer == LAYERS - 1
    section = f"peer{layer}"
    t0, length = (SEQ, SEQ) if last_layer else (0, 2 * SEQ)
    segs = [(0, SEQ)] if last_layer else [(0, SEQ), (SEQ, 2 * SEQ)]
    first = 1 if last_layer else 0
    xs = x[:, :, t0:t0 + length]
    H, K = PEER_HEADS, TOPK
    routeT = core.route[:, :, 0:length]
    with ExitStack() as s:
        h = core.sb(s, "h", [P, KD, length])[:, :, :]
        q = core.sb(s, "q", [P, 2 * KD, length])
        with ExitStack() as t:
            squares, rstd = core.sb(t, "squares", [P, KD, length]), core.sb(t, "rstd", [P, length])
            norm_stage(core, xs, h, squares[:, :, :], rstd[:, :], segs,
                       lambda k, i: g2[:, k, first + i:first + i + 1],
                       lambda k, i: mod[:, 3 * KD + k, first + i:first + i + 1], section)
        store_stage(core, h_dram[:, :, 0:length], h)
        peer_query_stage(core, layer, h, q, length)
        w = {"scores": core.sb(s, "scores", [P, 2 * H, NKEYS]), "rest": core.sb(s, "rest", [P, 2 * H, NKEYS]),
             "top": core.sb(s, "top", [P, 2 * H, K]), "numbers": core.sb(s, "numbers", [P, 2 * H, K], U32),
             "numbers_f": core.sb(s, "numbers_f", [P, 2 * H, K]),
             "candidates": core.sb(s, "candidates", [P, H, K * K]), "candidate_rest": core.sb(s, "candidate_rest", [P, H, K * K]),
             "best": core.sb(s, "best", [P, H, K]), "position": core.sb(s, "position", [P, 2 * H, K], U32),
             "equal": core.sb(s, "equal", [P, H, K, K]), "halves": core.sb(s, "halves", [P, 2 * H, K]),
             "weights": core.sb(s, "route", [P, 3, P]), "stat": core.sb(s, "route_stat", [P, 2 * H])}
        keys = core.next_chunk
        core.next_chunk += 1
        route_stage(core, layer, q, length // P, keys, w, routeT)
    close_ring()
    with ExitStack() as s:
        g = core.sb(s, "expert_weights", [P, NKEYS, SEQ])
        h_parts = [core.sb(s, f"h_{name}", [P, KD, SEQ], F32R)[:, :, :] for name in ("high", "low")]
        parts = [core.sb(s, f"experts_{name}", [P, SLOTS, D], F32R) for name in ("high", "low")]
        acts = [core.sb(s, "activated", [P, SEQ])[:, :]] + [core.sb(s, f"activated_{name}", [P, 2, SEQ], F32R) for name in ("high", "low")]
        store_stage(core, x_dram, x)
        raw = x.rearrange("p k t -> p (k t)").rearrange("p (s n) -> p s n", s=SLOTS)
        for i, (a, b) in enumerate(segs):
            h_raw = raw[:, 0:2, :].rearrange("p s (k t) -> p (s k) t", t=SEQ)
            small_load_stage(core, [(h_raw, h_dram[:, :, a:b])])
            halves_stage(core, h_raw, *h_parts)
            pick, weight = (raw[:, n, :].rearrange("p (s n) -> p s n", n=P) for n in range(2))
            spread_stage(core, a, routeT, pick, weight, g)
            experts_stage(core, layer, h_parts, xs[:, :, a:b], x_dram[:, :, t0 + a:t0 + b], g, raw, parts, acts,
                          lambda m, i=i: mod[:, 5 * KD + m, first + i:first + i + 1], experts)
            if i < len(segs) - 1:
                store_stage(core, x_dram[:, :, t0 + a:t0 + b], xs[:, :, a:b])
        for a, b in segs[:-1]:
            small_load_stage(core, [(xs[:, :, a:b], x_dram[:, :, t0 + a:t0 + b])])



CONSTANTS = ("ident", "ones", "head_ones", "iota", "iota16")


def build(nc, dram, debug=None):
    with ExitStack() as stack:
        core = Core(nc, stack, dram)
        core.experts_loaded = [core.count(f"experts_loaded_{b}") for b in range(SLOTS)]
        x = core.sb(stack, "x", [P, KD, 2 * SEQ])[:, :, :]
        vec = core.sb(stack, "vectors", [P, core.nvec])
        core.vec = vec
        shapes = {k: v.shape[1] for k, v in constants().items()}
        for name in CONSTANTS:
            core.const[name] = core.sb(stack, name, [P, shapes[name]])[:, :]
        cc, mod = core.sb(stack, "silu_c", [P, KD, 2]), core.sb(stack, "modulation", [P, 48, 2])
        g1, g2 = core.sb(stack, "gain1", [P, KD, 2]), core.sb(stack, "gain2", [P, KD, 2])
        z_dram = [nc.dram_tensor(f"z_scratch_{i}", [P, 24, 2 * SEQ], F32, kind="Internal").ap() for i in range(LAYERS)]
        h_dram = [nc.dram_tensor(f"h_scratch_{i}", [P, KD, 2 * SEQ], F32, kind="Internal").ap() for i in range(LAYERS)]
        x_dram = [nc.dram_tensor(f"x_scratch_{i}", [P, KD, 2 * SEQ], F32, kind="Internal").ap() for i in range(LAYERS)]
        y_dram = [nc.dram_tensor(f"y_scratch_{i}", [P, KD, 2 * SEQ], F32, kind="Internal").ap() for i in range(LAYERS)]
        core.first_loads = [(x[:, :, 0:SEQ], dram["ctxT"]), (x[:, :, SEQ:], dram["xT"]), core.vector_load("common"), core.vector_load("first")]
        core.first_loads += [(core.const[name], dram["c_" + name]) for name in CONSTANTS]
        ring = WeightRing(nc, stack, None, dram["weights"])
        core.ring = ring
        xs = x[:, :, SEQ:]

        def mixer_layer(layer):
            small_load_stage(core, [core.vector_load(layer)])
            modulation_stage(core, layer, cc, mod, g1, g2)
            mixer(core, layer, x, mod, g1, z_dram[layer], y_dram[layer])
            if debug:
                debug(core, f"mixed{layer}", x[:, :, :])

        def peer_layer(layer, ring_stack):
            with ExitStack() as s:
                core.route = core.sb(s, "route_T", [P, 3, 2 * SEQ])
                inner = ExitStack()
                ring.slots = [core.sb(inner, f"weight_slot_{i}", [P, SLOT]) for i in range(RING)]
                peer(core, layer, x, mod, g2, dram["experts"], h_dram[layer], x_dram[layer], inner.close)
            if debug:
                debug(core, f"layer{layer}", x[:, :, :])

        with ExitStack() as s:
            ring.slots = [core.sb(s, f"weight_slot_{i}", [P, SLOT]) for i in range(RING)]
            load_stage(core, "mixer0")
            first_block(core, xs, dram["rel_bias"], stack)
            if debug:
                debug(core, "first", xs)
            mixer_layer(0)
        peer_layer(0, None)
        with ExitStack() as s:
            ring.slots = [core.sb(s, f"weight_slot_{i}", [P, SLOT]) for i in range(RING)]
            mixer_layer(1)
        peer_layer(1, None)
        with ExitStack() as s:
            squares, rstd = core.sb(s, "squares", [P, KD, SEQ]), core.sb(s, "rstd", [P, SEQ])
            norm_stage(core, xs, xs, squares[:, :, :], rstd[:, :], [(0, SEQ)], lambda k, i: core.v("final_g_2", k), None, "peer1")
        store_stage(core, dram["out"], xs)



def device_arrays(inputs):
    u, v = inputs["peer_u_2"], inputs["peer_v_2"]
    ut = u.reshape(LAYERS, NKEYS, NKEYS, KD, P).transpose(0, 2, 4, 3, 1).reshape(LAYERS, NKEYS, P, D)
    vt = v.reshape(LAYERS, NKEYS, NKEYS, D).transpose(0, 2, 1, 3)
    out = {
        "xT": inputs["x"][0].T.reshape(KD, P, SEQ).transpose(1, 0, 2),
        "ctxT": inputs["ctx_2"][0].T.reshape(KD, P, CTX).transpose(1, 0, 2),
        "rel_bias": inputs["rel_bias"],
        "weights": weight_stream(inputs),
        "experts": np.concatenate([ut, vt], 3),
    }
    out.update(vector_arrays(inputs))
    out.update({"c_" + k: a for k, a in constants().items()})
    return {k: np.ascontiguousarray(a) for k, a in out.items()}


def kernel(**inputs):
    from concourse import bacc
    from concourse.bass_utils import run_bass_kernel_spmd

    arrays = device_arrays(inputs)
    nc = bacc.Bacc("TRN2", target_bir_lowering=False, num_devices=1)
    dram = {k: nc.dram_tensor(k, a.shape, F32, kind="ExternalInput").ap() for k, a in arrays.items()}
    dram["out"] = nc.dram_tensor("out", (P, KD, SEQ), F32, kind="ExternalOutput").ap()
    build(nc, dram)
    r = run_bass_kernel_spmd(nc, [arrays], core_ids=[0])
    return np.ascontiguousarray(r.results[0]["out"].transpose(1, 0, 2).reshape(D, SEQ).T)[None]
```
